# Optimizing a Trainium2 kernel written in Bass

```python
import jax, jax.numpy as jnp
from jax import lax
import numpy as np

D_MODEL = 1024
BATCH = 1
SEQ = 1024
DEPTH = 2

N_HEADS = 8
HEAD_DIM = 64
ATT_WIDTH = N_HEADS * HEAD_DIM
POOL_GROUPS = 4
POOL_WIDTH = D_MODEL - ATT_WIDTH
POOL_GROUP_DIM = POOL_WIDTH // POOL_GROUPS
POOL_WINDOWS = (2, 4, 8, 16)
MIX_WIDTH = ATT_WIDTH + POOL_WIDTH
IN_WIDTH = 3 * ATT_WIDTH + POOL_WIDTH
DILATED_BRANCHES = ((128, 1), (512, 4), (2048, 16))
ROT_DIM = HEAD_DIM // 4
ROPE_THETA = 500000.0
N_EXPERT_GROUPS = 4
EXPERTS_PER_GROUP = 4
N_EXPERTS = N_EXPERT_GROUPS * EXPERTS_PER_GROUP
TOP_K_IN_GROUP = 2
D_EXPERT = D_MODEL // 4
RMS_EPS = 1e-6
NEG_INF = -1e30

kernel_name = "hybrid_dilated_attn_pool_hiermoe"

def rms_norm(x, g):
    x32 = x.astype(jnp.float32)
    y = x32 * lax.rsqrt(jnp.mean(x32 * x32, axis=-1, keepdims=True) + RMS_EPS)
    return (y * g.astype(jnp.float32)).astype(x.dtype)

def rope_tables(seq):
    inv_freq = ROPE_THETA ** (-jnp.arange(0, ROT_DIM, 2, dtype=jnp.float32) / ROT_DIM)
    ang = jnp.arange(seq, dtype=jnp.float32)[:, None] * inv_freq[None, :]
    return jnp.cos(ang), jnp.sin(ang)

def apply_partial_rope(t, cos, sin):
    half = ROT_DIM // 2
    t1, t2, rest = t[..., :half], t[..., half:ROT_DIM], t[..., ROT_DIM:]
    c = cos[None, :, None, :]
    s = sin[None, :, None, :]
    return jnp.concatenate([t1 * c - t2 * s, t2 * c + t1 * s, rest], axis=-1)

def dilated_branch(q, k, v, window, dilation):
    B, S, H, Dh = q.shape
    span = window // dilation
    blk = span
    unit = dilation * blk
    P = -(-S // unit) * unit
    L = P // dilation
    nb = L // blk

    def split(t):
        t = jnp.pad(t, ((0, 0), (0, P - S), (0, 0), (0, 0)))
        t = t.reshape(B, L, dilation, H, Dh).transpose(0, 2, 3, 1, 4)
        return t.reshape(B, dilation, H, nb, blk, Dh)

    qb, kb, vb = split(q), split(k), split(v)
    pad_prev = ((0, 0), (0, 0), (0, 0), (1, 0), (0, 0), (0, 0))
    kcat = jnp.concatenate([jnp.pad(kb, pad_prev)[:, :, :, :-1], kb], axis=4)
    vcat = jnp.concatenate([jnp.pad(vb, pad_prev)[:, :, :, :-1], vb], axis=4)

    qi = jnp.arange(blk)[:, None]
    kj = jnp.arange(2 * blk)[None, :]
    dist = blk + qi - kj
    band = (dist >= 0) & (dist <= span)
    has_prev = (jnp.arange(nb) > 0)[:, None, None] | (kj >= blk)[None]
    mask = band[None] & has_prev

    s = jnp.einsum('brhnqc,brhnkc->brhnqk', qb, kcat)
    s = jnp.where(mask, s, NEG_INF)
    m = jnp.max(s, axis=-1, keepdims=True)
    p = jnp.exp(s - m)
    den = jnp.sum(p, axis=-1, keepdims=True)
    num = jnp.einsum('brhnqk,brhnkc->brhnqc', p, vcat)

    def merge(t):
        X = t.shape[-1]
        t = t.reshape(B, dilation, H, L, X).transpose(0, 3, 1, 2, 4)
        return t.reshape(B, P, H, X)[:, :S]

    return merge(num), merge(m), merge(den)

def dilated_attention(q, k, v):
    outs = [dilated_branch(q, k, v, w, d) for (w, d) in DILATED_BRANCHES]
    m_all = jnp.max(jnp.stack([o[1] for o in outs], axis=0), axis=0)
    num = sum(jnp.exp(o[1] - m_all) * o[0] for o in outs)
    den = sum(jnp.exp(o[1] - m_all) * o[2] for o in outs)
    return num / den

def pool_mixer(u, w_pool, pool_scale):
    B, S, _ = u.shape
    ug = u.astype(jnp.float32).reshape(B, S, POOL_GROUPS, POOL_GROUP_DIM)
    cs = jnp.cumsum(ug, axis=1)
    t1 = jnp.arange(1, S + 1, dtype=jnp.float32)
    outs = []
    for gi, w in enumerate(POOL_WINDOWS):
        c = cs[:, :, gi]
        lower = jnp.pad(c, ((0, 0), (w, 0), (0, 0)))[:, :S]
        cnt = jnp.minimum(t1, float(w))[None, :, None]
        outs.append((c - lower) / cnt - ug[:, :, gi])
    r = jnp.stack(outs, axis=2)
    y = jnp.einsum('bsgc,gce->bsge', r, w_pool.astype(jnp.float32)).reshape(B, S, POOL_WIDTH)
    return (y * pool_scale.astype(jnp.float32)).astype(u.dtype)

def hier_moe(h, w_group, b_group, w_router, b_router, w_gate, w_up, w_down):
    B, S, D = h.shape
    t = h.reshape(B * S, D)
    g_prob = jax.nn.softmax((t @ w_group + b_group).astype(jnp.float32), axis=-1)
    p_top, g_idx = lax.top_k(g_prob, 1)
    e_logit = (t @ w_router + b_router).astype(jnp.float32).reshape(-1, N_EXPERT_GROUPS, EXPERTS_PER_GROUP)
    g_onehot = jax.nn.one_hot(g_idx[:, 0], N_EXPERT_GROUPS, dtype=jnp.float32)
    e_sel = jnp.einsum('tg,tge->te', g_onehot, e_logit)
    v2, i2 = lax.top_k(e_sel, TOP_K_IN_GROUP)
    w2 = jax.nn.softmax(v2, axis=-1) * p_top
    eid = g_idx * EXPERTS_PER_GROUP + i2
    gates = jnp.sum(jax.nn.one_hot(eid, N_EXPERTS, dtype=jnp.float32) * w2[..., None], axis=1)
    hg = jnp.einsum('td,edf->tef', t, w_gate)
    hu = jnp.einsum('td,edf->tef', t, w_up)
    a = jax.nn.silu(hg) * hu * gates[..., None].astype(t.dtype)
    y = jnp.einsum('tef,efd->td', a, w_down)
    return y.reshape(B, S, D)

def setup_inputs(seed: int = 0) -> dict:
    key = jax.random.key(seed)
    ks = jax.random.split(key, 16)
    f32 = jnp.float32
    nrm = lambda k, shape: jax.random.normal(k, shape, dtype=f32)
    return {
        "x": nrm(ks[0], (BATCH, SEQ, D_MODEL)),
        "norm1_gain": 1.0 + 0.02 * nrm(ks[1], (DEPTH, D_MODEL)),
        "w_in": nrm(ks[2], (DEPTH, D_MODEL, IN_WIDTH)) * D_MODEL ** -0.5,
        "q_norm_gain": 1.0 + 0.02 * nrm(ks[3], (DEPTH, HEAD_DIM)),
        "k_norm_gain": 1.0 + 0.02 * nrm(ks[4], (DEPTH, HEAD_DIM)),
        "w_pool": nrm(ks[5], (DEPTH, POOL_GROUPS, POOL_GROUP_DIM, POOL_GROUP_DIM)) * POOL_GROUP_DIM ** -0.5,
        "pool_scale": 1.0 + 0.02 * nrm(ks[6], (DEPTH, POOL_WIDTH)),
        "w_out": nrm(ks[7], (DEPTH, MIX_WIDTH, D_MODEL)) * MIX_WIDTH ** -0.5,
        "norm2_gain": 1.0 + 0.02 * nrm(ks[8], (DEPTH, D_MODEL)),
        "w_group": nrm(ks[9], (DEPTH, D_MODEL, N_EXPERT_GROUPS)) * D_MODEL ** -0.5,
        "b_group": 0.01 * nrm(ks[10], (DEPTH, N_EXPERT_GROUPS)),
        "w_router": nrm(ks[11], (DEPTH, D_MODEL, N_EXPERTS)) * D_MODEL ** -0.5,
        "b_router": 0.01 * nrm(ks[12], (DEPTH, N_EXPERTS)),
        "w_gate": nrm(ks[13], (DEPTH, N_EXPERTS, D_MODEL, D_EXPERT)) * D_MODEL ** -0.5,
        "w_up": nrm(ks[14], (DEPTH, N_EXPERTS, D_MODEL, D_EXPERT)) * D_MODEL ** -0.5,
        "w_down": nrm(ks[15], (DEPTH, N_EXPERTS, D_EXPERT, D_MODEL)) * D_EXPERT ** -0.5,
    }

def reference(x, norm1_gain, w_in, q_norm_gain, k_norm_gain, w_pool, pool_scale, w_out,
              norm2_gain, w_group, b_group, w_router, b_router, w_gate, w_up, w_down):
    B, S, _ = x.shape
    cos, sin = rope_tables(S)
    scale = HEAD_DIM ** -0.5
    for l in range(DEPTH):
        h = rms_norm(x, norm1_gain[l])
        z = h @ w_in[l]
        q, k, v, u = jnp.split(z, [ATT_WIDTH, 2 * ATT_WIDTH, 3 * ATT_WIDTH], axis=-1)
        q = rms_norm(q.reshape(B, S, N_HEADS, HEAD_DIM), q_norm_gain[l]).astype(jnp.float32)
        k = rms_norm(k.reshape(B, S, N_HEADS, HEAD_DIM), k_norm_gain[l]).astype(jnp.float32)
        q = apply_partial_rope(q, cos, sin) * scale
        k = apply_partial_rope(k, cos, sin)
        v = v.reshape(B, S, N_HEADS, HEAD_DIM).astype(jnp.float32)
        att = dilated_attention(q, k, v).reshape(B, S, ATT_WIDTH).astype(x.dtype)
        pool = pool_mixer(u, w_pool[l], pool_scale[l])
        x = x + jnp.concatenate([att, pool], axis=-1) @ w_out[l]
        x = x + hier_moe(rms_norm(x, norm2_gain[l]), w_group[l], b_group[l], w_router[l], b_router[l],
                         w_gate[l], w_up[l], w_down[l])
    return x


_drawn_inputs = setup_inputs


def setup_inputs(seed=0):
    import zlib

    import numpy as np

    out = dict(_drawn_inputs(seed))
    spreads = {}
    factors = {'q_norm_gain': 6.743, 'k_norm_gain': 8.0, 'b_group': 2.873, 'b_router': 4.261}
    for name, (base, spread) in spreads.items():
        noise = np.random.default_rng([zlib.crc32(name.encode()), seed]).standard_normal(out[name].shape)
        drawn = base * np.exp(spread * noise) if base else spread * noise
        out[name] = __import__('jax').numpy.asarray(drawn.astype(out[name].dtype))
    for name, factor in factors.items():
        out[name] = (out[name] * factor).astype(out[name].dtype)
    return out
```

```python
import math
from contextlib import ExitStack

import numpy as np

import concourse.bass as bass
from concourse import mybir

P = 128
DEPTH, SEQ, D = 2, 1024, 1024
HEADS, HD = 8, 64
ATT = HEADS * HD
NG, GD = 4, 128
POOL_WINDOWS = (2, 4, 8, 16)
BRANCHES = ((128, 1), (512, 4), (2048, 16))
ROT, THETA = HD // 4, 500000.0
EG, EPG = 4, 4
NE, FE = EG * EPG, 256
EPS = 1e-6
NEG = -1e30

T = SEQ // P
K = D // P
PAIRS = HEADS // 2
BLOCKS = (2 * SEQ - NE) // P + NE
ROWS = BLOCKS * P
NR = EG + NE

C_MASK, C_ID, C_LOW, C_ONE = 0, SEQ, SEQ + P, SEQ + 2 * P
C_COS = C_ONE + P
C_SIN = C_COS + T * ROT
C_JJ = C_SIN + T * ROT
C_DESC = C_JJ + 32
C_THR = C_DESC + 4
C_LT = C_THR + T
C_INV = C_LT + NE * NE
C_ALL = C_INV + 16

G1, G2, PSC = 0, K, 2 * K
GQK = 2 * K + NG
BIAS_R = GQK + 2 * HD
NPAR = BIAS_R + NR

RING = 3
BIAS = RING - 1


def shape_constants():
    c = np.zeros((P, C_ALL), np.float32)
    row = np.arange(P)[:, None]
    dist = (T - 1) * P + row - np.arange(SEQ)[None, :]
    count = np.zeros(dist.shape, np.int64)
    for window, dilation in BRANCHES:
        count += (dist >= 0) & (dist <= window) & (dist % dilation == 0)
    c[:, C_MASK:C_MASK + SEQ] = np.where(count > 0, np.log(np.maximum(count, 1)), NEG)
    c[:, C_ID:C_ID + P] = np.eye(P)
    c[:, C_LOW:C_LOW + P] = row < np.arange(P)[None, :]
    c[:, C_ONE:C_ONE + P] = 1.0
    inv_freq = np.float32(THETA) ** (-np.arange(0, ROT, 2, dtype=np.float32) / np.float32(ROT))
    ang = np.arange(SEQ, dtype=np.float32)[:, None] * inv_freq.astype(np.float32)[None, :]
    cos, sin = np.cos(ang).astype(np.float32), np.sin(ang).astype(np.float32)
    both = np.concatenate([cos, cos], 1), np.concatenate([-sin, sin], 1)
    for at, table in zip((C_COS, C_SIN), both):
        c[:, at:at + T * ROT] = table.reshape(T, P, ROT).transpose(1, 0, 2).reshape(P, T * ROT)
    c[:, C_JJ:C_JJ + 32] = np.arange(32)
    c[:, C_DESC:C_DESC + 4] = 4 - np.arange(4)
    c[:, C_THR:C_THR + T] = P * np.arange(T)
    e = np.arange(NE)
    c[:, C_LT:C_LT + NE * NE] = (e[None, :] < e[:, None]).reshape(-1)
    c[:, C_INV:C_INV + 16] = 1.0 / (1.0 + np.arange(16))
    return c


def trunk(nc, x, norm1_gain, w_in, q_norm_gain, k_norm_gain, w_pool, pool_scale, w_out,
          norm2_gain, w_group, b_group, w_router, b_router, w_gate, w_up, w_down, consts, out):
    f32, i32, bf16 = mybir.dt.float32, mybir.dt.int32, mybir.dt.bfloat16
    ALU, ACT, AX = mybir.AluOpType, mybir.ActivationFunctionType, mybir.AxisListType
    ds = bass.ds

    ctx = ExitStack()
    with ctx:
        def sb(name, shape, dt=f32):
            return ctx.enter_context(nc.sbuf_tensor(name, shape, dt))

        def sem(name):
            return ctx.enter_context(nc.semaphore(name))

        ctx.enter_context(nc.allow_non_contiguous_dma(reason="small parameters, once"))
        row_table = nc.dram_tensor("row_table", (ROWS, D), f32, kind="Internal").ap()
        y_table = nc.dram_tensor("y_table", (ROWS, D), f32, kind="Internal").ap()

        xr = sb("x_res", [P, T, D])
        W = sb("W", [P, 4, K, 512])
        qT_r = sb("qT", [P, 4 * SEQ])
        kT_r = sb("kT", [P, 4 * SEQ])
        v_r = sb("v", [P, T * ATT])
        PAD = 16
        uT = sb("uT", [P, NG, PAD + SEQ])
        A = sb("arena", [P, 8192])
        cst = sb("cst", [P, C_ALL])
        zero = sb("zero", [P, 256])
        par_all = sb("par_all", [P, DEPTH, NPAR])
        par = sb("par", [P, NPAR])
        wr_all = sb("wr_all", [P, DEPTH * K * NR + P])
        wpool = sb("wpool", [P, NG, GD])
        st = sb("st", [P, 160])
        gate_w = sb("gate_w", [P, 2, T])
        pos_i = sb("pos_i", [P, 2, T], i32)
        block_e = sb("block_e", [P, 32], i32)
        ps = ctx.enter_context(nc.psum_tensor("ps", [P, 8, 512], f32))

        qT = qT_r[:, :].rearrange("p (a s) -> p a s", a=PAIRS)
        kT = kT_r[:, :].rearrange("p (a s) -> p a s", a=PAIRS)
        attT, poolT = qT, kT
        v = v_r[:, :].rearrange("p (t c) -> p t c", t=T)
        w_o = [W[:, h, :, :] for h in range(2)]
        xs2_all = W[:, 2:4, :, :].rearrange("p a k n -> p (a k n)").rearrange("p (t d) -> p t d", t=T)
        wgu = [v_r[:, :].rearrange("p (k n) -> p k n", k=K),
               uT[:, :, :].rearrange("p g s -> p (g s)")[:, 0:4096].rearrange("p (k n) -> p k n", k=K),
               W[:, 2, :, :]]
        wd = [kT_r[:, 2048 * i:2048 * i + 2048].rearrange("p (k n) -> p k n", k=2) for i in range(2)]
        wd.append(W[:, 3, 0:4, :].rearrange("p a n -> p (a n)").rearrange("p (k n) -> p k n", k=2))
        gath = [qT_r[:, 2048 * i:2048 * i + 2048].rearrange("p (k n) -> p k n", k=2) for i in range(2)]

        def ring(at, size, n=2, inner=None):
            r = [A[:, at + size * i:at + size * (i + 1)] for i in range(n)]
            return [a.rearrange("p (k n) -> p k n", n=inner) for a in r] if inner else r

        rope = A[:, 0:512].rearrange("p (a h c) -> p a h c", a=2, h=16)
        u_nat = A[:, 512:1024].rearrange("p (g c) -> p g c", g=NG)
        xs = ring(1024, D)
        hT = ring(3072, D, inner=P)
        zn = ring(5120, D, inner=HD)
        sqz = A[:, 7168:8192].rearrange("p (h c) -> p h c", c=HD)
        qst, kst = A[:, 0:1024], A[:, 1024:2048]
        att = A[:, 2048:3072].rearrange("p (t c) -> p t c", c=P)
        prT = ring(3072, SEQ, inner=P)
        pr = ring(5120, SEQ)
        cat = ring(0, D, inner=P)
        xs2 = ring(2048, D)
        h2T = ring(4096, D, inner=P)
        junk2 = A[:, 6144:6656].bitcast(bf16)
        xg = ring(0, D, RING)
        xgT = A[:, 3072:4096].rearrange("p (k n) -> p k n", n=P)
        sg, act = A[:, 4096:4352], A[:, 4352:4608]
        aT = A[:, 4608:4864].rearrange("p (k n) -> p k n", n=P)
        y = ring(4864, D, RING)

        ident = cst[:, C_ID:C_ID + P]
        low = cst[:, C_LOW:C_LOW + P]
        ones = cst[:, C_ONE:C_ONE + P]
        desc = cst[:, C_DESC:C_DESC + 4]

        x_ready = sem("x_ready")
        params = sem("params")
        sd1 = sem("sd1")
        xs_ready = sem("xs_ready")
        xt_done = sem("xt_done")
        hT_ready = sem("hT_ready")
        z_done = sem("z_done")
        sqz_done = sem("sqz_done")
        var_ready = sem("var_ready")
        sdz = sem("sdz")
        zqk_free = sem("zqk_free")
        v_copied = sem("v_copied")
        u_copied = sem("u_copied")
        qk_ready = sem("qk_ready")
        tqk_done = sem("tqk_done")
        t_evac = sem("t_evac")
        pooled = sem("pooled")
        staged = sem("staged")
        s_done = sem("s_done")
        sm_ready = sem("sm_ready")
        p_ready = sem("p_ready")
        pt0_done = sem("pt0_done")
        pt1_done = sem("pt1_done")
        pt0_ev = sem("pt0_ev")
        pt1_ev = sem("pt1_ev")
        pv_done = sem("pv_done")
        o_ev = sem("o_ev")
        at_done = sem("at_done")
        at_ev = sem("at_ev")
        pm_done = sem("pm_done")
        poolT_ready = sem("poolT_ready")
        cat_ready = sem("cat_ready")
        op_done = sem("op_done")
        x_upd = sem("x_upd")
        sd2 = sem("sd2")
        xs2_ready = sem("xs2_ready")
        xs2_saved = sem("xs2_saved")
        xt2_done = sem("xt2_done")
        h2T_ready = sem("h2T_ready")
        rt_done = sem("rt_done")
        logits = sem("logits")
        ge_ready = sem("ge_ready")
        ge_exp = sem("ge_exp")
        dm_ready = sem("dm_ready")
        dm_exp = sem("dm_exp")
        onehots = sem("onehots")
        ranks = sem("ranks")
        routed = sem("routed")
        xtm_done = sem("xtm_done")
        xgT_ready = sem("xgT_ready")
        gu_done = sem("gu_done")
        silu_done = sem("silu_done")
        a_ready = sem("a_ready")
        a_t_done = sem("a_t_done")
        aT_ready = sem("aT_ready")
        dn_done = sem("dn_done")
        y0_ready = sem("y0_ready")
        y1_ready = sem("y1_ready")
        s_passed = sem("s_passed")

        def upto(l, per_layer, n):
            return l * per_layer + n + BIAS

        s_cst, s_x, s_par = sem("s_cst"), [sem(f"s_x{t}") for t in range(T)], sem("s_par")
        s_mask = sem("s_mask")
        s_win = [sem(f"s_win{c}") for c in range(4)]
        s_wout = [sem(f"s_wout{c}") for c in range(2)]
        s_wpool, s_zero = sem("s_wpool"), sem("s_zero")
        s_scat = sem("s_scat")
        s_gu = [sem(f"s_gu{i}") for i in range(RING)]
        s_d = [sem(f"s_d{i}") for i in range(RING)]
        s_xg = [sem(f"s_xg{i}") for i in range(RING)]
        s_y = [sem(f"s_y{i}") for i in range(RING)]
        s_gath = [sem(f"s_gath{i}") for i in range(2)]
        s_out = sem("s_out")
        s_ms = sem("s_ms")
        s_dve, s_act, s_pool = sem("s_dve"), sem("s_act"), sem("s_pool")

        USES = [(BLOCKS + RING - 1 - i) // RING for i in range(RING)]

        class Chain:

            def __init__(self, eng, s):
                self.eng, self.s, self.n = eng, s, 0

            def link(self, ins):
                ins.then_inc(self.s, 1)
                self.n += 1
                self.eng.wait_ge(self.s, self.n)

            def restart(self):
                self.eng.sem_clear(self.s)
                self.n = 0

        def steps(eng, n, body, chain=None, ring=2):
            body(0, 0, 0)
            with eng.Fori(0, (n - 2) // ring) as j:
                if chain:
                    chain.restart()
                for i in range(1, ring + 1):
                    body(ring * j + i, i % ring, j + i // ring)
            if chain:
                chain.restart()
            for t in range(1 + ring * ((n - 2) // ring), n):
                body(t, t % ring, t // ring)

        def before(slot, m):
            return (slot - 1) % RING, m - 1 if slot == 0 else m

        def after(slot, m):
            return (slot + 1) % RING, m + 1 if slot == RING - 1 else m

        def first(t):
            return isinstance(t, int) and t == 0

        def last(t, n):
            return isinstance(t, int) and t == n - 1

        def spread(ap, n):
            return ap.unsqueeze(2).to_broadcast([ap.shape[0], ap.shape[1], n])

        places, at = {}, 6656
        for name, n in (("lg", T * NR), ("ge", T * EG), ("ee", T * EG), ("gm", T), ("gs", T), ("pt", T),
                        ("is1", T * 4), ("sm", T), ("goh", T * EG), ("es", T * EPG), ("m1", T), ("oh1", T * 4),
                        ("es2", T * EPG), ("m2", T), ("oh2", T * 4), ("dm", T), ("e2", T), ("rd", T),
                        ("te", NE), ("start", NE), ("cnt", NE), ("posf", 2 * T), ("bef", 32), ("M", T * NE)):
            places[name] = A[:, at:at + n]
            at += n
        assert at <= 8192
        at = 0
        for name, n in (("tmp", 512), ("tmp2", 512), ("OH1", T * NE), ("OH2", T * NE), ("off", T * NE),
                        ("tot", T * NE), ("base", T * NE)):
            places[name] = A[:, at:at + n]
            at += n
        assert at <= 2048

        def R(name, inner=None):
            return places[name].rearrange("p (a b) -> p a b", b=inner) if inner else places[name]

        block = ctx.enter_context(nc.Block())

        @block.sync
        def _(sp):
            for t in range(T):
                sp.dma_start(xr[:, t, :], x[0, t * P:(t + 1) * P, :]).then_inc(s_x[t], 16)
                if t == 0:
                    sp.dma_start(cst[:, C_ID:C_ALL], consts[:, C_ID:C_ALL]).then_inc(s_cst, 16)
            with sp.Fori(0, DEPTH) as l:
                win = w_in[ds(l, 1), :, :].rearrange("a (k p) n -> p (a k) n", p=P)
                wout = w_out[ds(l, 1), :, :].rearrange("a (k p) n -> p (a k) n", p=P)
                for c in range(4):
                    if c == 0:
                        sp.wait_ge(op_done, upto(l, T, 0))
                    if c == 2:
                        sp.wait_ge(dn_done, upto(l, BLOCKS, 0))
                    sp.dma_start(W[:, c, :, :], win[:, :, c * 512:(c + 1) * 512]).then_inc(s_win[c], 16)
                sp.wait_ge(pm_done, upto(l, 2 * NG, 0))
                sp.dma_start(wpool[:, :, :], w_pool[ds(l, 1), :, :, :].rearrange("a g c e -> c (a g) e"))\
                    .then_inc(s_wpool, 16)
                for h in range(2):
                    sp.wait_ge(z_done, upto(l, 4 * T, 4 * T - 3 + h))
                    sp.dma_start(w_o[h], wout[:, :, h * 512:(h + 1) * 512]).then_inc(s_wout[h], 16)
                sp.wait_ge(routed, upto(l, 1, 1))
                sp.wait_ge(s_scat, (l + 1) * (16 * 2 * T))
                sp.sem_inc(s_passed, 1)

                def load_block(j, slot, m):
                    e = sp.value_load(block_e[0:1, ds(j, 1)], min_val=0, max_val=NE - 1)
                    if not first(j):
                        sp.wait_ge(gu_done, upto(l, BLOCKS, j - RING + 1))
                    gu = wgu[slot]
                    at = e + l * NE
                    for w, c in ((w_gate, 0), (w_up, FE)):
                        sp.dma_start(gu[:, :, c:c + FE],
                                     w.rearrange("l e (k p) f -> p (l e) k f", p=P)[:, ds(at, 1), :, :]
                                     .rearrange("p a k f -> p (a k) f")).then_inc(s_gu[slot], 16)
                    if not first(j):
                        sp.wait_ge(xtm_done, upto(l, BLOCKS, j - RING + 1))
                    sp.dma_start(xg[slot], row_table[ds(j * P, P), :]).then_inc(s_xg[slot], 16)
                    if not first(j):
                        sp.wait_ge(dn_done, upto(l, BLOCKS, j - RING + 1))
                    sp.dma_start(wd[slot],
                                 w_down.rearrange("l e (k p) f -> p (l e) k f", p=P)[:, ds(at, 1), :, :]
                                 .rearrange("p a k f -> p (a k) f")).then_inc(s_d[slot], 16)

                steps(sp, BLOCKS, load_block, ring=RING)

        @block.gpsimd
        def _(pool):
            ch = Chain(pool, s_pool)
            nc.gpsimd.memset(zero[:, :], 0.0).then_inc(s_ms, 1)
            nc.gpsimd.memset(st[:, 159:160], EPS).then_inc(s_ms, 1)
            pool.wait_ge(s_ms, 2)
            for s in (x_ready, pooled, staged, cat_ready):
                pool.sem_inc(s, BIAS)
            for t in range(T):
                pool.wait_ge(s_x[t], 16)
                pool.sem_inc(x_ready, 1)
            pool.dma_start(cst[:, C_MASK:C_ID], consts[:, C_MASK:C_ID]).then_inc(s_mask, 16)
            pool.wait_ge(z_done, upto(0, 4 * T, 5))
            rt = row_table.rearrange("(p r) (b c) -> p (r b) c", p=P, c=256)
            per = BLOCKS
            for i in range(4):
                pool.dma_start(rt[:, i * per:(i + 1) * per, :],
                               zero[:, :].unsqueeze(1).to_broadcast([P, per, 256])).then_inc(s_zero, 16)
            with pool.Fori(0, DEPTH) as l:
                ch.restart()
                pool.wait_ge(t_evac, upto(l, 3 * T, 3 * T))
                sA = W[:, 2, :, :].rearrange("p k n -> p (k n)")[:, 0:PAD + SEQ]
                sB = W[:, 2, :, :].rearrange("p k n -> p (k n)")[:, 1280:1280 + PAD + SEQ]
                pool.wait_ge(z_done, upto(l, 4 * T, 4 * T))
                pool.sem_inc(s_passed, 1)
                nc.gpsimd.memset(sA[:, 0:PAD], 0.0)
                nc.gpsimd.memset(uT[:, :, 0:PAD], 0.0)
                ch.link(nc.gpsimd.memset(sB[:, 0:PAD], 0.0))

                def stage(p, a):
                    r = slice(HD * a, HD * (a + 1))
                    ch.link(nc.gpsimd.tensor_copy(qst[r, :], qT[r, p, :]))
                    nc.gpsimd.tensor_copy(kst[r, :], kT[r, p, :]).then_inc(staged, 1)
                    pool.wait_ge(staged, upto(l, 2 * PAIRS, 2 * p + a + 1))
                    pool.sem_inc(s_passed, 1)

                for a in range(2):
                    stage(0, a)

                def pool_group(g):
                    win = POOL_WINDOWS[g]
                    u = uT[:, g, :]
                    src, step, bufs = u, 1, [sA, sB]
                    while step < win:
                        dst = bufs[0]
                        bufs.reverse()
                        ch.link(nc.gpsimd.tensor_tensor(out=dst[:, PAD:], in0=src[:, PAD:],
                                                        in1=src[:, PAD - step:PAD + SEQ - step], op=ALU.add))
                        src, step = dst, 2 * step
                    other = bufs[0]
                    n = win - 1
                    ch.link(nc.gpsimd.tensor_tensor(out=src[:, PAD:PAD + n], in0=src[:, PAD:PAD + n],
                                                    in1=cst[:, C_INV:C_INV + n], op=ALU.mult))
                    ch.link(nc.gpsimd.tensor_scalar(src[:, PAD + n:], src[:, PAD + n:], 1.0 / win, None, ALU.mult))
                    ins = nc.gpsimd.tensor_tensor(out=u[:, PAD:], in0=src[:, PAD:], in1=u[:, PAD:],
                                                  op=ALU.subtract)
                    ins.then_inc(pooled, 1)
                    pool.wait_ge(pooled, upto(l, NG, g + 1))
                    pool.sem_inc(s_passed, 1)

                pool_group(0)
                for p in range(1, PAIRS):
                    for a in range(2):
                        pool.wait_ge(s_done, upto(l, 16 * PAIRS, 16 * (p - 1) + 8 * (a + 1)))
                        pool.sem_inc(s_passed, 1)
                        stage(p, a)
                    pool_group(p)

                pool.wait_ge(at_ev, upto(l, 2 * PAIRS, 2 * PAIRS))
                pool.wait_ge(poolT_ready, upto(l, 2 * NG, 2 * NG))
                pool.sem_inc(s_passed, 1)

                def cat_tile(t, par, m):
                    if not first(t):
                        pool.wait_ge(op_done, upto(l, T, t - 1))
                        pool.sem_inc(s_passed, 1)
                    nc.gpsimd.tensor_copy(cat[par][:, 0:4, :], attT[:, :, ds(t * P, P)])
                    nc.gpsimd.tensor_copy(cat[par][:, 4:8, :], poolT[:, :, ds(t * P, P)]).then_inc(cat_ready, 1)

                steps(pool, T, cat_tile)

                pool.wait_ge(s_zero, 16 * 4)
                pool.wait_ge(xs2_saved, upto(l, T, T))
                pool.wait_ge(routed, upto(l, 1, 1))
                pool.sem_inc(s_passed, 1)
                for t in range(T):
                    for k in range(2):
                        pool.indirect_dma_start(
                            out=row_table, out_offset=bass.IndirectOffsetOnAxis(ap=pos_i[:, k, t:t + 1], axis=0),
                            in_=xs2_all[:, t, :], in_offset=None).then_inc(s_scat, 16)

                for i in range(RING):
                    pool.wait_ge(s_y[i], (l + 1) * (16 * USES[i]) + 1)
                    pool.sem_inc(s_passed, 1)
                for t in range(T):
                    if t >= 2:
                        pool.wait_ge(x_ready, upto(l + 1, T, t - 1))
                        pool.sem_inc(s_passed, 1)
                    for k in range(2):
                        pool.indirect_dma_start(
                            out=gath[t % 2][:, k, :], out_offset=None,
                            in_=y_table, in_offset=bass.IndirectOffsetOnAxis(ap=pos_i[:, k, t:t + 1], axis=0),
                        ).then_inc(s_gath[t % 2], 16)
                for t in range(T):
                    pool.wait_ge(x_ready, upto(l + 1, T, t + 1))
                    pool.sem_inc(s_passed, 1)
                    pool.dma_start(out[0, t * P:(t + 1) * P, :], xr[:, t, :]).then_inc(s_out, 16)
                pool.wait_ge(s_out, (l + 1) * (16 * T))

        @block.scalar
        def _(a_):
            sc = nc.scalar
            for s in (params, sd1, sqz_done, sdz, v_copied, u_copied, t_evac, p_ready, pt0_ev, at_ev, sd2,
                      xs2_saved, ge_exp, dm_exp, silu_done, aT_ready, y1_ready):
                a_.sem_inc(s, BIAS)
            for i in range(RING):
                a_.sem_inc(s_y[i], 1)
            wr = wr_all[:, 0:DEPTH * K * NR].rearrange("p (l k n) -> p l k n", l=DEPTH, k=K)
            for l in range(DEPTH):
                for src, at, n in ((norm1_gain, G1, K), (norm2_gain, G2, K), (pool_scale, PSC, NG)):
                    a_.dma_start(par_all[:, l, at:at + n], src[l, :].rearrange("(k p) -> p k", p=P)).then_inc(s_par, 16)
                for src, at, n in ((q_norm_gain, GQK, HD), (k_norm_gain, GQK + HD, HD), (b_group, BIAS_R, EG),
                                   (b_router, BIAS_R + EG, NE)):
                    a_.dma_start(par_all[:, l, at:at + n], src[l, :].partition_broadcast(P)).then_inc(s_par, 16)
                for src, at, n in ((w_group, 0, EG), (w_router, EG, NE)):
                    a_.dma_start(wr[:, l, :, at:at + n], src[l, :, :].rearrange("(k p) n -> p k n", p=P)).then_inc(s_par, 16)
            a_.wait_ge(s_par, DEPTH * 9 * 16)
            ch = Chain(a_, s_act)
            eps = st[:, 159:160]
            with a_.Fori(0, DEPTH) as l:
                ch.restart()
                a_.wait_ge(x_ready, upto(l, T, 1))
                sc.activation(par[:, :], par_all[:, l, :], ACT.Copy).then_inc(params, 1)

                def square_x(t, par_):
                    a_.wait_ge(x_ready, upto(l, T, t + 1))
                    if not first(t):
                        a_.wait_ge(xs_ready, upto(l, T, t))
                        a_.wait_ge(xt_done, upto(l, T, t - 1))
                    ch.link(sc.activation(xs[par_], xr[:, t, :], ACT.Square, accum_out=st[:, par_:par_ + 1]))
                    sc.activation(st[:, 2 + par_:3 + par_], st[:, par_:par_ + 1], ACT.Sqrt,
                                      bias=eps, scale=1.0 / D).then_inc(sd1, 1)

                def evac_turned(t):
                    for n, (dst, bank) in enumerate(((qT[:, :, ds(t * P, P)], 6), (kT[:, :, ds(t * P, P)], 7),
                                                     (uT[:, :, ds(PAD + t * P, P)], 6))):
                        a_.wait_ge(tqk_done, upto(l, 3 * T, 3 * t + n + 1))
                        sc.activation(dst, ps[:, bank, :].rearrange("p (a c) -> p a c", c=P), ACT.Copy).then_inc(t_evac, 1)

                square_x(0, 0)

                def in_act(t, par_, m):
                    if not last(t, T):
                        square_x(t + 1, 1 - par_)
                    for n in range(2):
                        a_.wait_ge(z_done, upto(l, 4 * T, 4 * t + n + 1))
                        sc.activation(sqz[:, 8 * n:8 * n + 8, :],
                                          ps[:, 2 + n, :].rearrange("p (h c) -> p h c", c=HD), ACT.Square).then_inc(sqz_done, 1)
                    a_.wait_ge(var_ready, upto(l, T, t + 1))
                    sc.activation(st[:, 32:48], st[:, 16:32], ACT.Sqrt).then_inc(sdz, 1)
                    if not first(t):
                        evac_turned(t - 1)
                    else:
                        a_.wait_ge(x_ready, upto(l, T, T))
                    a_.wait_ge(z_done, upto(l, 4 * T, 4 * t + 3))
                    sc.activation(v[:, t, :], ps[:, 4, :], ACT.Copy).then_inc(v_copied, 1)
                    a_.wait_ge(z_done, upto(l, 4 * T, 4 * t + 4))
                    sc.activation(u_nat, ps[:, 5, :].rearrange("p (g c) -> p g c", g=NG), ACT.Copy).then_inc(u_copied, 1)

                steps(a_, T, in_act, ch)
                evac_turned(T - 1)

                with a_.Fori(0, PAIRS) as p:
                    def exp(n):
                        i, b = n % T, n % 2
                        nk = (i + 1) * P
                        a_.wait_ge(sm_ready, upto(l, 16 * PAIRS, p * 16 + n + 1))
                        sc.activation(pr[b][:, 0:nk], pr[b][:, 0:nk], ACT.Exp, scale=-1.0,
                                          bias=st[:, 64 + n:65 + n], accum_out=st[:, 80 + n:81 + n]).then_inc(p_ready, 1)

                    exp(0)
                    for n in range(16):
                        i, b = n % T, n % 2
                        if n + 1 < 16:
                            exp(n + 1)
                        nb = min(i + 1, 4)
                        a_.wait_ge(pt0_done, upto(l, 16 * PAIRS, p * 16 + n + 1))
                        if n >= 2:
                            a_.wait_ge(pv_done, upto(l, 16 * PAIRS, p * 16 + n - 1))
                        sc.activation(prT[b][:, 0:nb, :], ps[:, 4, 0:nb * P]
                                          .rearrange("p (a c) -> p a c", c=P), ACT.Copy).then_inc(pt0_ev, 1)
                    for h in range(2):
                        a_.wait_ge(at_done, upto(l, 2 * PAIRS, p * 2 + h + 1))
                        sc.activation(attT[:, p, h * 512:(h + 1) * 512], ps[:, 4 + h, :], ACT.Copy).then_inc(at_ev, 1)

                ch.restart()

                def out_act(t, par_, m):
                    a_.wait_ge(x_upd, upto(l, T, t + 1))
                    if not first(t):
                        a_.wait_ge(xs2_ready, upto(l, T, t))
                    ch.link(sc.activation(junk2, xr[:, t, :], ACT.Square, accum_out=st[:, par_:par_ + 1]))
                    sc.activation(st[:, 2 + par_:3 + par_], st[:, par_:par_ + 1], ACT.Sqrt,
                                      bias=eps, scale=1.0 / D).then_inc(sd2, 1)
                    a_.wait_ge(xs2_ready, upto(l, T, t + 1))
                    sc.activation(xs2_all[:, t, :], xr[:, t, :], ACT.Copy,
                                      scale=st[:, 8 + par_:9 + par_]).then_inc(xs2_saved, 1)

                a_.wait_ge(pooled, upto(l, NG, NG))
                steps(a_, T, out_act, ch)

                a_.wait_ge(ge_ready, upto(l, 1, 1))
                sc.activation(R("ee"), R("ge"), ACT.Exp).then_inc(ge_exp, 1)
                a_.wait_ge(dm_ready, upto(l, 1, 1))
                sc.activation(R("e2"), R("dm"), ACT.Exp).then_inc(dm_exp, 1)

                def moe_down(t, slot, m):
                    a_.wait_ge(dn_done, upto(l, BLOCKS, t + 1))
                    a_.wait_ge(s_y[slot], l * (16 * USES[slot]) + 16 * m + 1)
                    sc.activation(y[slot][:, 512:1024], ps[:, 5, :], ACT.Copy).then_inc(y1_ready, 1)
                    a_.wait_ge(y0_ready, upto(l, BLOCKS, t + 1))
                    a_.wait_ge(y1_ready, upto(l, BLOCKS, t + 1))
                    a_.dma_start(y_table[ds(t * P, P), :], y[slot]).then_inc(s_y[slot], 16)

                def moe_act(t, slot, m):
                    a_.wait_ge(gu_done, upto(l, BLOCKS, t + 1))
                    sc.activation(sg, ps[:, 2, 0:FE], ACT.Silu).then_inc(silu_done, 1)
                    if not first(t):
                        moe_down(t - 1, *before(slot, m))
                    a_.wait_ge(a_t_done, upto(l, BLOCKS, t + 1))
                    sc.activation(aT, ps[:, 3, 0:FE].rearrange("p (k c) -> p k c", c=P), ACT.Copy).then_inc(aT_ready, 1)

                steps(a_, BLOCKS, moe_act, ring=RING)
                moe_down(BLOCKS - 1, (BLOCKS - 1) % RING, (BLOCKS - 1) // RING)

        @block.vector
        def _(dve):
            ve = nc.vector
            ch = Chain(dve, s_dve)
            for s in (xs_ready, hT_ready, var_ready, zqk_free, qk_ready, sm_ready, pt1_ev, o_ev,
                      poolT_ready, x_upd, xs2_ready, h2T_ready, logits, ge_ready, dm_ready, onehots, routed,
                      xgT_ready, a_ready, y0_ready):
                dve.sem_inc(s, BIAS)
            ch.link(ve.memset(wr_all[:, DEPTH * K * NR:], 0.0))
            dve.wait_ge(s_cst, 16)

            def rsqrt(ss, sd, r, tmp, scale, parts=((0, None, 1.0),)):
                ch.link(ve.tensor_scalar(tmp, ss, scale, EPS, ALU.mult, ALU.add))
                ch.link(ve.reciprocal(r, sd))
                ch.link(ve.tensor_tensor(out=tmp, in0=tmp, in1=r, op=ALU.mult))
                ch.link(ve.tensor_tensor(out=tmp, in0=tmp, in1=r, op=ALU.mult))
                for lo, hi, factor in parts:
                    ins = ve.tensor_scalar(tmp[:, lo:hi], tmp[:, lo:hi], -0.5 * factor, 1.5 * factor, ALU.mult, ALU.add)
                ch.link(ins)
                ch.link(ve.tensor_tensor(out=r, in0=tmp, in1=r, op=ALU.mult))

            def times_gain(dst, gain, banks, waited):
                for h in range(2):
                    ins = ve.tensor_tensor(out=dst[:, 4 * h:4 * h + 4, :],
                                           in0=ps[:, banks + h, :].rearrange("p (a c) -> p a c", c=P),
                                           in1=spread(par[:, gain + 4 * h:gain + 4 * h + 4], P), op=ALU.mult)
                ins.then_inc(waited, 1)

            with dve.Fori(0, DEPTH) as l:
                ch.restart()
                dve.wait_ge(params, upto(l, 1, 1))

                def norm_x(t, par_):
                    dve.wait_ge(sd1, upto(l, T, t + 1))
                    rsqrt(st[:, par_:par_ + 1], st[:, 2 + par_:3 + par_], st[:, 4 + par_:5 + par_],
                          st[:, 6:7], 1.0 / D)
                    ve.tensor_scalar(xs[par_], xr[:, t, :], st[:, 4 + par_:5 + par_], None, ALU.mult).then_inc(xs_ready, 1)

                norm_x(0, 0)

                def in_dve(t, par_, m):
                    dve.wait_ge(xt_done, upto(l, T, t + 1))
                    times_gain(hT[par_], G1, 0, hT_ready)
                    if not last(t, T):
                        norm_x(t + 1, 1 - par_)
                    dve.wait_ge(sqz_done, upto(l, 2 * T, 2 * t + 2))
                    ch.link(ve.tensor_reduce(st[:, 16:32], sqz, AX.X, ALU.add))
                    ch.link(ve.tensor_scalar(st[:, 16:32], st[:, 16:32], 1.0 / HD, EPS, ALU.mult, ALU.add))
                    dve.sem_inc(var_ready, 1)
                    dve.wait_ge(sdz, upto(l, T, t + 1))
                    r, tmp, var = st[:, 48:64], st[:, 96:112], st[:, 16:32]
                    ch.link(ve.reciprocal(r, st[:, 32:48]))
                    ch.link(ve.tensor_tensor(out=tmp, in0=var, in1=r, op=ALU.mult))
                    ch.link(ve.tensor_tensor(out=tmp, in0=tmp, in1=r, op=ALU.mult))
                    ve.tensor_scalar(tmp[:, 0:8], tmp[:, 0:8], -0.5 * HD ** -0.5, 1.5 * HD ** -0.5, ALU.mult, ALU.add)
                    ch.link(ve.tensor_scalar(tmp[:, 8:16], tmp[:, 8:16], -0.5, 1.5, ALU.mult, ALU.add))
                    ch.link(ve.tensor_tensor(out=r, in0=tmp, in1=r, op=ALU.mult))
                    z = zn[par_]
                    if not first(t):
                        dve.wait_ge(tqk_done, upto(l, 3 * T, 3 * t - 4))
                    for n in range(2):
                        ins = ve.tensor_tensor(out=z[:, 8 * n:8 * n + 8, :],
                                               in0=ps[:, 2 + n, :].rearrange("p (h c) -> p h c", c=HD),
                                               in1=spread(r[:, 8 * n:8 * n + 8], HD), op=ALU.mult)
                        ins.then_inc(zqk_free, 1)
                    dve.wait_ge(zqk_free, upto(l, 2 * T, 2 * t + 2))
                    for n in range(2):
                        g = par[:, GQK + HD * n:GQK + HD * (n + 1)].unsqueeze(1).to_broadcast([P, 8, HD])
                        ins = ve.tensor_tensor(out=z[:, 8 * n:8 * n + 8, :], in0=z[:, 8 * n:8 * n + 8, :], in1=g, op=ALU.mult)
                    ch.link(ins)
                    half = ROT // 2

                    def table(at, lo, n):
                        return cst[:, ds(at + lo + t * ROT, n)].unsqueeze(1).to_broadcast([P, 16, n])

                    ve.tensor_tensor(out=rope[:, 0, :, :], in0=z[:, :, 0:ROT], in1=table(C_COS, 0, ROT), op=ALU.mult)
                    ve.tensor_tensor(out=rope[:, 1, :, 0:half], in0=z[:, :, half:ROT], in1=table(C_SIN, 0, half), op=ALU.mult)
                    ch.link(ve.tensor_tensor(out=rope[:, 1, :, half:ROT], in0=z[:, :, 0:half],
                                             in1=table(C_SIN, half, half), op=ALU.mult))
                    ve.tensor_tensor(out=z[:, :, 0:ROT], in0=rope[:, 0, :, :], in1=rope[:, 1, :, :], op=ALU.add).then_inc(qk_ready, 1)

                steps(dve, T, in_dve, ch)

                dve.wait_ge(s_mask, 16)
                with dve.Fori(0, PAIRS) as p:
                    ch.restart()

                    def mask(n):
                        i, b = n % T, n % 2
                        nk = (i + 1) * P
                        if n >= 2:
                            j = n - 2
                            if j % T >= 4:
                                dve.wait_ge(pt1_done, upto(l, 8 * PAIRS, p * 8 + 4 * (j // T) + j % T - 3))
                            else:
                                dve.wait_ge(pt0_done, upto(l, 16 * PAIRS, p * 16 + j + 1))
                        dve.wait_ge(s_done, upto(l, 16 * PAIRS, p * 16 + n + 1))
                        dve.sem_inc(s_passed, 1)
                        ve.tensor_tensor_reduce(
                            out=pr[b][:, 0:nk], in0=ps[:, 2 * b:2 * b + 2, :].rearrange("p a c -> p (a c)")[:, 0:nk],
                            in1=cst[:, C_MASK + SEQ - nk:C_MASK + SEQ], scale=-1.0, scalar=3.0e38, op0=ALU.add,
                            op1=ALU.min, accum_out=st[:, 64 + n:65 + n]).then_inc(sm_ready, 1)

                    mask(0)
                    for n in range(16):
                        a, i, b = n // T, n % T, n % 2
                        if n + 1 < 16:
                            mask(n + 1)
                        if i >= 4:
                            dve.wait_ge(pt1_done, upto(l, 8 * PAIRS, p * 8 + 4 * a + i - 3))
                            if n >= 2:
                                dve.wait_ge(pv_done, upto(l, 16 * PAIRS, p * 16 + n - 1))
                            ve.tensor_copy(prT[b][:, 4:i + 1, :], ps[:, 5, 0:(i - 3) * P]
                                               .rearrange("p (a c) -> p a c", c=P)).then_inc(pt1_ev, 1)
                        dve.wait_ge(pv_done, upto(l, 16 * PAIRS, p * 16 + n + 1))
                        ch.link(ve.reciprocal(st[:, 112 + n:113 + n], st[:, 80 + n:81 + n]))
                        dve.wait_ge(at_done, upto(l, 2 * PAIRS, p * 2))
                        ve.tensor_scalar(att[:, i, HD * a:HD * (a + 1)], ps[:, 6 + b, HD * a:HD * (a + 1)],
                                             st[:, 112 + n:113 + n], None, ALU.mult).then_inc(o_ev, 1)

                for n in range(2 * NG):
                    g, h = n // 2, n % 2
                    dve.wait_ge(pm_done, upto(l, 2 * NG, n + 1))
                    ve.tensor_scalar(poolT[:, g, 512 * h:512 * h + 512], ps[:, n % 4, :],
                                         par[:, PSC + g:PSC + g + 1], None, ALU.mult).then_inc(poolT_ready, 1)

                ch.restart()

                def add_bias(t, par_):
                    dve.wait_ge(rt_done, upto(l, T, t + 1))
                    ve.tensor_tensor(out=R("lg", NR)[:, ds(t, 1), :],
                                         in0=ps[:, 6 + par_, 0:NR].unsqueeze(1),
                                         in1=par[:, BIAS_R:BIAS_R + NR].unsqueeze(1), op=ALU.add).then_inc(logits, 1)

                def gain2(t, par_):
                    dve.wait_ge(xt2_done, upto(l, T, t + 1))
                    times_gain(h2T[par_], G2, 4, h2T_ready)

                def out_dve(t, par_, m):
                    if not first(t):
                        gain2(t - 1, 1 - par_)
                    dve.wait_ge(op_done, upto(l, T, t + 1))
                    ve.tensor_tensor(out=xr[:, t, :], in0=ps[:, 2 * par_:2 * par_ + 2, :].rearrange("p a c -> p (a c)"),
                                         in1=xr[:, t, :], op=ALU.add).then_inc(x_upd, 1)
                    dve.wait_ge(sd2, upto(l, T, t + 1))
                    if not first(t):
                        dve.wait_ge(xs2_saved, upto(l, T, t))
                    r = st[:, 8 + par_:9 + par_]
                    rsqrt(st[:, par_:par_ + 1], st[:, 2 + par_:3 + par_], r, st[:, 6:7], 1.0 / D)
                    ve.tensor_scalar(xs2[par_], xr[:, t, :], r, None, ALU.mult).then_inc(xs2_ready, 1)
                    if not first(t):
                        add_bias(t - 1, 1 - par_)

                steps(dve, T, out_dve, ch)
                gain2(T - 1, (T - 1) % 2)
                add_bias(T - 1, (T - 1) % 2)
                dve.wait_ge(logits, upto(l, T, T))

                lg = R("lg", NR)
                gl, el = lg[:, :, 0:EG], lg[:, :, EG:NR]
                dsc = desc.unsqueeze(1).to_broadcast([P, T, 4])

                def tt(out_, a, b, op):
                    ch.link(ve.tensor_tensor(out=out_, in0=a, in1=b, op=op))

                def first_of_max(vals, m, onehot):
                    tt(R("is1", 4), vals, spread(m, 4), ALU.is_equal)
                    tt(R("is1", 4), R("is1", 4), dsc, ALU.mult)
                    ch.link(ve.tensor_reduce(R("sm"), R("is1", 4), AX.X, ALU.max))
                    tt(onehot, dsc, spread(R("sm"), 4), ALU.is_equal)

                ch.link(ve.tensor_reduce(R("gm"), gl, AX.X, ALU.max))
                ch.link(ve.tensor_tensor(out=R("ge", EG), in0=gl, in1=spread(R("gm"), EG), op=ALU.subtract))
                dve.sem_inc(ge_ready, 1)
                first_of_max(gl, R("gm"), R("goh", EG))
                tmp4 = R("tmp")[:, 0:T * 16].rearrange("p (t e g) -> p t e g", e=EPG, g=EG)
                tt(tmp4, el.rearrange("p t (g e) -> p t e g", g=EG),
                   R("goh", EG).unsqueeze(2).to_broadcast([P, T, EPG, EG]), ALU.mult)
                ch.link(ve.tensor_reduce(R("es", EPG), tmp4, AX.X, ALU.add))
                ch.link(ve.tensor_reduce(R("m1"), R("es", EPG), AX.X, ALU.max))
                first_of_max(R("es", EPG), R("m1"), R("oh1", 4))
                ch.link(ve.scalar_tensor_tensor(out=R("es2"), in0=R("oh1"), scalar=NEG, in1=R("es"),
                                                op0=ALU.mult, op1=ALU.add))
                ch.link(ve.tensor_reduce(R("m2"), R("es2", EPG), AX.X, ALU.max))
                tt(R("dm"), R("m2"), R("m1"), ALU.subtract)
                dve.sem_inc(dm_ready, 1)
                first_of_max(R("es2", EPG), R("m2"), R("oh2", 4))
                for OH, oh in (("OH1", "oh1"), ("OH2", "oh2")):
                    tt(R(OH).rearrange("p (t g e) -> p t g e", g=EG, e=EPG),
                       R("goh", EG).unsqueeze(3).to_broadcast([P, T, EG, EPG]),
                       R(oh, 4).unsqueeze(2).to_broadcast([P, T, EG, EPG]), ALU.mult)
                ve.tensor_tensor(out=R("M"), in0=R("OH1"), in1=R("OH2"), op=ALU.add).then_inc(onehots, 1)
                dve.wait_ge(ge_exp, upto(l, 1, 1))
                ch.link(ve.tensor_reduce(R("gs"), R("ee", EG), AX.X, ALU.add))
                ch.link(ve.reciprocal(R("pt"), R("gs")))
                dve.wait_ge(dm_exp, upto(l, 1, 1))
                ch.link(ve.tensor_scalar(R("rd"), R("e2"), 1.0, None, ALU.add))
                ch.link(ve.reciprocal(R("rd"), R("rd")))
                tt(gate_w[:, 0, :], R("rd"), R("pt"), ALU.mult)
                tt(gate_w[:, 1, :], gate_w[:, 0, :], R("e2"), ALU.mult)
                dve.wait_ge(ranks, upto(l, 1, 1))
                ch.link(ve.tensor_copy(R("tot"), ps[:, 1, 0:T * NE]))
                tot, off = R("tot", NE), R("off", NE)
                ch.link(ve.memset(off[:, 0, :], 0.0))
                for t in range(1, T):
                    tt(off[:, t, :], off[:, t - 1, :], tot[:, t - 1, :], ALU.add)
                tt(R("cnt"), off[:, T - 1, :], tot[:, T - 1, :], ALU.add)
                big = R("tmp")[:, 0:NE * T].rearrange("p (e t) -> p e t", t=T)
                tt(big, spread(R("cnt"), T), cst[:, C_THR:C_THR + T].unsqueeze(1).to_broadcast([P, NE, T]), ALU.is_gt)
                ch.link(ve.tensor_reduce(R("te"), big, AX.X, ALU.add))
                big = R("tmp")[:, 0:NE * NE].rearrange("p (e f) -> p e f", f=NE)
                tt(big, R("te").unsqueeze(1).to_broadcast([P, NE, NE]),
                   cst[:, C_LT:C_LT + NE * NE].rearrange("p (e f) -> p e f", f=NE), ALU.mult)
                ch.link(ve.tensor_reduce(R("start"), big, AX.X, ALU.add))
                big = R("tmp").rearrange("p (j e) -> p j e", e=NE)
                tt(big, cst[:, C_JJ:C_JJ + 32].unsqueeze(2).to_broadcast([P, 32, NE]),
                   R("start").unsqueeze(1).to_broadcast([P, 32, NE]), ALU.is_ge)
                ch.link(ve.tensor_reduce(R("bef"), big, AX.X, ALU.add))
                ch.link(ve.tensor_scalar(block_e[:, :], R("bef"), -1.0, None, ALU.add))
                base = R("base", NE)
                ch.link(ve.scalar_tensor_tensor(out=base, in0=R("start").unsqueeze(1).to_broadcast([P, T, NE]),
                                                scalar=float(P), in1=off, op0=ALU.mult, op1=ALU.add))
                ch.link(ve.tensor_tensor(out=R("base"), in0=ps[:, 0, 0:T * NE], in1=R("base"), op=ALU.add))
                for k, OH in enumerate(("OH1", "OH2")):
                    tt(R("tmp")[:, 0:T * NE], R(OH), R("base"), ALU.mult)
                    ch.link(ve.tensor_reduce(R("posf")[:, k * T:(k + 1) * T],
                                             R("tmp")[:, 0:T * NE].rearrange("p (t e) -> p t e", e=NE), AX.X, ALU.add))
                ve.tensor_copy(pos_i[:, :, :].rearrange("p k t -> p (k t)"), R("posf")).then_inc(routed, 1)

                def rows_evac(t):
                    dve.wait_ge(xtm_done, upto(l, BLOCKS, t + 1))
                    times_gain(xgT, G2, 0, xgT_ready)

                def y_evac(t, slot, m):
                    dve.wait_ge(dn_done, upto(l, BLOCKS, t + 1))
                    dve.wait_ge(s_y[slot], l * (16 * USES[slot]) + 16 * m + 1)
                    ve.tensor_copy(y[slot][:, 0:512], ps[:, 4, :]).then_inc(y0_ready, 1)

                rows_evac(0)

                def moe_dve(t, slot, m):
                    if not last(t, BLOCKS):
                        rows_evac(t + 1)
                    dve.wait_ge(silu_done, upto(l, BLOCKS, t + 1))
                    ve.tensor_tensor(out=act, in0=ps[:, 2, FE:2 * FE], in1=sg, op=ALU.mult).then_inc(a_ready, 1)
                    if not first(t):
                        y_evac(t - 1, *before(slot, m))

                steps(dve, BLOCKS, moe_dve, ring=RING)
                y_evac(BLOCKS - 1, (BLOCKS - 1) % RING, (BLOCKS - 1) // RING)

                ch.restart()
                for t in range(T):
                    b = t % 2
                    dve.wait_ge(s_gath[b], l * (16 * 2 * (T // 2)) + 32 * (t // 2 + 1))
                    ch.link(ve.scalar_tensor_tensor(out=xr[:, t, :], in0=gath[b][:, 0, :], scalar=gate_w[:, 0, t:t + 1],
                                                    in1=xr[:, t, :], op0=ALU.mult, op1=ALU.add))
                    ve.scalar_tensor_tensor(out=xr[:, t, :], in0=gath[b][:, 1, :], scalar=gate_w[:, 1, t:t + 1],
                                                in1=xr[:, t, :], op0=ALU.mult, op1=ALU.add).then_inc(x_ready, 1)

        @block.tensor
        def _(pe):
            te = nc.tensor
            for s in (xt_done, z_done, tqk_done, s_done, pt0_done, pt1_done, pv_done, at_done, pm_done,
                      op_done, xt2_done, rt_done, ranks, xtm_done, gu_done, a_t_done, dn_done):
                pe.sem_inc(s, BIAS)
            pe.wait_ge(s_cst, 16)

            def transposes(bank, srcs):
                for i, src in enumerate(srcs):
                    ins = te.transpose(ps[:, bank + i // 4, (i % 4) * P:(i % 4 + 1) * P], src, ident)
                return ins

            def cols(ap, n):
                return [ap[:, i * P:(i + 1) * P] for i in range(n)]

            with pe.Fori(0, DEPTH) as l:
                def xt(t, par_):
                    pe.wait_ge(xs_ready, upto(l, T, t + 1))
                    transposes(0, cols(xs[par_], K)).then_inc(xt_done, 1)

                def z(t, par_, c):
                    for k in range(K):
                        ins = te.matmul(ps[:, 2 + c, :], hT[par_][:, k, :], W[:, c, k, :], start=k == 0, stop=k == K - 1)
                    ins.then_inc(z_done, 1)

                def turn(t, par_):
                    zr = zn[par_].rearrange("p h c -> p (h c)")
                    pe.wait_ge(qk_ready, upto(l, T, t + 1))
                    pe.wait_ge(t_evac, upto(l, 3 * T, 3 * t))
                    transposes(6, cols(zr[:, 0:ATT], 4)).then_inc(tqk_done, 1)
                    transposes(7, cols(zr[:, ATT:2 * ATT], 4)).then_inc(tqk_done, 1)
                    pe.wait_ge(u_copied, upto(l, T, t + 1))
                    pe.wait_ge(t_evac, upto(l, 3 * T, 3 * t + 1))
                    transposes(6, [u_nat[:, g, :] for g in range(NG)]).then_inc(tqk_done, 1)

                xt(0, 0)

                def in_pe(t, par_, m):
                    pe.wait_ge(hT_ready, upto(l, T, t + 1))
                    for c in range(4):
                        if first(t):
                            pe.wait_ge(s_win[c], (l + 1) * 16)
                        elif c < 2:
                            pe.wait_ge(zqk_free, upto(l, 2 * T, 2 * t - 1 + c))
                        elif c == 2:
                            pe.wait_ge(v_copied, upto(l, T, t))
                        else:
                            pe.wait_ge(u_copied, upto(l, T, t))
                        z(t, par_, c)
                        if c == 0 and not last(t, T):
                            xt(t + 1, 1 - par_)
                        if c == 1 and not first(t):
                            turn(t - 1, 1 - par_)

                steps(pe, T, in_pe)
                turn(T - 1, (T - 1) % 2)

                pe.wait_ge(t_evac, upto(l, 3 * T, 3 * T))
                pe.wait_ge(v_copied, upto(l, T, T))
                pe.wait_ge(zqk_free, upto(l, 2 * T, 2 * T))
                pe.sem_inc(s_passed, 1)
                with pe.Fori(0, PAIRS) as p:
                    def scores(n):
                        a, i, b = n // T, n % T, n % 2
                        r = slice(HD * a, HD * (a + 1))
                        if i == 0:
                            pe.wait_ge(staged, upto(l, 2 * PAIRS, p * 2 + a + 1))
                        if n >= 2:
                            pe.wait_ge(sm_ready, upto(l, 16 * PAIRS, p * 16 + n - 1))
                        nk = (i + 1) * P
                        for c in range(0, nk, 512):
                            w = min(512, nk - c)
                            ins = te.matmul(ps[:, 2 * b + c // 512, 0:w], qst[r, i * P:(i + 1) * P], kst[r, c:c + w],
                                            start=True, stop=True)
                        ins.then_inc(s_done, 1)

                    pe.wait_ge(sm_ready, upto(l, 16 * PAIRS, p * 16))
                    scores(0)
                    scores(1)
                    pe.wait_ge(at_ev, upto(l, 2 * PAIRS, p * 2))
                    pe.wait_ge(o_ev, upto(l, 16 * PAIRS, p * 16))
                    for n in range(16):
                        a, i, b = n // T, n % T, n % 2
                        pe.wait_ge(p_ready, upto(l, 16 * PAIRS, p * 16 + n + 1))
                        if n >= 1:
                            pe.wait_ge(pt0_ev, upto(l, 16 * PAIRS, p * 16 + n))
                        blocks = cols(pr[b], i + 1)
                        transposes(4, blocks[0:4]).then_inc(pt0_done, 1)
                        if i >= 4:
                            done = 4 * a + i - 4
                            pe.wait_ge(pt1_ev, upto(l, 8 * PAIRS, p * 8 + done))
                            transposes(5, blocks[4:]).then_inc(pt1_done, 1)
                        if n + 2 < 16:
                            scores(n + 2)
                        pe.wait_ge(pt0_ev, upto(l, 16 * PAIRS, p * 16 + n + 1))
                        if i >= 4:
                            pe.wait_ge(pt1_ev, upto(l, 8 * PAIRS, p * 8 + done + 1))
                        if n >= 2:
                            pe.wait_ge(o_ev, upto(l, 16 * PAIRS, p * 16 + n - 1))
                        for j in range(i + 1):
                            ins = te.matmul(ps[:, 6 + b, 0:P], prT[b][:, j, :], v[:, j, ds(p * P, P)],
                                            start=j == 0, stop=j == i)
                        ins.then_inc(pv_done, 1)
                    pe.wait_ge(o_ev, upto(l, 16 * PAIRS, p * 16 + 16))
                    for h in range(2):
                        transposes(4 + h, [att[:, 4 * h + i, :] for i in range(4)]).then_inc(at_done, 1)

                pe.wait_ge(s_wpool, (l + 1) * 16)
                pe.wait_ge(pooled, upto(l, NG, NG))
                for n in range(2 * NG):
                    g, h = n // 2, n % 2
                    if n >= 4:
                        pe.wait_ge(poolT_ready, upto(l, 2 * NG, n - 3))
                    te.matmul(ps[:, n % 4, :], wpool[:, g, :], uT[:, g, PAD + 512 * h:PAD + 512 * h + 512],
                                  start=True, stop=True).then_inc(pm_done, 1)

                pe.wait_ge(poolT_ready, upto(l, 2 * NG, 2 * NG))
                pe.wait_ge(at_ev, upto(l, 2 * PAIRS, 2 * PAIRS))

                def project(par_, h):
                    for k in range(K):
                        ins = te.matmul(ps[:, 2 * par_ + h, :], cat[par_][:, k, :], w_o[h][:, k, :],
                                        start=k == 0, stop=k == K - 1)
                    return ins

                def xt2(t, par_):
                    pe.wait_ge(xs2_ready, upto(l, T, t + 1))
                    if not first(t):
                        pe.wait_ge(h2T_ready, upto(l, T, t))
                    transposes(4, cols(xs2[par_], K)).then_inc(xt2_done, 1)

                def router(t, par_):
                    pe.wait_ge(h2T_ready, upto(l, T, t + 1))
                    for k in range(K):
                        ins = te.matmul(ps[:, 6 + par_, 0:P], h2T[par_][:, k, :],
                                        wr_all[:, ds(l * (K * NR) + k * NR, P)],
                                        start=k == 0, stop=k == K - 1)
                    ins.then_inc(rt_done, 1)

                def out_pe(t, par_, m):
                    if first(t):
                        for h in range(2):
                            pe.wait_ge(s_wout[h], (l + 1) * 16)
                    else:
                        pe.wait_ge(x_upd, upto(l, T, t - 1))
                    pe.wait_ge(cat_ready, upto(l, T, t + 1))
                    project(par_, 0)
                    if not first(t):
                        xt2(t - 1, 1 - par_)
                    project(par_, 1).then_inc(op_done, 1)
                    if not first(t):
                        pe.wait_ge(logits, upto(l, T, t - 1))
                        router(t - 1, 1 - par_)

                steps(pe, T, out_pe)
                xt2(T - 1, (T - 1) % 2)
                router(T - 1, (T - 1) % 2)

                pe.wait_ge(onehots, upto(l, 1, 1))
                te.matmul(ps[:, 0, 0:T * NE], low, R("M"), start=True, stop=True)
                te.matmul(ps[:, 1, 0:T * NE], ones, R("M"), start=True, stop=True).then_inc(ranks, 1)

                def xtm(t, slot, m):
                    pe.wait_ge(s_xg[slot], l * (16 * USES[slot]) + 16 * (m + 1))
                    if first(t):
                        pe.wait_ge(routed, upto(l, 1, 1))
                    else:
                        pe.wait_ge(xgT_ready, upto(l, BLOCKS, t))
                    transposes(0, cols(xg[slot], K)).then_inc(xtm_done, 1)

                def down(t, slot, m):
                    pe.wait_ge(aT_ready, upto(l, BLOCKS, t + 1))
                    pe.wait_ge(s_d[slot], l * (16 * USES[slot]) + 16 * (m + 1))
                    if not first(t):
                        pe.wait_ge(y0_ready, upto(l, BLOCKS, t))
                        pe.wait_ge(y1_ready, upto(l, BLOCKS, t))
                    for h in range(2):
                        for k in range(2):
                            ins = te.matmul(ps[:, 4 + h, :], aT[:, k, :], wd[slot][:, k, 512 * h:512 * h + 512],
                                            start=k == 0, stop=k == 1)
                    ins.then_inc(dn_done, 1)

                xtm(0, 0, 0)

                def moe_pe(t, slot, m):
                    pe.wait_ge(xgT_ready, upto(l, BLOCKS, t + 1))
                    pe.wait_ge(s_gu[slot], l * (32 * USES[slot]) + 32 * (m + 1))
                    if not first(t):
                        pe.wait_ge(a_ready, upto(l, BLOCKS, t))
                    for k in range(K):
                        ins = te.matmul(ps[:, 2, :], xgT[:, k, :], wgu[slot][:, k, :], start=k == 0, stop=k == K - 1)
                    ins.then_inc(gu_done, 1)
                    if not last(t, BLOCKS):
                        xtm(t + 1, *after(slot, m))
                    if not first(t):
                        down(t - 1, *before(slot, m))
                    pe.wait_ge(a_ready, upto(l, BLOCKS, t + 1))
                    transposes(3, cols(act, 2)).then_inc(a_t_done, 1)

                steps(pe, BLOCKS, moe_pe, ring=RING)
                down(BLOCKS - 1, (BLOCKS - 1) % RING, (BLOCKS - 1) // RING)


_INS = ["x", "norm1_gain", "w_in", "q_norm_gain", "k_norm_gain", "w_pool", "pool_scale", "w_out", "norm2_gain",
        "w_group", "b_group", "w_router", "b_router", "w_gate", "w_up", "w_down"]


def kernel(**inputs):
    import concourse.bacc as bacc
    from concourse.bass_utils import run_bass_kernel_spmd

    nc = bacc.Bacc("TRN2", target_bir_lowering=False, num_devices=1)
    arrays = {n: np.ascontiguousarray(inputs[n]) for n in _INS}
    arrays["consts"] = shape_constants()
    args = [nc.dram_tensor(f"in_{n}", a.shape, mybir.dt.from_np(a.dtype), kind="ExternalInput").ap()
            for n, a in arrays.items()]
    args.append(nc.dram_tensor("out_x", (1, SEQ, D), mybir.dt.float32, kind="ExternalOutput").ap())
    trunk(nc, *args)
    r = run_bass_kernel_spmd(nc, [{f"in_{n}": a for n, a in arrays.items()}], core_ids=[0])
    return r.results[0]["out_x"]
```

```python
import math
from contextlib import ExitStack

import numpy as np

import concourse.bass as bass
from concourse import mybir

P = 128
DEPTH, SEQ, D = 2, 1024, 1024
HEADS, HD = 8, 64
ATT = HEADS * HD
NG, GD = 4, 128
POOL_WINDOWS = (2, 4, 8, 16)
BRANCHES = ((128, 1), (512, 4), (2048, 16))
ROT, THETA = HD // 4, 500000.0
EG, EPG = 4, 4
NE, FE = EG * EPG, 256
EPS = 1e-6
NEG = -1e30

T = SEQ // P
K = D // P
PAIRS = HEADS // 2
BLOCKS = (2 * SEQ - NE) // P + NE
ROWS = BLOCKS * P
NR = EG + NE

C_MASK, C_ID, C_LOW, C_ONE = 0, SEQ, SEQ + P, SEQ + 2 * P
C_COS = C_ONE + P
C_SIN = C_COS + T * ROT
C_JJ = C_SIN + T * ROT
C_DESC = C_JJ + 32
C_THR = C_DESC + 4
C_LT = C_THR + T
C_INV = C_LT + NE * NE
C_ALL = C_INV + 16

G1, G2, PSC = 0, K, 2 * K
GQK = 2 * K + NG
BIAS_R = GQK + 2 * HD
NPAR = BIAS_R + NR

RING = 3
SLOTS = 4
BIAS = RING - 1


def shape_constants():
    c = np.zeros((P, C_ALL), np.float32)
    row = np.arange(P)[:, None]
    dist = (T - 1) * P + row - np.arange(SEQ)[None, :]
    count = np.zeros(dist.shape, np.int64)
    for window, dilation in BRANCHES:
        count += (dist >= 0) & (dist <= window) & (dist % dilation == 0)
    c[:, C_MASK:C_MASK + SEQ] = np.where(count > 0, np.log(np.maximum(count, 1)), NEG)
    c[:, C_ID:C_ID + P] = np.eye(P)
    c[:, C_LOW:C_LOW + P] = row < np.arange(P)[None, :]
    c[:, C_ONE:C_ONE + P] = 1.0
    inv_freq = np.float32(THETA) ** (-np.arange(0, ROT, 2, dtype=np.float32) / np.float32(ROT))
    ang = np.arange(SEQ, dtype=np.float32)[:, None] * inv_freq.astype(np.float32)[None, :]
    cos, sin = np.cos(ang).astype(np.float32), np.sin(ang).astype(np.float32)
    both = np.concatenate([cos, cos], 1), np.concatenate([-sin, sin], 1)
    for at, table in zip((C_COS, C_SIN), both):
        c[:, at:at + T * ROT] = table.reshape(T, P, ROT).transpose(1, 0, 2).reshape(P, T * ROT)
    c[:, C_JJ:C_JJ + 32] = np.arange(32)
    c[:, C_DESC:C_DESC + 4] = 4 - np.arange(4)
    c[:, C_THR:C_THR + T] = P * np.arange(T)
    e = np.arange(NE)
    c[:, C_LT:C_LT + NE * NE] = (e[None, :] < e[:, None]).reshape(-1)
    c[:, C_INV:C_INV + 16] = 1.0 / (1.0 + np.arange(16))
    return c


def trunk(nc, x, norm1_gain, w_in, q_norm_gain, k_norm_gain, w_pool, pool_scale, w_out,
          norm2_gain, w_group, b_group, w_router, b_router, w_gate, w_up, w_down, consts, out):
    f32, i32, bf16 = mybir.dt.float32, mybir.dt.int32, mybir.dt.bfloat16
    ALU, ACT, AX = mybir.AluOpType, mybir.ActivationFunctionType, mybir.AxisListType
    ds = bass.ds

    ctx = ExitStack()
    with ctx:
        def sb(name, shape, dt=f32):
            return ctx.enter_context(nc.sbuf_tensor(name, shape, dt))

        def sem(name):
            return ctx.enter_context(nc.semaphore(name))

        ctx.enter_context(nc.allow_non_contiguous_dma(reason="small parameters, once"))
        row_table = nc.dram_tensor("row_table", (ROWS, D), f32, kind="Internal").ap()
        y_table = nc.dram_tensor("y_table", (ROWS, D), f32, kind="Internal").ap()

        xr = sb("x_res", [P, T, D])
        PAD = 16
        AT_V = 4 * K * 512
        AT_U = AT_V + T * ATT
        AT_K = AT_U + NG * (PAD + SEQ)
        AT_Q = AT_K + 4 * SEQ
        big = sb("big", [P, AT_Q + 4 * SEQ])
        W = big[:, 0:AT_V].rearrange("p (c k n) -> p c k n", c=4, k=K)
        v_r = big[:, AT_V:AT_U]
        uT = big[:, AT_U:AT_K].rearrange("p (g s) -> p g s", g=NG)
        kT_r = big[:, AT_K:AT_Q]
        qT_r = big[:, AT_Q:AT_Q + 4 * SEQ]
        A = sb("arena", [P, 8192])
        cst = sb("cst", [P, C_ALL])
        zero = sb("zero", [P, 256])
        par_all = sb("par_all", [P, DEPTH, NPAR])
        par = sb("par", [P, NPAR])
        wr_all = sb("wr_all", [P, DEPTH * K * NR + P])
        wpool = sb("wpool", [P, NG, GD])
        st = sb("st", [P, 160])
        gate_w = sb("gate_w", [P, 2, T])
        pos_i = sb("pos_i", [P, 2, T], i32)
        block_e = sb("block_e", [P, 32], i32)
        start_i = sb("start_i", [P, NE + 1], i32)
        ps = ctx.enter_context(nc.psum_tensor("ps", [P, 8, 512], f32))

        qT = qT_r[:, :].rearrange("p (a s) -> p a s", a=PAIRS)
        kT = kT_r[:, :].rearrange("p (a s) -> p a s", a=PAIRS)
        attT, poolT = qT, kT
        v = v_r[:, :].rearrange("p (t c) -> p t c", t=T)
        w_o = [W[:, h, :, :] for h in range(2)]
        par_rows = kT_r[0:DEPTH * GQK, 0:P]
        AT_E, E_GU, E_ALL = AT_V // 2, K * 2 * FE, K * 2 * FE + 2 * D
        assert AT_E + SLOTS * E_ALL <= AT_Q + 4 * SEQ
        w_gu = [big[:, AT_E + i * E_ALL:AT_E + i * E_ALL + E_GU].rearrange("p (k n) -> p k n", k=K)
                for i in range(SLOTS)]
        w_dn = [big[:, AT_E + i * E_ALL + E_GU:AT_E + (i + 1) * E_ALL].rearrange("p (k n) -> p k n", k=2)
                for i in range(SLOTS)]
        gath = [qT_r[:, 2048 * i:2048 * i + 2048].rearrange("p (k n) -> p k n", k=2) for i in range(2)]

        def ring(at, size, n=2, inner=None):
            r = [A[:, at + size * i:at + size * (i + 1)] for i in range(n)]
            return [a.rearrange("p (k n) -> p k n", n=inner) for a in r] if inner else r

        rope = A[:, 0:512].rearrange("p (a h c) -> p a h c", a=2, h=16)
        u_nat = A[:, 512:1024].rearrange("p (g c) -> p g c", g=NG)
        xs = ring(1024, D)
        hT = ring(3072, D, inner=P)
        zn = ring(5120, D, inner=HD)
        sqz = A[:, 7168:8192].rearrange("p (h c) -> p h c", c=HD)
        qst, kst = A[:, 0:1024], A[:, 1024:2048]
        att = A[:, 2048:3072].rearrange("p (t c) -> p t c", c=P)
        prT = ring(3072, SEQ, inner=P)
        pr = ring(5120, SEQ)
        cat = ring(0, D, inner=P)
        xs2 = ring(2048, D)
        h2T = ring(4096, D, inner=P)
        to_scat = ring(2048, D, 4)
        junk2 = A[:, 6144:6656].bitcast(bf16)
        xg = ring(0, D, RING)
        xgT = A[:, 3072:4096].rearrange("p (k n) -> p k n", n=P)
        sg, act = A[:, 4096:4352], A[:, 4352:4608]
        aT = A[:, 4608:4864].rearrange("p (k n) -> p k n", n=P)
        y = ring(4864, D, RING)

        ident = cst[:, C_ID:C_ID + P]
        low = cst[:, C_LOW:C_LOW + P]
        ones = cst[:, C_ONE:C_ONE + P]
        desc = cst[:, C_DESC:C_DESC + 4]

        x_ready = sem("x_ready")
        params = sem("params")
        sd1 = sem("sd1")
        xs_ready = sem("xs_ready")
        xt_done = sem("xt_done")
        hT_ready = sem("hT_ready")
        z_done = sem("z_done")
        sqz_done = sem("sqz_done")
        var_ready = sem("var_ready")
        sdz = sem("sdz")
        zqk_free = sem("zqk_free")
        v_copied = sem("v_copied")
        u_copied = sem("u_copied")
        qk_ready = sem("qk_ready")
        tqk_done = sem("tqk_done")
        t_evac = sem("t_evac")
        pooled = sem("pooled")
        staged = sem("staged")
        s_done = sem("s_done")
        sm_ready = sem("sm_ready")
        p_ready = sem("p_ready")
        pt0_done = sem("pt0_done")
        pt1_done = sem("pt1_done")
        pt0_ev = sem("pt0_ev")
        pt1_ev = sem("pt1_ev")
        pv_done = sem("pv_done")
        o_ev = sem("o_ev")
        at_done = sem("at_done")
        at_ev = sem("at_ev")
        pm_done = sem("pm_done")
        poolT_ready = sem("poolT_ready")
        cat_ready = sem("cat_ready")
        op_done = sem("op_done")
        x_upd = sem("x_upd")
        sd2 = sem("sd2")
        xs2_ready = sem("xs2_ready")
        xs2_saved = sem("xs2_saved")
        xt2_done = sem("xt2_done")
        h2T_ready = sem("h2T_ready")
        rt_done = sem("rt_done")
        logits = sem("logits")
        ge_ready = sem("ge_ready")
        ge_exp = sem("ge_exp")
        dm_ready = sem("dm_ready")
        dm_exp = sem("dm_exp")
        onehots = sem("onehots")
        ranks = sem("ranks")
        routed = sem("routed")
        w_loaded = sem("w_loaded")
        xtm_done = sem("xtm_done")
        xgT_ready = sem("xgT_ready")
        gu_done = sem("gu_done")
        silu_done = sem("silu_done")
        a_ready = sem("a_ready")
        a_t_done = sem("a_t_done")
        aT_ready = sem("aT_ready")
        dn_done = sem("dn_done")
        y0_ready = sem("y0_ready")
        y1_ready = sem("y1_ready")
        rows_t = sem("rows_t")
        rows_in = sem("rows_in")
        s_passed = sem("s_passed")

        def upto(l, per_layer, n):
            return l * per_layer + n + BIAS

        s_cst, s_x, s_par = sem("s_cst"), [sem(f"s_x{t}") for t in range(T)], sem("s_par")
        s_rows, s_wr = sem("s_rows"), sem("s_wr")
        s_mask = sem("s_mask")
        s_win = [sem(f"s_win{c}") for c in range(4)]
        s_wout = [sem(f"s_wout{c}") for c in range(2)]
        s_wpool, s_zero = sem("s_wpool"), sem("s_zero")
        s_scat = [sem(f"s_scat{i}") for i in range(4)]
        s_w = [sem(f"s_w{i}") for i in range(SLOTS)]
        s_xg = [sem(f"s_xg{i}") for i in range(RING)]
        s_y = [sem(f"s_y{i}") for i in range(RING)]
        s_gath = [sem(f"s_gath{i}") for i in range(2)]
        s_out = sem("s_out")
        s_ms = sem("s_ms")
        s_dve, s_act, s_pool = sem("s_dve"), sem("s_act"), sem("s_pool")

        USES = [(BLOCKS + RING - 1 - i) // RING for i in range(RING)]

        class Chain:

            def __init__(self, eng, s):
                self.eng, self.s, self.n = eng, s, 0

            def link(self, ins):
                ins.then_inc(self.s, 1)
                self.n += 1
                self.eng.wait_ge(self.s, self.n)

            def restart(self):
                self.eng.sem_clear(self.s)
                self.n = 0

        def steps(eng, n, body, chain=None, ring=2, sure=0, maybe=None):
            body(0, 0, 0)
            loops = (n - 2) // ring
            for lo, hi in ((0, sure), (sure, loops)):
                if lo == hi:
                    continue
                if maybe and lo == sure:
                    body = maybe
                with eng.Fori(lo, hi) as j:
                    if chain:
                        chain.restart()
                    for i in range(1, ring + 1):
                        body(ring * j + i, i % ring, j + i // ring)
            if chain:
                chain.restart()
            for t in range(1 + ring * loops, n):
                body(t, t % ring, t // ring)

        def before(slot, m):
            return (slot - 1) % RING, m - 1 if slot == 0 else m

        def after(slot, m):
            return (slot + 1) % RING, m + 1 if slot == RING - 1 else m

        def first(t):
            return isinstance(t, int) and t == 0

        def last(t, n):
            return isinstance(t, int) and t == n - 1

        def spread(ap, n):
            return ap.unsqueeze(2).to_broadcast([ap.shape[0], ap.shape[1], n])

        places, at = {}, 6656
        for name, n in (("lg", T * NR), ("ge", T * EG), ("ee", T * EG), ("gm", T), ("gs", T), ("pt", T),
                        ("is1", T * 4), ("sm", T), ("goh", T * EG), ("es", T * EPG), ("m1", T), ("oh1", T * 4),
                        ("es2", T * EPG), ("m2", T), ("oh2", T * 4), ("dm", T), ("e2", T), ("rd", T),
                        ("te", NE), ("start", NE), ("cnt", NE), ("posf", 2 * T), ("bef", 32), ("M", T * NE)):
            places[name] = A[:, at:at + n]
            at += n
        assert at <= 8192
        at = 0
        for name, n in (("tmp", 512), ("tmp2", 512), ("OH1", T * NE), ("OH2", T * NE), ("off", T * NE),
                        ("tot", T * NE), ("base", T * NE)):
            places[name] = A[:, at:at + n]
            at += n
        assert at <= 2048

        def R(name, inner=None):
            return places[name].rearrange("p (a b) -> p a b", b=inner) if inner else places[name]

        block = ctx.enter_context(nc.Block())

        @block.sync
        def _(sp):
            sp.sem_inc(w_loaded, BIAS)
            sp.dma_start(xr[:, 0, :], x[0, 0:P, :]).then_inc(s_x[0], 16)
            sp.dma_start(cst[:, C_ID:C_ALL], consts[:, C_ID:C_ALL]).then_inc(s_cst, 16)
            with sp.Fori(0, DEPTH) as l:
                win = w_in[ds(l, 1), :, :].rearrange("a (k p) n -> p (a k) n", p=P)
                wout = w_out[ds(l, 1), :, :].rearrange("a (k p) n -> p (a k) n", p=P)
                for c in range(4):
                    if c == 0:
                        sp.wait_ge(op_done, upto(l, T, 0))
                    if c == 1:
                        sp.wait_ge(s_rows, DEPTH * 3 * 16)
                        sp.wait_ge(s_par, DEPTH * 4 * 16)
                    if c == 2:
                        sp.wait_ge(dn_done, upto(l, BLOCKS, 0))
                    sp.dma_start(W[:, c, :, :], win[:, :, c * 512:(c + 1) * 512]).then_inc(s_win[c], 16)
                sp.wait_ge(pm_done, upto(l, 2 * NG, 0))
                sp.dma_start(wpool[:, :, :], w_pool[ds(l, 1), :, :, :].rearrange("a g c e -> c (a g) e"))\
                    .then_inc(s_wpool, 16)
                for h in range(2):
                    sp.wait_ge(z_done, upto(l, 4 * T, 4 * T - 3 + h))
                    sp.dma_start(w_o[h], wout[:, :, h * 512:(h + 1) * 512]).then_inc(s_wout[h], 16)
                def load_expert(e, slot):
                    at = e + l * NE
                    for w, c in ((w_gate, 0), (w_up, FE)):
                        sp.dma_start(w_gu[slot][:, :, c:c + FE],
                                     w.rearrange("l e (k p) f -> p (l e) k f", p=P)[:, ds(at, 1), :, :]
                                     .rearrange("p a k f -> p (a k) f")).then_inc(s_w[slot], 16)
                    sp.dma_start(w_dn[slot],
                                 w_down.rearrange("l e (k p) f -> p (l e) k f", p=P)[:, ds(at, 1), :, :]
                                 .rearrange("p a k f -> p (a k) f")).then_inc(s_w[slot], 16)

                def report(slot, use):
                    sp.wait_ge(s_w[slot], l * (48 * (NE // SLOTS)) + 48 * (use + 1))
                    sp.sem_inc(w_loaded, 1)

                sp.wait_ge(z_done, upto(l, 4 * T, 4 * T))
                sp.wait_ge(pooled, upto(l, NG, NG))
                load_expert(0, 0)
                sp.wait_ge(pv_done, upto(l, 16 * PAIRS, 16 * PAIRS))
                load_expert(1, 1)
                report(0, 0)
                sp.wait_ge(pm_done, upto(l, 2 * NG, 2 * NG))
                sp.wait_ge(cat_ready, upto(l, T, T))
                load_expert(2, 2)
                report(1, 0)
                load_expert(3, 3)
                report(2, 0)
                sp.wait_ge(routed, upto(l, 1, 1))
                sp.sem_inc(s_passed, 1)
                with sp.Fori(1, NE // SLOTS) as g:
                    for slot in range(SLOTS):
                        e = g * SLOTS + slot
                        ended = sp.value_load(start_i[0:1, ds(e - SLOTS + 1, 1)], min_val=0, max_val=BLOCKS)
                        sp.wait_ge(dn_done, upto(l, BLOCKS, ended))
                        load_expert(e, slot)
                        report((slot - 1) % SLOTS, g if slot else g - 1)
                report(SLOTS - 1, NE // SLOTS - 1)

        @block.gpsimd
        def _(pool):
            ch = Chain(pool, s_pool)
            nc.gpsimd.memset(zero[:, :], 0.0).then_inc(s_ms, 1)
            nc.gpsimd.memset(st[:, 159:160], EPS).then_inc(s_ms, 1)
            pool.wait_ge(s_ms, 2)
            for s in (x_ready, pooled, staged, cat_ready):
                pool.sem_inc(s, BIAS)
            pool.wait_ge(s_x[0], 16)
            pool.sem_inc(x_ready, 1)
            pool.dma_start(xr[:, 1, :], x[0, P:2 * P, :]).then_inc(s_x[1], 16)
            pool.wait_ge(s_win[0], 16)
            for t in range(2, T):
                pool.dma_start(xr[:, t, :], x[0, t * P:(t + 1) * P, :]).then_inc(s_x[t], 16)
            for t in range(1, T):
                pool.wait_ge(s_x[t], 16)
                pool.sem_inc(x_ready, 1)
            pool.dma_start(cst[:, C_MASK:C_ID], consts[:, C_MASK:C_ID]).then_inc(s_mask, 16)
            pool.wait_ge(z_done, upto(0, 4 * T, 5))
            wr = wr_all[:, 0:DEPTH * K * NR].rearrange("p (l k n) -> p l k n", l=DEPTH, k=K)
            for l in range(DEPTH):
                for src, at, n in ((w_group, 0, EG), (w_router, EG, NE)):
                    pool.dma_start(wr[:, l, :, at:at + n], src[l, :, :].rearrange("(k p) n -> p k n", p=P))\
                        .then_inc(s_wr, 16)
            rt = row_table.rearrange("(p r) (b c) -> p (r b) c", p=P, c=256)
            per = BLOCKS
            for i in range(4):
                pool.dma_start(rt[:, i * per:(i + 1) * per, :],
                               zero[:, :].unsqueeze(1).to_broadcast([P, per, 256])).then_inc(s_zero, 16)
            with pool.Fori(0, DEPTH) as l:
                ch.restart()
                pool.wait_ge(t_evac, upto(l, 3 * T, 3 * T))
                sA = W[:, 2, :, :].rearrange("p k n -> p (k n)")[:, 0:PAD + SEQ]
                sB = W[:, 2, :, :].rearrange("p k n -> p (k n)")[:, 1280:1280 + PAD + SEQ]
                pool.wait_ge(z_done, upto(l, 4 * T, 4 * T))
                pool.sem_inc(s_passed, 1)
                nc.gpsimd.memset(sA[:, 0:PAD], 0.0)
                nc.gpsimd.memset(uT[:, :, 0:PAD], 0.0)
                ch.link(nc.gpsimd.memset(sB[:, 0:PAD], 0.0))

                def stage(p, a):
                    r = slice(HD * a, HD * (a + 1))
                    ch.link(nc.gpsimd.tensor_copy(qst[r, :], qT[r, p, :]))
                    nc.gpsimd.tensor_copy(kst[r, :], kT[r, p, :]).then_inc(staged, 1)
                    pool.wait_ge(staged, upto(l, 2 * PAIRS, 2 * p + a + 1))
                    pool.sem_inc(s_passed, 1)

                for a in range(2):
                    stage(0, a)

                def pool_group(g):
                    win = POOL_WINDOWS[g]
                    u = uT[:, g, :]
                    src, step, bufs = u, 1, [sA, sB]
                    while step < win:
                        dst = bufs[0]
                        bufs.reverse()
                        ch.link(nc.gpsimd.tensor_tensor(out=dst[:, PAD:], in0=src[:, PAD:],
                                                        in1=src[:, PAD - step:PAD + SEQ - step], op=ALU.add))
                        src, step = dst, 2 * step
                    other = bufs[0]
                    n = win - 1
                    ch.link(nc.gpsimd.tensor_tensor(out=src[:, PAD:PAD + n], in0=src[:, PAD:PAD + n],
                                                    in1=cst[:, C_INV:C_INV + n], op=ALU.mult))
                    ch.link(nc.gpsimd.tensor_scalar(src[:, PAD + n:], src[:, PAD + n:], 1.0 / win, None, ALU.mult))
                    ins = nc.gpsimd.tensor_tensor(out=u[:, PAD:], in0=src[:, PAD:], in1=u[:, PAD:],
                                                  op=ALU.subtract)
                    ins.then_inc(pooled, 1)
                    pool.wait_ge(pooled, upto(l, NG, g + 1))
                    pool.sem_inc(s_passed, 1)

                pool_group(0)
                for p in range(1, PAIRS):
                    for a in range(2):
                        pool.wait_ge(s_done, upto(l, 16 * PAIRS, 16 * (p - 1) + 8 * (a + 1)))
                        pool.sem_inc(s_passed, 1)
                        stage(p, a)
                    pool_group(p)

                pool.wait_ge(at_ev, upto(l, 2 * PAIRS, 2 * PAIRS))
                pool.wait_ge(poolT_ready, upto(l, 2 * NG, 2 * NG))
                pool.sem_inc(s_passed, 1)

                def cat_tile(t, par, m):
                    if not first(t):
                        pool.wait_ge(op_done, upto(l, T, t - 1))
                        pool.sem_inc(s_passed, 1)
                    nc.gpsimd.tensor_copy(cat[par][:, 0:4, :], attT[:, :, ds(t * P, P)])
                    nc.gpsimd.tensor_copy(cat[par][:, 4:8, :], poolT[:, :, ds(t * P, P)]).then_inc(cat_ready, 1)

                steps(pool, T, cat_tile)

                pool.wait_ge(s_zero, 16 * 4)
                pool.wait_ge(routed, upto(l, 1, 1))
                for t in range(T):
                    pool.wait_ge(xs2_saved, upto(l, T, t + 1))
                    pool.sem_inc(s_passed, 1)
                    for k in range(2):
                        pool.indirect_dma_start(
                            out=row_table, out_offset=bass.IndirectOffsetOnAxis(ap=pos_i[:, k, t:t + 1], axis=0),
                            in_=to_scat[t % 4], in_offset=None).then_inc(s_scat[t % 4], 16)

                for i in range(4):
                    pool.wait_ge(s_scat[i], (l + 1) * (16 * 2 * (T // 4)))
                    pool.sem_inc(s_passed, 1)

                def load_rows(j, slot, m):
                    if not first(j):
                        pool.wait_ge(xtm_done, upto(l, BLOCKS, j - RING + 1))
                        pool.sem_inc(s_passed, 1)
                    pool.dma_start(xg[slot], row_table[ds(j * P, P), :]).then_inc(s_xg[slot], 16)

                steps(pool, BLOCKS, load_rows, ring=RING)

                for i in range(RING):
                    pool.wait_ge(s_y[i], (l + 1) * (16 * USES[i]) + 1)
                    pool.sem_inc(s_passed, 1)
                for t in range(T):
                    if t >= 2:
                        pool.wait_ge(x_ready, upto(l + 1, T, t - 1))
                        pool.sem_inc(s_passed, 1)
                    for k in range(2):
                        pool.indirect_dma_start(
                            out=gath[t % 2][:, k, :], out_offset=None,
                            in_=y_table, in_offset=bass.IndirectOffsetOnAxis(ap=pos_i[:, k, t:t + 1], axis=0),
                        ).then_inc(s_gath[t % 2], 16)
                for t in range(T):
                    pool.wait_ge(x_ready, upto(l + 1, T, t + 1))
                    pool.sem_inc(s_passed, 1)
                    pool.dma_start(out[0, t * P:(t + 1) * P, :], xr[:, t, :]).then_inc(s_out, 16)
                pool.wait_ge(s_out, (l + 1) * (16 * T))

        @block.scalar
        def _(a_):
            sc = nc.scalar
            for s in (params, sd1, sqz_done, sdz, v_copied, u_copied, t_evac, p_ready, pt0_ev, at_ev, sd2,
                      xs2_saved, ge_exp, dm_exp, silu_done, aT_ready, y1_ready):
                a_.sem_inc(s, BIAS)
            for i in range(RING):
                a_.sem_inc(s_y[i], 1)
            for l in range(DEPTH):
                for src, at, n in ((norm1_gain, G1, K), (norm2_gain, G2, K), (pool_scale, PSC, NG)):
                    a_.dma_start(par_rows[l * GQK + at:l * GQK + at + n, :], src[l, :].rearrange("(k p) -> k p", p=P))\
                        .then_inc(s_rows, 16)
            for l in range(DEPTH):
                for src, at, n in ((q_norm_gain, GQK, HD), (k_norm_gain, GQK + HD, HD), (b_group, BIAS_R, EG),
                                   (b_router, BIAS_R + EG, NE)):
                    a_.dma_start(par_all[:, l, at:at + n], src[l, :].partition_broadcast(P)).then_inc(s_par, 16)
            a_.wait_ge(rows_t, 1)
            sc.activation(par_all[:, :, 0:GQK], ps[:, 7, 0:DEPTH * GQK].rearrange("p (l n) -> p l n", l=DEPTH),
                          ACT.Copy).then_inc(rows_in, 1)
            a_.wait_ge(rows_in, 1)
            a_.wait_ge(s_par, DEPTH * 4 * 16)
            ch = Chain(a_, s_act)
            eps = st[:, 159:160]
            with a_.Fori(0, DEPTH) as l:
                ch.restart()
                a_.wait_ge(x_ready, upto(l, T, 1))
                sc.activation(par[:, :], par_all[:, l, :], ACT.Copy).then_inc(params, 1)

                def square_x(t, par_):
                    a_.wait_ge(x_ready, upto(l, T, t + 1))
                    if not first(t):
                        a_.wait_ge(xs_ready, upto(l, T, t))
                        a_.wait_ge(xt_done, upto(l, T, t - 1))
                    ch.link(sc.activation(xs[par_], xr[:, t, :], ACT.Square, accum_out=st[:, par_:par_ + 1]))
                    sc.activation(st[:, 2 + par_:3 + par_], st[:, par_:par_ + 1], ACT.Sqrt,
                                      bias=eps, scale=1.0 / D).then_inc(sd1, 1)

                def evac_turned(t):
                    for n, (dst, bank) in enumerate(((qT[:, :, ds(t * P, P)], 6), (kT[:, :, ds(t * P, P)], 7),
                                                     (uT[:, :, ds(PAD + t * P, P)], 6))):
                        a_.wait_ge(tqk_done, upto(l, 3 * T, 3 * t + n + 1))
                        sc.activation(dst, ps[:, bank, :].rearrange("p (a c) -> p a c", c=P), ACT.Copy).then_inc(t_evac, 1)

                square_x(0, 0)

                def in_act(t, par_, m):
                    if not last(t, T):
                        square_x(t + 1, 1 - par_)
                    for n in range(2):
                        a_.wait_ge(z_done, upto(l, 4 * T, 4 * t + n + 1))
                        sc.activation(sqz[:, 8 * n:8 * n + 8, :],
                                          ps[:, 2 + n, :].rearrange("p (h c) -> p h c", c=HD), ACT.Square).then_inc(sqz_done, 1)
                    a_.wait_ge(var_ready, upto(l, T, t + 1))
                    sc.activation(st[:, 32:48], st[:, 16:32], ACT.Sqrt).then_inc(sdz, 1)
                    if not first(t):
                        evac_turned(t - 1)
                    else:
                        a_.wait_ge(x_ready, upto(l, T, T))
                    a_.wait_ge(z_done, upto(l, 4 * T, 4 * t + 3))
                    sc.activation(v[:, t, :], ps[:, 4, :], ACT.Copy).then_inc(v_copied, 1)
                    a_.wait_ge(z_done, upto(l, 4 * T, 4 * t + 4))
                    sc.activation(u_nat, ps[:, 5, :].rearrange("p (g c) -> p g c", g=NG), ACT.Copy).then_inc(u_copied, 1)

                steps(a_, T, in_act, ch)
                evac_turned(T - 1)

                with a_.Fori(0, PAIRS) as p:
                    def exp(n):
                        i, b = n % T, n % 2
                        nk = (i + 1) * P
                        a_.wait_ge(sm_ready, upto(l, 16 * PAIRS, p * 16 + n + 1))
                        sc.activation(pr[b][:, 0:nk], pr[b][:, 0:nk], ACT.Exp, scale=-1.0,
                                          bias=st[:, 64 + n:65 + n], accum_out=st[:, 80 + n:81 + n]).then_inc(p_ready, 1)

                    exp(0)
                    for n in range(16):
                        i, b = n % T, n % 2
                        if n + 1 < 16:
                            exp(n + 1)
                        nb = min(i + 1, 4)
                        a_.wait_ge(pt0_done, upto(l, 16 * PAIRS, p * 16 + n + 1))
                        if n >= 2:
                            a_.wait_ge(pv_done, upto(l, 16 * PAIRS, p * 16 + n - 1))
                        sc.activation(prT[b][:, 0:nb, :], ps[:, 4, 0:nb * P]
                                          .rearrange("p (a c) -> p a c", c=P), ACT.Copy).then_inc(pt0_ev, 1)
                    for h in range(2):
                        a_.wait_ge(at_done, upto(l, 2 * PAIRS, p * 2 + h + 1))
                        sc.activation(attT[:, p, h * 512:(h + 1) * 512], ps[:, 4 + h, :], ACT.Copy).then_inc(at_ev, 1)

                ch.restart()

                def out_act(t, par_, m):
                    a_.wait_ge(x_upd, upto(l, T, t + 1))
                    if not first(t):
                        a_.wait_ge(xs2_ready, upto(l, T, t))
                    ch.link(sc.activation(junk2, xr[:, t, :], ACT.Square, accum_out=st[:, par_:par_ + 1]))
                    sc.activation(st[:, 2 + par_:3 + par_], st[:, par_:par_ + 1], ACT.Sqrt,
                                      bias=eps, scale=1.0 / D).then_inc(sd2, 1)

                steps(a_, T, out_act, ch)

                a_.wait_ge(ge_ready, upto(l, 1, 1))
                sc.activation(R("ee"), R("ge"), ACT.Exp).then_inc(ge_exp, 1)
                a_.wait_ge(dm_ready, upto(l, 1, 1))
                sc.activation(R("e2"), R("dm"), ACT.Exp).then_inc(dm_exp, 1)

                a_.wait_ge(rt_done, upto(l, T, T))
                a_.wait_ge(xs2_ready, upto(l, T, T))
                for t in range(T):
                    if t >= 4:
                        a_.wait_ge(s_scat[t % 4], l * (16 * 2 * (T // 4)) + 32)
                    sc.activation(to_scat[t % 4], xr[:, t, :], ACT.Copy,
                                  scale=st[:, 128 + t:129 + t]).then_inc(xs2_saved, 1)

                def moe_down(t, slot, m):
                    a_.wait_ge(dn_done, upto(l, BLOCKS, t + 1))
                    a_.wait_ge(s_y[slot], l * (16 * USES[slot]) + 16 * m + 1)
                    sc.activation(y[slot][:, 512:1024], ps[:, 5, :], ACT.Copy).then_inc(y1_ready, 1)
                    a_.wait_ge(y0_ready, upto(l, BLOCKS, t + 1))
                    a_.wait_ge(y1_ready, upto(l, BLOCKS, t + 1))
                    a_.dma_start(y_table[ds(t * P, P), :], y[slot]).then_inc(s_y[slot], 16)

                def moe_act(t, slot, m):
                    a_.wait_ge(gu_done, upto(l, BLOCKS, t + 1))
                    sc.activation(sg, ps[:, 2, 0:FE], ACT.Silu).then_inc(silu_done, 1)
                    if not first(t):
                        moe_down(t - 1, *before(slot, m))
                    a_.wait_ge(a_t_done, upto(l, BLOCKS, t + 1))
                    sc.activation(aT, ps[:, 3, 0:FE].rearrange("p (k c) -> p k c", c=P), ACT.Copy).then_inc(aT_ready, 1)

                steps(a_, BLOCKS, moe_act, ring=RING)
                moe_down(BLOCKS - 1, (BLOCKS - 1) % RING, (BLOCKS - 1) // RING)

        @block.vector
        def _(dve):
            ve = nc.vector
            ch = Chain(dve, s_dve)
            for s in (xs_ready, hT_ready, var_ready, zqk_free, qk_ready, sm_ready, pt1_ev, o_ev,
                      poolT_ready, x_upd, xs2_ready, h2T_ready, logits, ge_ready, dm_ready, onehots, routed,
                      xgT_ready, a_ready, y0_ready):
                dve.sem_inc(s, BIAS)
            ch.link(ve.memset(wr_all[:, DEPTH * K * NR:], 0.0))
            dve.wait_ge(s_cst, 16)

            def rsqrt(ss, sd, r, tmp, scale, parts=((0, None, 1.0),)):
                ch.link(ve.tensor_scalar(tmp, ss, scale, EPS, ALU.mult, ALU.add))
                ch.link(ve.reciprocal(r, sd))
                ch.link(ve.tensor_tensor(out=tmp, in0=tmp, in1=r, op=ALU.mult))
                ch.link(ve.tensor_tensor(out=tmp, in0=tmp, in1=r, op=ALU.mult))
                for lo, hi, factor in parts:
                    ins = ve.tensor_scalar(tmp[:, lo:hi], tmp[:, lo:hi], -0.5 * factor, 1.5 * factor, ALU.mult, ALU.add)
                ch.link(ins)
                ch.link(ve.tensor_tensor(out=r, in0=tmp, in1=r, op=ALU.mult))

            def times_gain(dst, gain, banks, waited):
                for h in range(2):
                    ins = ve.tensor_tensor(out=dst[:, 4 * h:4 * h + 4, :],
                                           in0=ps[:, banks + h, :].rearrange("p (a c) -> p a c", c=P),
                                           in1=spread(par[:, gain + 4 * h:gain + 4 * h + 4], P), op=ALU.mult)
                ins.then_inc(waited, 1)

            with dve.Fori(0, DEPTH) as l:
                ch.restart()
                dve.wait_ge(params, upto(l, 1, 1))

                def norm_x(t, par_):
                    dve.wait_ge(sd1, upto(l, T, t + 1))
                    rsqrt(st[:, par_:par_ + 1], st[:, 2 + par_:3 + par_], st[:, 4 + par_:5 + par_],
                          st[:, 6:7], 1.0 / D)
                    ve.tensor_scalar(xs[par_], xr[:, t, :], st[:, 4 + par_:5 + par_], None, ALU.mult).then_inc(xs_ready, 1)

                norm_x(0, 0)

                def in_dve(t, par_, m):
                    dve.wait_ge(xt_done, upto(l, T, t + 1))
                    times_gain(hT[par_], G1, 0, hT_ready)
                    if not last(t, T):
                        norm_x(t + 1, 1 - par_)
                    dve.wait_ge(sqz_done, upto(l, 2 * T, 2 * t + 2))
                    ch.link(ve.tensor_reduce(st[:, 16:32], sqz, AX.X, ALU.add))
                    ch.link(ve.tensor_scalar(st[:, 16:32], st[:, 16:32], 1.0 / HD, EPS, ALU.mult, ALU.add))
                    dve.sem_inc(var_ready, 1)
                    dve.wait_ge(sdz, upto(l, T, t + 1))
                    r, tmp, var = st[:, 48:64], st[:, 96:112], st[:, 16:32]
                    ch.link(ve.reciprocal(r, st[:, 32:48]))
                    ch.link(ve.tensor_tensor(out=tmp, in0=var, in1=r, op=ALU.mult))
                    ch.link(ve.tensor_tensor(out=tmp, in0=tmp, in1=r, op=ALU.mult))
                    ve.tensor_scalar(tmp[:, 0:8], tmp[:, 0:8], -0.5 * HD ** -0.5, 1.5 * HD ** -0.5, ALU.mult, ALU.add)
                    ch.link(ve.tensor_scalar(tmp[:, 8:16], tmp[:, 8:16], -0.5, 1.5, ALU.mult, ALU.add))
                    ch.link(ve.tensor_tensor(out=r, in0=tmp, in1=r, op=ALU.mult))
                    z = zn[par_]
                    if not first(t):
                        dve.wait_ge(tqk_done, upto(l, 3 * T, 3 * t - 4))
                    for n in range(2):
                        ins = ve.tensor_tensor(out=z[:, 8 * n:8 * n + 8, :],
                                               in0=ps[:, 2 + n, :].rearrange("p (h c) -> p h c", c=HD),
                                               in1=spread(r[:, 8 * n:8 * n + 8], HD), op=ALU.mult)
                        ins.then_inc(zqk_free, 1)
                    dve.wait_ge(zqk_free, upto(l, 2 * T, 2 * t + 2))
                    for n in range(2):
                        g = par[:, GQK + HD * n:GQK + HD * (n + 1)].unsqueeze(1).to_broadcast([P, 8, HD])
                        ins = ve.tensor_tensor(out=z[:, 8 * n:8 * n + 8, :], in0=z[:, 8 * n:8 * n + 8, :], in1=g, op=ALU.mult)
                    ch.link(ins)
                    half = ROT // 2

                    def table(at, lo, n):
                        return cst[:, ds(at + lo + t * ROT, n)].unsqueeze(1).to_broadcast([P, 16, n])

                    ve.tensor_tensor(out=rope[:, 0, :, :], in0=z[:, :, 0:ROT], in1=table(C_COS, 0, ROT), op=ALU.mult)
                    ve.tensor_tensor(out=rope[:, 1, :, 0:half], in0=z[:, :, half:ROT], in1=table(C_SIN, 0, half), op=ALU.mult)
                    ch.link(ve.tensor_tensor(out=rope[:, 1, :, half:ROT], in0=z[:, :, 0:half],
                                             in1=table(C_SIN, half, half), op=ALU.mult))
                    ve.tensor_tensor(out=z[:, :, 0:ROT], in0=rope[:, 0, :, :], in1=rope[:, 1, :, :], op=ALU.add).then_inc(qk_ready, 1)

                steps(dve, T, in_dve, ch)

                dve.wait_ge(s_mask, 16)
                with dve.Fori(0, PAIRS) as p:
                    ch.restart()

                    def mask(n):
                        i, b = n % T, n % 2
                        nk = (i + 1) * P
                        if n >= 2:
                            j = n - 2
                            if j % T >= 4:
                                dve.wait_ge(pt1_done, upto(l, 8 * PAIRS, p * 8 + 4 * (j // T) + j % T - 3))
                            else:
                                dve.wait_ge(pt0_done, upto(l, 16 * PAIRS, p * 16 + j + 1))
                        dve.wait_ge(s_done, upto(l, 16 * PAIRS, p * 16 + n + 1))
                        dve.sem_inc(s_passed, 1)
                        ve.tensor_tensor_reduce(
                            out=pr[b][:, 0:nk], in0=ps[:, 2 * b:2 * b + 2, :].rearrange("p a c -> p (a c)")[:, 0:nk],
                            in1=cst[:, C_MASK + SEQ - nk:C_MASK + SEQ], scale=-1.0, scalar=3.0e38, op0=ALU.add,
                            op1=ALU.min, accum_out=st[:, 64 + n:65 + n]).then_inc(sm_ready, 1)

                    def half_evac(n):
                        a, i, b = n // T, n % T, n % 2
                        dve.wait_ge(pt1_done, upto(l, 8 * PAIRS, p * 8 + 4 * a + i - 3))
                        if n >= 2:
                            dve.wait_ge(pv_done, upto(l, 16 * PAIRS, p * 16 + n - 1))
                        ve.tensor_copy(prT[b][:, 4:i + 1, :], ps[:, 5, 0:(i - 3) * P]
                                       .rearrange("p (a c) -> p a c", c=P)).then_inc(pt1_ev, 1)

                    def over_sum(n):
                        a, i, b = n // T, n % T, n % 2
                        dve.wait_ge(p_ready, upto(l, 16 * PAIRS, p * 16 + n + 1))
                        ch.link(ve.reciprocal(st[:, 112 + n:113 + n], st[:, 80 + n:81 + n]))
                        dve.wait_ge(pv_done, upto(l, 16 * PAIRS, p * 16 + n + 1))
                        dve.wait_ge(at_done, upto(l, 2 * PAIRS, p * 2))
                        ve.tensor_scalar(att[:, i, HD * a:HD * (a + 1)], ps[:, 6 + b, HD * a:HD * (a + 1)],
                                         st[:, 112 + n:113 + n], None, ALU.mult).then_inc(o_ev, 1)

                    mask(0)
                    mask(1)
                    for n in range(16):
                        if n % T >= 4:
                            half_evac(n)
                        if n + 2 < 16:
                            mask(n + 2)
                        if n >= 1:
                            over_sum(n - 1)
                    over_sum(15)

                for n in range(2 * NG):
                    g, h = n // 2, n % 2
                    dve.wait_ge(pm_done, upto(l, 2 * NG, n + 1))
                    ve.tensor_scalar(poolT[:, g, 512 * h:512 * h + 512], ps[:, n % 4, :],
                                         par[:, PSC + g:PSC + g + 1], None, ALU.mult).then_inc(poolT_ready, 1)

                ch.restart()

                def add_bias(t, par_):
                    dve.wait_ge(rt_done, upto(l, T, t + 1))
                    ve.tensor_tensor(out=R("lg", NR)[:, ds(t, 1), :],
                                         in0=ps[:, 6 + par_, 0:NR].unsqueeze(1),
                                         in1=par[:, BIAS_R:BIAS_R + NR].unsqueeze(1), op=ALU.add).then_inc(logits, 1)

                def gain2(t, par_):
                    dve.wait_ge(xt2_done, upto(l, T, t + 1))
                    times_gain(h2T[par_], G2, 4, h2T_ready)

                def out_dve(t, par_, m):
                    if not first(t):
                        gain2(t - 1, 1 - par_)
                    dve.wait_ge(op_done, upto(l, T, t + 1))
                    ve.tensor_tensor(out=xr[:, t, :], in0=ps[:, 2 * par_:2 * par_ + 2, :].rearrange("p a c -> p (a c)"),
                                         in1=xr[:, t, :], op=ALU.add).then_inc(x_upd, 1)
                    dve.wait_ge(sd2, upto(l, T, t + 1))
                    r = st[:, 8 + par_:9 + par_]
                    rsqrt(st[:, par_:par_ + 1], st[:, 2 + par_:3 + par_], r, st[:, 6:7], 1.0 / D)
                    ve.tensor_copy(st[:, ds(128 + t, 1)], r)
                    ve.tensor_scalar(xs2[par_], xr[:, t, :], r, None, ALU.mult).then_inc(xs2_ready, 1)
                    if not first(t):
                        add_bias(t - 1, 1 - par_)

                steps(dve, T, out_dve, ch)
                gain2(T - 1, (T - 1) % 2)
                add_bias(T - 1, (T - 1) % 2)
                dve.wait_ge(logits, upto(l, T, T))

                lg = R("lg", NR)
                gl, el = lg[:, :, 0:EG], lg[:, :, EG:NR]
                dsc = desc.unsqueeze(1).to_broadcast([P, T, 4])

                def tt(out_, a, b, op):
                    ch.link(ve.tensor_tensor(out=out_, in0=a, in1=b, op=op))

                def first_of_max(vals, m, onehot):
                    tt(R("is1", 4), vals, spread(m, 4), ALU.is_equal)
                    tt(R("is1", 4), R("is1", 4), dsc, ALU.mult)
                    ch.link(ve.tensor_reduce(R("sm"), R("is1", 4), AX.X, ALU.max))
                    tt(onehot, dsc, spread(R("sm"), 4), ALU.is_equal)

                ch.link(ve.tensor_reduce(R("gm"), gl, AX.X, ALU.max))
                ch.link(ve.tensor_tensor(out=R("ge", EG), in0=gl, in1=spread(R("gm"), EG), op=ALU.subtract))
                dve.sem_inc(ge_ready, 1)
                first_of_max(gl, R("gm"), R("goh", EG))
                tmp4 = R("tmp")[:, 0:T * 16].rearrange("p (t e g) -> p t e g", e=EPG, g=EG)
                tt(tmp4, el.rearrange("p t (g e) -> p t e g", g=EG),
                   R("goh", EG).unsqueeze(2).to_broadcast([P, T, EPG, EG]), ALU.mult)
                ch.link(ve.tensor_reduce(R("es", EPG), tmp4, AX.X, ALU.add))
                ch.link(ve.tensor_reduce(R("m1"), R("es", EPG), AX.X, ALU.max))
                first_of_max(R("es", EPG), R("m1"), R("oh1", 4))
                ch.link(ve.scalar_tensor_tensor(out=R("es2"), in0=R("oh1"), scalar=NEG, in1=R("es"),
                                                op0=ALU.mult, op1=ALU.add))
                ch.link(ve.tensor_reduce(R("m2"), R("es2", EPG), AX.X, ALU.max))
                tt(R("dm"), R("m2"), R("m1"), ALU.subtract)
                dve.sem_inc(dm_ready, 1)
                first_of_max(R("es2", EPG), R("m2"), R("oh2", 4))
                for OH, oh in (("OH1", "oh1"), ("OH2", "oh2")):
                    tt(R(OH).rearrange("p (t g e) -> p t g e", g=EG, e=EPG),
                       R("goh", EG).unsqueeze(3).to_broadcast([P, T, EG, EPG]),
                       R(oh, 4).unsqueeze(2).to_broadcast([P, T, EG, EPG]), ALU.mult)
                ve.tensor_tensor(out=R("M"), in0=R("OH1"), in1=R("OH2"), op=ALU.add).then_inc(onehots, 1)
                dve.wait_ge(ge_exp, upto(l, 1, 1))
                ch.link(ve.tensor_reduce(R("gs"), R("ee", EG), AX.X, ALU.add))
                ch.link(ve.reciprocal(R("pt"), R("gs")))
                dve.wait_ge(dm_exp, upto(l, 1, 1))
                ch.link(ve.tensor_scalar(R("rd"), R("e2"), 1.0, None, ALU.add))
                ch.link(ve.reciprocal(R("rd"), R("rd")))
                tt(gate_w[:, 0, :], R("rd"), R("pt"), ALU.mult)
                tt(gate_w[:, 1, :], gate_w[:, 0, :], R("e2"), ALU.mult)
                dve.wait_ge(ranks, upto(l, 1, 1))
                ch.link(ve.tensor_copy(R("tot"), ps[:, 1, 0:T * NE]))
                tot, off = R("tot", NE), R("off", NE)
                ch.link(ve.memset(off[:, 0, :], 0.0))
                for t in range(1, T):
                    tt(off[:, t, :], off[:, t - 1, :], tot[:, t - 1, :], ALU.add)
                tt(R("cnt"), off[:, T - 1, :], tot[:, T - 1, :], ALU.add)
                big = R("tmp")[:, 0:NE * T].rearrange("p (e t) -> p e t", t=T)
                tt(big, spread(R("cnt"), T), cst[:, C_THR:C_THR + T].unsqueeze(1).to_broadcast([P, NE, T]), ALU.is_gt)
                ch.link(ve.tensor_reduce(R("te"), big, AX.X, ALU.add))
                big = R("tmp")[:, 0:NE * NE].rearrange("p (e f) -> p e f", f=NE)
                tt(big, R("te").unsqueeze(1).to_broadcast([P, NE, NE]),
                   cst[:, C_LT:C_LT + NE * NE].rearrange("p (e f) -> p e f", f=NE), ALU.mult)
                ch.link(ve.tensor_reduce(R("start"), big, AX.X, ALU.add))
                ch.link(ve.tensor_copy(start_i[:, 0:NE], R("start")))
                ch.link(ve.tensor_tensor(out=start_i[:, NE:NE + 1], in0=R("start")[:, NE - 1:NE],
                                         in1=R("te")[:, NE - 1:NE], op=ALU.add))
                big = R("tmp").rearrange("p (j e) -> p j e", e=NE)
                tt(big, cst[:, C_JJ:C_JJ + 32].unsqueeze(2).to_broadcast([P, 32, NE]),
                   R("start").unsqueeze(1).to_broadcast([P, 32, NE]), ALU.is_ge)
                ch.link(ve.tensor_reduce(R("bef"), big, AX.X, ALU.add))
                ch.link(ve.tensor_scalar(block_e[:, :], R("bef"), -1.0, None, ALU.add))
                base = R("base", NE)
                ch.link(ve.scalar_tensor_tensor(out=base, in0=R("start").unsqueeze(1).to_broadcast([P, T, NE]),
                                                scalar=float(P), in1=off, op0=ALU.mult, op1=ALU.add))
                ch.link(ve.tensor_tensor(out=R("base"), in0=ps[:, 0, 0:T * NE], in1=R("base"), op=ALU.add))
                for k, OH in enumerate(("OH1", "OH2")):
                    tt(R("tmp")[:, 0:T * NE], R(OH), R("base"), ALU.mult)
                    ch.link(ve.tensor_reduce(R("posf")[:, k * T:(k + 1) * T],
                                             R("tmp")[:, 0:T * NE].rearrange("p (t e) -> p t e", e=NE), AX.X, ALU.add))
                ve.tensor_copy(pos_i[:, :, :].rearrange("p k t -> p (k t)"), R("posf")).then_inc(routed, 1)

                def rows_evac(t):
                    dve.wait_ge(xtm_done, upto(l, BLOCKS, t + 1))
                    times_gain(xgT, G2, 0, xgT_ready)

                def y_evac(t, slot, m):
                    dve.wait_ge(dn_done, upto(l, BLOCKS, t + 1))
                    dve.wait_ge(s_y[slot], l * (16 * USES[slot]) + 16 * m + 1)
                    ve.tensor_copy(y[slot][:, 0:512], ps[:, 4, :]).then_inc(y0_ready, 1)

                rows_evac(0)

                def moe_dve(t, slot, m):
                    if not last(t, BLOCKS):
                        rows_evac(t + 1)
                    dve.wait_ge(silu_done, upto(l, BLOCKS, t + 1))
                    ve.tensor_tensor(out=act, in0=ps[:, 2, FE:2 * FE], in1=sg, op=ALU.mult).then_inc(a_ready, 1)
                    if not first(t):
                        y_evac(t - 1, *before(slot, m))

                steps(dve, BLOCKS, moe_dve, ring=RING)
                y_evac(BLOCKS - 1, (BLOCKS - 1) % RING, (BLOCKS - 1) // RING)

                ch.restart()
                for t in range(T):
                    b = t % 2
                    dve.wait_ge(s_gath[b], l * (16 * 2 * (T // 2)) + 32 * (t // 2 + 1))
                    ch.link(ve.scalar_tensor_tensor(out=xr[:, t, :], in0=gath[b][:, 0, :], scalar=gate_w[:, 0, t:t + 1],
                                                    in1=xr[:, t, :], op0=ALU.mult, op1=ALU.add))
                    ve.scalar_tensor_tensor(out=xr[:, t, :], in0=gath[b][:, 1, :], scalar=gate_w[:, 1, t:t + 1],
                                                in1=xr[:, t, :], op0=ALU.mult, op1=ALU.add).then_inc(x_ready, 1)

        @block.tensor
        def _(pe):
            te = nc.tensor
            for s in (xt_done, z_done, tqk_done, s_done, pt0_done, pt1_done, pv_done, at_done, pm_done,
                      op_done, xt2_done, rt_done, ranks, xtm_done, gu_done, a_t_done, dn_done):
                pe.sem_inc(s, BIAS)
            pe.wait_ge(s_cst, 16)
            pe.wait_ge(s_rows, DEPTH * 3 * 16)
            te.transpose(ps[:, 7, 0:DEPTH * GQK], par_rows, ident[0:DEPTH * GQK, 0:DEPTH * GQK]).then_inc(rows_t, 1)

            def transposes(bank, srcs):
                for i, src in enumerate(srcs):
                    ins = te.transpose(ps[:, bank + i // 4, (i % 4) * P:(i % 4 + 1) * P], src, ident)
                return ins

            def cols(ap, n):
                return [ap[:, i * P:(i + 1) * P] for i in range(n)]

            with pe.Fori(0, DEPTH) as l:
                def xt(t, par_):
                    pe.wait_ge(xs_ready, upto(l, T, t + 1))
                    transposes(0, cols(xs[par_], K)).then_inc(xt_done, 1)

                def z(t, par_, c):
                    for k in range(K):
                        ins = te.matmul(ps[:, 2 + c, :], hT[par_][:, k, :], W[:, c, k, :], start=k == 0, stop=k == K - 1)
                    ins.then_inc(z_done, 1)

                def turn(t, par_):
                    zr = zn[par_].rearrange("p h c -> p (h c)")
                    pe.wait_ge(qk_ready, upto(l, T, t + 1))
                    pe.wait_ge(t_evac, upto(l, 3 * T, 3 * t))
                    transposes(6, cols(zr[:, 0:ATT], 4)).then_inc(tqk_done, 1)
                    transposes(7, cols(zr[:, ATT:2 * ATT], 4)).then_inc(tqk_done, 1)
                    pe.wait_ge(u_copied, upto(l, T, t + 1))
                    pe.wait_ge(t_evac, upto(l, 3 * T, 3 * t + 1))
                    transposes(6, [u_nat[:, g, :] for g in range(NG)]).then_inc(tqk_done, 1)

                xt(0, 0)

                def in_pe(t, par_, m):
                    pe.wait_ge(hT_ready, upto(l, T, t + 1))
                    for c in range(4):
                        if first(t):
                            pe.wait_ge(s_win[c], (l + 1) * 16)
                        elif c < 2:
                            pe.wait_ge(zqk_free, upto(l, 2 * T, 2 * t - 1 + c))
                        elif c == 2:
                            pe.wait_ge(v_copied, upto(l, T, t))
                        else:
                            pe.wait_ge(u_copied, upto(l, T, t))
                        z(t, par_, c)
                        if c == 0 and not last(t, T):
                            xt(t + 1, 1 - par_)
                        if c == 1 and not first(t):
                            turn(t - 1, 1 - par_)

                steps(pe, T, in_pe)
                turn(T - 1, (T - 1) % 2)

                pe.wait_ge(t_evac, upto(l, 3 * T, 3 * T))
                pe.wait_ge(v_copied, upto(l, T, T))
                pe.wait_ge(zqk_free, upto(l, 2 * T, 2 * T))
                pe.sem_inc(s_passed, 1)
                with pe.Fori(0, PAIRS) as p:
                    def scores(n):
                        a, i, b = n // T, n % T, n % 2
                        r = slice(HD * a, HD * (a + 1))
                        if i == 0:
                            pe.wait_ge(staged, upto(l, 2 * PAIRS, p * 2 + a + 1))
                        if n >= 2:
                            pe.wait_ge(sm_ready, upto(l, 16 * PAIRS, p * 16 + n - 1))
                        nk = (i + 1) * P
                        for c in range(0, nk, 512):
                            w = min(512, nk - c)
                            ins = te.matmul(ps[:, 2 * b + c // 512, 0:w], qst[r, i * P:(i + 1) * P], kst[r, c:c + w],
                                            start=True, stop=True)
                        ins.then_inc(s_done, 1)

                    pe.wait_ge(sm_ready, upto(l, 16 * PAIRS, p * 16))
                    scores(0)
                    scores(1)
                    pe.wait_ge(at_ev, upto(l, 2 * PAIRS, p * 2))
                    pe.wait_ge(o_ev, upto(l, 16 * PAIRS, p * 16))

                    def probs_t(n):
                        a, i, b = n // T, n % T, n % 2
                        pe.wait_ge(p_ready, upto(l, 16 * PAIRS, p * 16 + n + 1))
                        pe.wait_ge(pt0_ev, upto(l, 16 * PAIRS, p * 16 + n))
                        blocks = cols(pr[b], i + 1)
                        transposes(4, blocks[0:4]).then_inc(pt0_done, 1)
                        if i >= 4:
                            pe.wait_ge(pt1_ev, upto(l, 8 * PAIRS, p * 8 + 4 * a + i - 4))
                            transposes(5, blocks[4:]).then_inc(pt1_done, 1)

                    def probs_v(n):
                        a, i, b = n // T, n % T, n % 2
                        pe.wait_ge(pt0_ev, upto(l, 16 * PAIRS, p * 16 + n + 1))
                        if i >= 4:
                            pe.wait_ge(pt1_ev, upto(l, 8 * PAIRS, p * 8 + 4 * a + i - 3))
                        if n >= 2:
                            pe.wait_ge(o_ev, upto(l, 16 * PAIRS, p * 16 + n - 1))
                        for j in range(i + 1):
                            ins = te.matmul(ps[:, 6 + b, 0:P], prT[b][:, j, :], v[:, j, ds(p * P, P)],
                                            start=j == 0, stop=j == i)
                        ins.then_inc(pv_done, 1)

                    for n in range(16):
                        probs_t(n)
                        if n + 2 < 16:
                            scores(n + 2)
                        if n >= 1:
                            probs_v(n - 1)
                    probs_v(15)
                    pe.wait_ge(o_ev, upto(l, 16 * PAIRS, p * 16 + 16))
                    for h in range(2):
                        transposes(4 + h, [att[:, 4 * h + i, :] for i in range(4)]).then_inc(at_done, 1)

                pe.wait_ge(s_wpool, (l + 1) * 16)
                pe.wait_ge(pooled, upto(l, NG, NG))
                for n in range(2 * NG):
                    g, h = n // 2, n % 2
                    if n >= 4:
                        pe.wait_ge(poolT_ready, upto(l, 2 * NG, n - 3))
                    te.matmul(ps[:, n % 4, :], wpool[:, g, :], uT[:, g, PAD + 512 * h:PAD + 512 * h + 512],
                                  start=True, stop=True).then_inc(pm_done, 1)

                pe.wait_ge(poolT_ready, upto(l, 2 * NG, 2 * NG))
                pe.wait_ge(at_ev, upto(l, 2 * PAIRS, 2 * PAIRS))

                def project(par_, h):
                    for k in range(K):
                        ins = te.matmul(ps[:, 2 * par_ + h, :], cat[par_][:, k, :], w_o[h][:, k, :],
                                        start=k == 0, stop=k == K - 1)
                    return ins

                def xt2(t, par_):
                    pe.wait_ge(xs2_ready, upto(l, T, t + 1))
                    if not first(t):
                        pe.wait_ge(h2T_ready, upto(l, T, t))
                    transposes(4, cols(xs2[par_], K)).then_inc(xt2_done, 1)

                def router(t, par_):
                    pe.wait_ge(h2T_ready, upto(l, T, t + 1))
                    for k in range(K):
                        ins = te.matmul(ps[:, 6 + par_, 0:P], h2T[par_][:, k, :],
                                        wr_all[:, ds(l * (K * NR) + k * NR, P)],
                                        start=k == 0, stop=k == K - 1)
                    ins.then_inc(rt_done, 1)

                def out_pe(t, par_, m):
                    if first(t):
                        pe.wait_ge(s_wr, DEPTH * 2 * 16)
                        for h in range(2):
                            pe.wait_ge(s_wout[h], (l + 1) * 16)
                    else:
                        pe.wait_ge(x_upd, upto(l, T, t - 1))
                    pe.wait_ge(cat_ready, upto(l, T, t + 1))
                    project(par_, 0)
                    if not first(t):
                        xt2(t - 1, 1 - par_)
                    project(par_, 1).then_inc(op_done, 1)
                    if not first(t):
                        pe.wait_ge(logits, upto(l, T, t - 1))
                        router(t - 1, 1 - par_)

                steps(pe, T, out_pe)
                xt2(T - 1, (T - 1) % 2)
                router(T - 1, (T - 1) % 2)

                pe.wait_ge(onehots, upto(l, 1, 1))
                te.matmul(ps[:, 0, 0:T * NE], low, R("M"), start=True, stop=True)
                te.matmul(ps[:, 1, 0:T * NE], ones, R("M"), start=True, stop=True).then_inc(ranks, 1)

                def xtm(t, slot, m):
                    pe.wait_ge(s_xg[slot], l * (16 * USES[slot]) + 16 * (m + 1))
                    if first(t):
                        pe.wait_ge(routed, upto(l, 1, 1))
                    else:
                        pe.wait_ge(xgT_ready, upto(l, BLOCKS, t))
                    transposes(0, cols(xg[slot], K)).then_inc(xtm_done, 1)

                def if_used(t, sure, product):
                    if sure:
                        product(t)
                    else:
                        with pe.If(used > t):
                            product(t)
                        with pe.Else():
                            pe.sem_inc(gu_done if product is gate_up else dn_done, 1)

                def weights(t):
                    e = pe.value_load(block_e[0:1, ds(t, 1)], min_val=0, max_val=NE - 1)
                    pe.wait_ge(w_loaded, upto(l, NE, e + 1))
                    return (e % SLOTS) * E_ALL + AT_E

                def gate_up(t):
                    at = weights(t)
                    for k in range(K):
                        ins = te.matmul(ps[:, 2, :], xgT[:, k, :], big[:, ds(at + k * 2 * FE, 2 * FE)],
                                        start=k == 0, stop=k == K - 1)
                    ins.then_inc(gu_done, 1)

                def down(t):
                    at = weights(t)
                    for h in range(2):
                        for k in range(2):
                            ins = te.matmul(ps[:, 4 + h, :], aT[:, k, :], big[:, ds(at + (E_GU + k * D + 512 * h), 512)],
                                            start=k == 0, stop=k == 1)
                    ins.then_inc(dn_done, 1)

                def ready_down(t):
                    pe.wait_ge(aT_ready, upto(l, BLOCKS, t + 1))
                    if not first(t):
                        pe.wait_ge(y0_ready, upto(l, BLOCKS, t))
                        pe.wait_ge(y1_ready, upto(l, BLOCKS, t))
                    pe.sem_inc(s_passed, 1)

                xtm(0, 0, 0)
                used = pe.value_load(start_i[0:1, NE:NE + 1], min_val=2 * SEQ // P, max_val=BLOCKS)

                def moe_pe(t, slot, m, sure=True):
                    pe.wait_ge(xgT_ready, upto(l, BLOCKS, t + 1))
                    if not first(t):
                        pe.wait_ge(a_ready, upto(l, BLOCKS, t))
                    pe.sem_inc(s_passed, 1)
                    if_used(t, sure, gate_up)
                    if not last(t, BLOCKS):
                        xtm(t + 1, *after(slot, m))
                    if not first(t):
                        ready_down(t - 1)
                        if_used(t - 1, sure, down)
                    pe.wait_ge(a_ready, upto(l, BLOCKS, t + 1))
                    transposes(3, cols(act, 2)).then_inc(a_t_done, 1)

                def maybe_pe(t, slot, m):
                    moe_pe(t, slot, m, sure=False)

                steps(pe, BLOCKS, moe_pe, ring=RING, sure=(2 * SEQ // P - 1) // RING, maybe=maybe_pe)
                ready_down(BLOCKS - 1)
                if_used(BLOCKS - 1, False, down)


_INS = ["x", "norm1_gain", "w_in", "q_norm_gain", "k_norm_gain", "w_pool", "pool_scale", "w_out", "norm2_gain",
        "w_group", "b_group", "w_router", "b_router", "w_gate", "w_up", "w_down"]


def kernel(**inputs):
    import concourse.bacc as bacc
    from concourse.bass_utils import run_bass_kernel_spmd

    nc = bacc.Bacc("TRN2", target_bir_lowering=False, num_devices=1)
    arrays = {n: np.ascontiguousarray(inputs[n]) for n in _INS}
    arrays["consts"] = shape_constants()
    args = [nc.dram_tensor(f"in_{n}", a.shape, mybir.dt.from_np(a.dtype), kind="ExternalInput").ap()
            for n, a in arrays.items()]
    args.append(nc.dram_tensor("out_x", (1, SEQ, D), mybir.dt.float32, kind="ExternalOutput").ap())
    trunk(nc, *args)
    r = run_bass_kernel_spmd(nc, [{f"in_{n}": a for n, a in arrays.items()}], core_ids=[0])
    return r.results[0]["out_x"]
```

```python
import math
from contextlib import ExitStack

import numpy as np

import concourse.bass as bass
from concourse import mybir

P = 128
DEPTH, SEQ, D = 2, 1024, 1024
HEADS, HD = 8, 64
ATT = HEADS * HD
NG, GD = 4, 128
POOL_WINDOWS = (2, 4, 8, 16)
BRANCHES = ((128, 1), (512, 4), (2048, 16))
ROT, THETA = HD // 4, 500000.0
EG, EPG = 4, 4
NE, FE = EG * EPG, 256
EPS = 1e-6
NEG = -1e30

T = SEQ // P
K = D // P
PAIRS = HEADS // 2
BLOCKS = (2 * SEQ - NE) // P + NE
ROWS = BLOCKS * P
NR = EG + NE

C_MASK, C_ID, C_LOW, C_ONE = 0, SEQ, SEQ + P, SEQ + 2 * P
C_COS = C_ONE + P
C_SIN = C_COS + T * ROT
C_JJ = C_SIN + T * ROT
C_TOK = C_JJ + P
C_DESC = C_TOK + 2 * T
C_THR = C_DESC + 4
C_LT = C_THR + T
C_INV = C_LT + NE * NE
C_ALL = C_INV + 16

G1, G2, PSC = 0, K, 2 * K
GQK = 2 * K + NG
BIAS_R = GQK + 2 * HD
NPAR = BIAS_R + NR

RING = 3
GATHS = 4
SLOTS = 4
BIAS = BLOCKS


def shape_constants():
    c = np.zeros((P, C_ALL), np.float32)
    row = np.arange(P)[:, None]
    dist = (T - 1) * P + row - np.arange(SEQ)[None, :]
    count = np.zeros(dist.shape, np.int64)
    for window, dilation in BRANCHES:
        count += (dist >= 0) & (dist <= window) & (dist % dilation == 0)
    c[:, C_MASK:C_MASK + SEQ] = np.where(count > 0, np.log(np.maximum(count, 1)), NEG)
    c[:, C_ID:C_ID + P] = np.eye(P)
    c[:, C_LOW:C_LOW + P] = row < np.arange(P)[None, :]
    c[:, C_ONE:C_ONE + P] = 1.0
    inv_freq = np.float32(THETA) ** (-np.arange(0, ROT, 2, dtype=np.float32) / np.float32(ROT))
    ang = np.arange(SEQ, dtype=np.float32)[:, None] * inv_freq.astype(np.float32)[None, :]
    cos, sin = np.cos(ang).astype(np.float32), np.sin(ang).astype(np.float32)
    both = np.concatenate([cos, cos], 1), np.concatenate([-sin, sin], 1)
    for at, table in zip((C_COS, C_SIN), both):
        c[:, at:at + T * ROT] = table.reshape(T, P, ROT).transpose(1, 0, 2).reshape(P, T * ROT)
    c[:, C_JJ:C_JJ + P] = np.arange(P)
    c[:, C_TOK:C_TOK + 2 * T] = np.tile(P * np.arange(T), 2)[None, :] + row
    c[:, C_DESC:C_DESC + 4] = 4 - np.arange(4)
    c[:, C_THR:C_THR + T] = np.where(np.arange(T) > 0, P * np.arange(T), -1)
    e = np.arange(NE)
    c[:, C_LT:C_LT + NE * NE] = (e[None, :] < e[:, None]).reshape(-1)
    c[:, C_INV:C_INV + 16] = 1.0 / (1.0 + np.arange(16))
    return c


def trunk(nc, x, norm1_gain, w_in, q_norm_gain, k_norm_gain, w_pool, pool_scale, w_out,
          norm2_gain, w_group, b_group, w_router, b_router, w_gate, w_up, w_down, consts, out):
    f16 = mybir.dt.float16
    f32, i32, bf16, f32r = mybir.dt.float32, mybir.dt.int32, mybir.dt.bfloat16, mybir.dt.float32r
    ALU, ACT, AX = mybir.AluOpType, mybir.ActivationFunctionType, mybir.AxisListType
    ds = bass.ds

    ctx = ExitStack()
    with ctx:
        def sb(name, shape, dt=f32):
            return ctx.enter_context(nc.sbuf_tensor(name, shape, dt))

        def sem(name):
            return ctx.enter_context(nc.semaphore(name))

        ctx.enter_context(nc.allow_non_contiguous_dma(reason="small parameters, once"))
        token_rows = nc.dram_tensor("token_rows", (SEQ, D), f32, kind="Internal").ap()
        y_table = nc.dram_tensor("y_table", (ROWS, D), f32, kind="Internal").ap()

        xr = sb("x_res", [P, T, D])
        PAD = 16
        AT_V = 4 * K * 512
        AT_U = AT_V + T * ATT
        AT_K = AT_U + NG * (PAD + SEQ)
        AT_Q = AT_K + 4 * SEQ
        big_start = -(-nc.sbuf_base // 32) * 32
        big = sb("big", [P, AT_Q + 4 * SEQ])

        def part(name, at, size):
            return nc.alloc_sbuf_tensor_at(name, [P, size], f32r, offset=big_start + 4 * at)[:, :]

        W = big[:, 0:AT_V].rearrange("p (c k n) -> p c k n", c=4, k=K)
        v_r = big[:, AT_V:AT_U]
        uT = big[:, AT_U:AT_K].rearrange("p (g s) -> p g s", g=NG)
        kT_r = big[:, AT_K:AT_Q]
        qT_r = big[:, AT_Q:AT_Q + 4 * SEQ]
        arena_start = -(-nc.sbuf_base // 32) * 32
        AT_A = (arena_start - big_start) // 4
        A = sb("arena", [P, 8192])
        cst = sb("cst", [P, C_ALL])
        par_flat = sb("par_flat", [P, DEPTH * NPAR + K])
        par_all = par_flat[:, 0:DEPTH * NPAR].rearrange("p (l n) -> p l n", l=DEPTH)
        par = sb("par", [P, NPAR])
        wr_all = sb("wr_all", [P, DEPTH * K * NR + P])
        wpool = sb("wpool", [P, NG, GD])
        st = sb("st", [P, 160])
        gate_w = sb("gate_w", [P, 2, T])
        pos_i = sb("pos_i", [P, 2, T], i32)
        row_tok = sb("row_tok", [P, 32], i32)
        next_tok = sb("next_tok", [P, RING], i32)
        block_e = sb("block_e", [P, 32], i32)
        start_i = sb("start_i", [P, NE + 1], i32)
        ps = ctx.enter_context(nc.psum_tensor("ps", [P, 8, 512], f32))

        qT = qT_r[:, :].rearrange("p (a s) -> p a s", a=PAIRS)
        kT = kT_r[:, :].rearrange("p (a s) -> p a s", a=PAIRS)
        attT, poolT = qT, kT
        v = v_r[:, :].rearrange("p (t c) -> p t c", t=T)
        u_flat = big[:, AT_U:AT_U + K * 512]
        raw_in = [W[:, 1, :, :], W[:, 3, :, :], kT_r.rearrange("p (k n) -> p k n", k=K),
                  u_flat.rearrange("p (k n) -> p k n", k=K)]
        w_in_hi = [part(f"w_in_hi{i}", 2 * i * K * 512, K * 512) for i in range(2)]
        w_in_lo = [part(f"w_in_lo{i}", (2 * i + 1) * K * 512, K * 512) for i in range(2)]
        HALF_IN = K * 512 // 2
        w_o = [W[:, h, :, :] for h in range(2)]
        w_o_lo = [part(f"w_o_lo{h}", h * K * 512, K * 512) for h in range(2)]
        w_o_hi = [part(f"w_o_hi{h}", (2 + h) * K * 512, K * 512) for h in range(2)]
        cat_hi = [part(f"cat_hi{i}", AT_V + i * D, D).rearrange("p (k n) -> p k n", n=P) for i in range(2)]
        cat_lo = [part(f"cat_lo{i}", AT_V + (2 + i) * D, D).rearrange("p (k n) -> p k n", n=P) for i in range(2)]
        par_rows = kT_r[0:DEPTH * GQK, 0:P]
        AT_E, E_GU, E_ALL = AT_V // 2, K * 2 * FE, K * 2 * FE + 2 * D
        assert AT_E + SLOTS * E_ALL <= AT_Q + 4 * SEQ
        w_gu = [big[:, AT_E + i * E_ALL:AT_E + i * E_ALL + E_GU].rearrange("p (k n) -> p k n", k=K)
                for i in range(SLOTS)]
        w_dn = [big[:, AT_E + i * E_ALL + E_GU:AT_E + (i + 1) * E_ALL].rearrange("p (k n) -> p k n", k=2)
                for i in range(SLOTS)]
        gath = [big[:, AT_K + 2 * D * i:AT_K + 2 * D * (i + 1)].rearrange("p (k n) -> p k n", k=2) for i in range(GATHS)]

        def ring(at, size, n=2, inner=None):
            r = [A[:, at + size * i:at + size * (i + 1)] for i in range(n)]
            return [a.rearrange("p (k n) -> p k n", n=inner) for a in r] if inner else r

        xs = A[:, 0:D]
        sqz = A[:, 1024:1536].rearrange("p (h c) -> p h c", c=HD)
        rope = A[:, 1536:1792].rearrange("p (a h c) -> p a h c", a=2, h=HEADS)
        hT_hi = [part(f"hT_hi{i}", AT_A + 2048 + 2 * i * D, D).rearrange("p (k n) -> p k n", n=P) for i in range(2)]
        hT_lo = [part(f"hT_lo{i}", AT_A + 3072 + 2 * i * D, D).rearrange("p (k n) -> p k n", n=P) for i in range(2)]
        zn = ring(6144, ATT, inner=HD)
        u_nat = A[:, 7168:7680].rearrange("p (g c) -> p g c", g=NG)
        AT_H1 = 4 * K * 512 - 2 * SEQ
        q_parts = [part("q_parts0", AT_A, SEQ), part("q_parts1", AT_H1, SEQ)]
        k_high = [part("k_high0", AT_A + SEQ, SEQ), part("k_high1", AT_H1 + SEQ, SEQ)]
        k_low = part("k_low", AT_A + 7168, SEQ)
        att = A[:, 2048:3072].rearrange("p (t c) -> p t c", c=P)
        prT = ring(3072, SEQ, inner=P)
        pr = ring(5120, SEQ)
        xs2 = ring(2048, D)
        h2T = ring(4096, D, inner=P)
        in_row = A[:, 4096:5120].bitcast(f16).rearrange("p (c r) -> p c r", r=P)
        in_block = A[:, 5120:5376].bitcast(f16).rearrange("p (c b) -> p c b", b=32)
        junk2 = A[:, 6144:6656].bitcast(bf16)
        xg = ring(0, D, RING)
        xgT = A[:, 3072:4096].rearrange("p (k n) -> p k n", n=P)
        sg, act = A[:, 4096:4352], A[:, 4352:4608]
        aT = A[:, 4608:4864].rearrange("p (k n) -> p k n", n=P)
        y = ring(4864, D, RING)

        ident = cst[:, C_ID:C_ID + P]
        low = cst[:, C_LOW:C_LOW + P]
        ones = cst[:, C_ONE:C_ONE + P]
        desc = cst[:, C_DESC:C_DESC + 4]

        x_ready = sem("x_ready")
        params = sem("params")
        sd1 = sem("sd1")
        xs_ready = sem("xs_ready")
        xt_done = sem("xt_done")
        hT_ready = sem("hT_ready")
        win_top = sem("win_top")
        win_split = sem("win_split")
        gain_in = sem("gain_in")
        z_done = sem("z_done")
        sqz_done = sem("sqz_done")
        var_ready = sem("var_ready")
        sdz = sem("sdz")
        zqk_free = sem("zqk_free")
        v_copied = sem("v_copied")
        u_copied = sem("u_copied")
        qk_ready = sem("qk_ready")
        tqk_done = sem("tqk_done")
        t_evac = sem("t_evac")
        pooled = sem("pooled")
        q_high_in = sem("q_high_in")
        k_high_in = sem("k_high_in")
        staged = sem("staged")
        s_done = sem("s_done")
        sm_ready = sem("sm_ready")
        p_ready = sem("p_ready")
        pt0_done = sem("pt0_done")
        pt1_done = sem("pt1_done")
        pt0_ev = sem("pt0_ev")
        pt1_ev = sem("pt1_ev")
        pv_done = sem("pv_done")
        o_ev = sem("o_ev")
        at_done = sem("at_done")
        at_ev = sem("at_ev")
        pm_done = sem("pm_done")
        poolT_ready = sem("poolT_ready")
        wo_split = sem("wo_split")
        cat_top = sem("cat_top")
        cat_ready = sem("cat_ready")
        op_done = sem("op_done")
        x_upd = sem("x_upd")
        sd2 = sem("sd2")
        xs2_ready = sem("xs2_ready")
        xt2_done = sem("xt2_done")
        h2T_ready = sem("h2T_ready")
        rt_done = sem("rt_done")
        logits = sem("logits")
        ge_ready = sem("ge_ready")
        ge_exp = sem("ge_exp")
        dm_ready = sem("dm_ready")
        dm_exp = sem("dm_exp")
        onehots = sem("onehots")
        ranks = sem("ranks")
        located = sem("located")
        listed = sem("listed")
        rows_known = sem("rows_known")
        routed = sem("routed")
        w_loaded = sem("w_loaded")
        xtm_done = sem("xtm_done")
        xgT_ready = sem("xgT_ready")
        gu_done = sem("gu_done")
        silu_done = sem("silu_done")
        a_ready = sem("a_ready")
        a_t_done = sem("a_t_done")
        aT_ready = sem("aT_ready")
        dn_done = sem("dn_done")
        y0_ready = sem("y0_ready")
        y1_ready = sem("y1_ready")
        rows_t = sem("rows_t")
        rows_in = sem("rows_in")
        s_passed = sem("s_passed")

        def upto(l, per_layer, n):
            return l * per_layer + n + BIAS

        s_cst, s_x, s_par = sem("s_cst"), [sem(f"s_x{t}") for t in range(T)], sem("s_par")
        s_rows, s_wr = sem("s_rows"), sem("s_wr")
        s_mask = sem("s_mask")
        s_win = [[sem(f"s_win{c}{g}") for g in range(2)] for c in range(4)]
        s_wout = [sem(f"s_wout{c}") for c in range(2)]
        s_wpool, s_fill = sem("s_wpool"), sem("s_fill")
        s_tok = [sem(f"s_tok{i}") for i in range(2)]
        s_w = [sem(f"s_w{i}") for i in range(SLOTS)]
        s_xg = [sem(f"s_xg{i}") for i in range(RING)]
        s_y = [sem(f"s_y{i}") for i in range(RING)]
        s_gath = [sem(f"s_gath{i}") for i in range(GATHS)]
        s_out = sem("s_out")
        s_ms = sem("s_ms")
        s_dve, s_act, s_pool = sem("s_dve"), sem("s_act"), sem("s_pool")

        USES = [(BLOCKS + RING - 1 - i) // RING for i in range(RING)]

        class Chain:

            def __init__(self, eng, s):
                self.eng, self.s, self.n = eng, s, 0

            def link(self, ins):
                ins.then_inc(self.s, 1)
                self.n += 1
                self.eng.wait_ge(self.s, self.n)

            def restart(self):
                self.eng.sem_clear(self.s)
                self.n = 0

        def steps(eng, n, body, chain=None, ring=2, sure=0, maybe=None, begun=False):
            if not begun:
                body(0, 0, 0)
            loops = (n - 2) // ring
            for lo, hi in ((0, sure), (sure, loops)):
                if lo == hi:
                    continue
                if maybe and lo == sure:
                    body = maybe
                with eng.Fori(lo, hi) as j:
                    if chain:
                        chain.restart()
                    for i in range(1, ring + 1):
                        body(ring * j + i, i % ring, j + i // ring)
            if chain:
                chain.restart()
            for t in range(1 + ring * loops, n):
                body(t, t % ring, t // ring)

        SURE = (2 * SEQ // P - 1) // RING

        def before(slot, m):
            return (slot - 1) % RING, m - 1 if slot == 0 else m

        def after(slot, m):
            return (slot + 1) % RING, m + 1 if slot == RING - 1 else m

        def first(t):
            return isinstance(t, int) and t == 0

        def last(t, n):
            return isinstance(t, int) and t == n - 1

        def spread(ap, n):
            return ap.unsqueeze(2).to_broadcast([ap.shape[0], ap.shape[1], n])

        places, at = {}, 6656
        for name, n in (("lg", T * NR), ("ge", T * EG), ("ee", T * EG), ("gm", T), ("gs", T), ("pt", T),
                        ("is1", T * 4), ("sm", T), ("goh", T * EG), ("es", T * EPG), ("m1", T), ("oh1", T * 4),
                        ("es2", T * EPG), ("m2", T), ("oh2", T * 4), ("dm", T), ("e2", T), ("rd", T),
                        ("te", NE), ("start", NE), ("cnt", NE), ("posf", 2 * T), ("blk", 2 * T), ("bef", 32), ("M", T * NE)):
            places[name] = A[:, at:at + n]
            at += n
        assert at <= 8192
        at = 0
        for name, n in (("tmp", 512), ("tmp2", 512), ("OH1", T * NE), ("OH2", T * NE), ("off", T * NE),
                        ("tot", T * NE), ("base", T * NE)):
            places[name] = A[:, at:at + n]
            at += n
        assert at <= 2048

        places["tmp3"] = A[:, 6144:6656]

        def R(name, inner=None):
            return places[name].rearrange("p (a b) -> p a b", b=inner) if inner else places[name]

        ROW_PARAMS = ((norm1_gain, G1, K), (norm2_gain, G2, K), (pool_scale, PSC, NG))

        block = ctx.enter_context(nc.Block())

        @block.sync
        def _(sp):
            sp.sem_inc(w_loaded, BIAS)
            sp.dma_start(xr[:, 0, :], x[0, 0:P, :]).then_inc(s_x[0], 16)
            for src, at, n in ROW_PARAMS:
                sp.dma_start(par_rows[DEPTH * at:DEPTH * (at + n), :], src.rearrange("l (k p) -> (l k) p", p=P))\
                    .then_inc(s_rows, 16)
            sp.dma_start(cst[:, C_ID:C_ALL], consts[:, C_ID:C_ALL]).then_inc(s_cst, 16)

            def load_in(l, i, c):
                win = w_in[ds(l, 1), :, :].rearrange("a (k p) n -> p (a k) n", p=P)
                for g in range(2):
                    k = slice(g * K // 2, (g + 1) * K // 2)
                    sp.dma_start(raw_in[i][:, k, :], win[:, k, c * 512:(c + 1) * 512]).then_inc(s_win[i][g], 16)

            load_in(0, 0, 0)
            sp.wait_ge(s_ms, 2)
            with sp.Fori(0, DEPTH) as l:
                wout = w_out[ds(l, 1), :, :].rearrange("a (k p) n -> p (a k) n", p=P)
                sp.wait_ge(s_par, DEPTH * 4 * 16)
                used = sp.value_load(start_i[0:1, NE:NE + 1], min_val=2 * SEQ // P, max_val=BLOCKS)
                sp.wait_ge(dn_done, upto(l, BLOCKS, used - BLOCKS))
                load_in(l, 1, 2)
                sp.wait_ge(pm_done, upto(l, 2 * NG, 0))
                sp.dma_start(wpool[:, :, :], w_pool[ds(l, 1), :, :, :].rearrange("a g c e -> c (a g) e"))\
                    .then_inc(s_wpool, 16)
                sp.wait_ge(rows_t, 1)
                sp.wait_ge(x_ready, upto(l, T, T))
                load_in(l, 2, 1)
                load_in(l, 3, 3)
                sp.wait_ge(z_done, upto(l, 4 * T, 4 * T - 1))
                for h in range(2):
                    sp.dma_start(w_o[h], wout[:, :, h * 512:(h + 1) * 512]).then_inc(s_wout[h], 16)
                def load_expert(e, slot):
                    at = e + l * NE
                    for w, c in ((w_gate, 0), (w_up, FE)):
                        sp.dma_start(w_gu[slot][:, :, c:c + FE],
                                     w.rearrange("l e (k p) f -> p (l e) k f", p=P)[:, ds(at, 1), :, :]
                                     .rearrange("p a k f -> p (a k) f")).then_inc(s_w[slot], 16)
                    sp.dma_start(w_dn[slot],
                                 w_down.rearrange("l e (k p) f -> p (l e) k f", p=P)[:, ds(at, 1), :, :]
                                 .rearrange("p a k f -> p (a k) f")).then_inc(s_w[slot], 16)

                def report(slot, use):
                    sp.wait_ge(s_w[slot], l * (48 * (NE // SLOTS)) + 48 * (use + 1))
                    sp.sem_inc(w_loaded, 1)

                sp.wait_ge(pm_done, upto(l, 2 * NG, 2 * NG))
                sp.wait_ge(cat_ready, upto(l, T, T))
                load_expert(0, 2)
                load_expert(1, 3)
                report(2, 0)
                sp.wait_ge(op_done, upto(l, T, T))
                load_in((l + 1) % DEPTH, 0, 0)
                load_expert(2, 0)
                report(3, 0)
                load_expert(3, 1)
                report(0, 0)
                sp.wait_ge(routed, upto(l, 1, 1))
                sp.sem_inc(s_passed, 1)
                with sp.Fori(1, NE // SLOTS) as g:
                    for i in range(SLOTS):
                        e, slot = g * SLOTS + i, (i + 2) % SLOTS
                        ended = sp.value_load(start_i[0:1, ds(e - SLOTS + 1, 1)], min_val=0, max_val=BLOCKS)
                        sp.wait_ge(dn_done, upto(l, BLOCKS, ended))
                        load_expert(e, slot)
                        report((slot - 1) % SLOTS, g if i else g - 1)
                report(1, NE // SLOTS - 1)

        @block.gpsimd
        def _(pool):
            ch = Chain(pool, s_pool)
            nc.gpsimd.memset(st[:, 159:160], EPS).then_inc(s_ms, 1)
            nc.gpsimd.memset(start_i[:, :], BLOCKS).then_inc(s_ms, 1)
            pool.wait_ge(s_ms, 2)
            for s in (x_ready, pooled, wo_split):
                pool.sem_inc(s, BIAS)
            pool.wait_ge(s_x[0], 16)
            pool.sem_inc(x_ready, 1)
            pool.dma_start(xr[:, 1, :], x[0, P:2 * P, :]).then_inc(s_x[1], 16)
            pool.wait_ge(s_win[0][1], 16)
            for t in range(2, T):
                pool.dma_start(xr[:, t, :], x[0, t * P:(t + 1) * P, :]).then_inc(s_x[t], 16)
            for t in range(1, T):
                pool.wait_ge(s_x[t], 16)
                pool.sem_inc(x_ready, 1)
            pool.dma_start(cst[:, C_MASK:C_ID], consts[:, C_MASK:C_ID]).then_inc(s_mask, 16)
            pool.wait_ge(z_done, upto(0, 4 * T, 5))
            wr = wr_all[:, 0:DEPTH * K * NR].rearrange("p (l k n) -> p l k n", l=DEPTH, k=K)
            for l in range(DEPTH):
                for src, at, n in ((w_group, 0, EG), (w_router, EG, NE)):
                    pool.dma_start(wr[:, l, :, at:at + n], src[l, :, :].rearrange("(k p) n -> p k n", p=P))\
                        .then_inc(s_wr, 16)
            for j in range(2 * SEQ // P, BLOCKS):
                pool.dma_start(y_table[j * P:(j + 1) * P, :], xr[:, 0, :]).then_inc(s_fill, 16)
            with pool.Fori(0, DEPTH) as l:
                ch.restart()
                pool.wait_ge(t_evac, upto(l, 3 * T, 3 * T))
                sA = W[:, 2, :, :].rearrange("p k n -> p (k n)")[:, 0:PAD + SEQ]
                sB = W[:, 2, :, :].rearrange("p k n -> p (k n)")[:, 1280:1280 + PAD + SEQ]
                pool.wait_ge(z_done, upto(l, 4 * T, 4 * T))
                pool.sem_inc(s_passed, 1)
                nc.gpsimd.memset(sA[:, 0:PAD], 0.0)
                nc.gpsimd.memset(uT[:, :, 0:PAD], 0.0)
                ch.link(nc.gpsimd.memset(sB[:, 0:PAD], 0.0))

                def pool_group(g):
                    win = POOL_WINDOWS[g]
                    u = uT[:, g, :]
                    src, step, bufs = u, 1, [sA, sB]
                    while step < win:
                        dst = bufs[0]
                        bufs.reverse()
                        ch.link(nc.gpsimd.tensor_tensor(out=dst[:, PAD:], in0=src[:, PAD:],
                                                        in1=src[:, PAD - step:PAD + SEQ - step], op=ALU.add))
                        src, step = dst, 2 * step
                    other = bufs[0]
                    n = win - 1
                    ch.link(nc.gpsimd.tensor_tensor(out=src[:, PAD:PAD + n], in0=src[:, PAD:PAD + n],
                                                    in1=cst[:, C_INV:C_INV + n], op=ALU.mult))
                    ch.link(nc.gpsimd.tensor_scalar(src[:, PAD + n:], src[:, PAD + n:], 1.0 / win, None, ALU.mult))
                    ins = nc.gpsimd.tensor_tensor(out=u[:, PAD:], in0=src[:, PAD:], in1=u[:, PAD:],
                                                  op=ALU.subtract)
                    ins.then_inc(pooled, 1)
                    pool.wait_ge(pooled, upto(l, NG, g + 1))
                    pool.sem_inc(s_passed, 1)

                for g in range(NG):
                    pool_group(g)

                def split_out(h, lo, hi):
                    raw = w_o[h].rearrange("p k n -> p (k n)")
                    ch.link(nc.gpsimd.tensor_copy(w_o_hi[h][:, lo:hi], raw[:, lo:hi]))
                    return nc.gpsimd.tensor_tensor(out=w_o_lo[h][:, lo:hi], in0=raw[:, lo:hi],
                                                   in1=w_o_hi[h][:, lo:hi].bitcast(f32), op=ALU.subtract)

                for h in range(2):
                    pool.wait_ge(s_wout[h], (l + 1) * 16)
                    pool.sem_inc(s_passed, 1)
                split_out(0, 0, K * 512).then_inc(wo_split, 1)
                split_out(1, 0, K * 512 - 2 * SEQ)
                pool.wait_ge(s_done, upto(l, 16 * PAIRS, 16 * PAIRS))
                pool.sem_inc(s_passed, 1)
                split_out(1, K * 512 - 2 * SEQ, K * 512).then_inc(wo_split, 1)

                pool.wait_ge(rows_known, upto(l, 1, 1))
                for i in range(2):
                    pool.wait_ge(s_tok[i], (l + 1) * (16 * (T // 2)) + 1)
                    pool.sem_inc(s_passed, 1)

                def load_rows(j, slot, m):
                    if not first(j):
                        pool.wait_ge(xtm_done, upto(l, BLOCKS, j - RING + 1))
                        pool.wait_ge(s_xg[slot], l * (16 * USES[slot]) + 16 * m)
                        pool.sem_inc(s_passed, 1)
                    ch.link(nc.gpsimd.tensor_copy(next_tok[:, slot:slot + 1], row_tok[:, ds(j, 1)]))
                    pool.indirect_dma_start(
                        out=xg[slot], out_offset=None, in_=token_rows,
                        in_offset=bass.IndirectOffsetOnAxis(ap=next_tok[:, slot:slot + 1], axis=0)).then_inc(s_xg[slot], 16)

                ch.restart()
                steps(pool, BLOCKS, load_rows, ch, ring=RING)

                for i in range(RING):
                    pool.wait_ge(s_y[i], (l + 1) * (16 * USES[i]) + 1)
                    pool.sem_inc(s_passed, 1)
                for t in range(T):
                    if t >= GATHS:
                        pool.wait_ge(x_ready, upto(l + 1, T, t - GATHS + 1))
                        pool.sem_inc(s_passed, 1)
                    for k in range(2):
                        pool.indirect_dma_start(
                            out=gath[t % GATHS][:, k, :], out_offset=None,
                            in_=y_table, in_offset=bass.IndirectOffsetOnAxis(ap=pos_i[:, k, t:t + 1], axis=0),
                        ).then_inc(s_gath[t % GATHS], 16)
            for t in range(T):
                pool.wait_ge(x_ready, upto(DEPTH, T, t + 1))
                pool.dma_start(out[0, t * P:(t + 1) * P, :], xr[:, t, :]).then_inc(s_out, 16)
            pool.wait_ge(s_out, 16 * T)

        @block.scalar
        def _(a_):
            sc = nc.scalar
            for s in (params, q_high_in, k_high_in, win_top, gain_in, sd1, sqz_done, sdz, cat_top, v_copied, u_copied, t_evac, p_ready, pt0_ev, at_ev, sd2,
                      ge_exp, dm_exp, silu_done, aT_ready, y1_ready):
                a_.sem_inc(s, BIAS)
            for s in s_y + s_tok:
                a_.sem_inc(s, 1)
            for l in range(DEPTH):
                for src, at, n in ((q_norm_gain, GQK, HD), (k_norm_gain, GQK + HD, HD), (b_group, BIAS_R, EG),
                                   (b_router, BIAS_R + EG, NE)):
                    a_.dma_start(par_all[:, l, at:at + n], src[l, :].partition_broadcast(P)).then_inc(s_par, 16)
            ch = Chain(a_, s_act)
            eps = st[:, 159:160]

            def square_x(l, t, par_):
                a_.wait_ge(x_ready, upto(l, T, t + 1))
                if not first(t):
                    a_.wait_ge(xs_ready, upto(l, 2 * T, t))
                    a_.wait_ge(xt_done, upto(l, 2 * T, t))
                ch.link(sc.activation(xs, xr[:, t, :], ACT.Square, accum_out=st[:, par_:par_ + 1]))
                sc.activation(st[:, 2 + par_:3 + par_], st[:, par_:par_ + 1], ACT.Sqrt,
                              bias=eps, scale=1.0 / D).then_inc(sd1, 1)

            def in_high(l, i):
                raw = raw_in[i].rearrange("p k n -> p (k n)")
                for g in range(2):
                    c = slice(g * HALF_IN, (g + 1) * HALF_IN)
                    a_.wait_ge(s_win[i][g], l * 16 + 16)
                    sc.activation(w_in_hi[i % 2][:, c], raw[:, c], ACT.Copy).then_inc(win_top, 1)

            def first_gain(l):
                sc.activation(par[:, G1:G1 + K], par_flat[:, ds(l * NPAR + G1, K)], ACT.Copy).then_inc(gain_in, 1)

            square_x(0, 0, 0)
            a_.wait_ge(rows_t, 1)
            for src, at, n in ROW_PARAMS:
                sc.activation(par_all[:, :, at:at + n], ps[:, 7, DEPTH * at:DEPTH * (at + n)]
                              .rearrange("p (l n) -> p l n", l=DEPTH), ACT.Copy).then_inc(rows_in, 1)
            a_.wait_ge(rows_in, 3)
            first_gain(0)
            in_high(0, 0)
            in_high(0, 1)
            a_.wait_ge(s_par, DEPTH * 4 * 16)
            with a_.Fori(0, DEPTH) as l:
                ch.restart()
                a_.wait_ge(x_ready, upto(l, T, 1))
                sc.activation(par[:, K:NPAR], par_flat[:, ds(l * NPAR + K, NPAR - K)], ACT.Copy).then_inc(params, 1)

                def evac_turned(h, t, n):
                    dst, bank = ((qT[:, :, ds(t * P, P)], 6), (kT[:, :, ds(t * P, P)], 6),
                                 (uT[:, :, ds(PAD + t * P, P)], 7))[n]
                    a_.wait_ge(tqk_done, upto(l, 3 * T, t + 1 if n == 0 else T + 2 * t + n))
                    sc.activation(dst, ps[:, bank, :].rearrange("p (a c) -> p a c", c=P), ACT.Copy).then_inc(t_evac, 1)

                def heads(a):
                    return slice(HD * a, HD * (a + 1)), slice(HD * (1 - a), HD * (2 - a))

                def q_top(p, a):
                    own, other = heads(a)
                    sc.activation(q_parts[a][own, :], qT[own, p, :], ACT.Copy).then_inc(q_high_in, 1)

                def k_top(p, a, c=slice(0, SEQ)):
                    own, other = heads(a)
                    sc.activation(k_high[a][own, c], kT[own, p, c], ACT.Copy)

                def k_top_again(p, a, c=slice(0, SEQ)):
                    own, other = heads(a)
                    sc.activation(k_high[a][other, c], kT[own, p, c], ACT.Copy).then_inc(k_high_in, 1)

                def in_act(t, par_, h):
                    n = h * T + t
                    if h == 0 and not last(t, T):
                        square_x(l, t + 1, 1 - par_)
                    a_.wait_ge(z_done, upto(l, 4 * T, 2 * n + 1))
                    sc.activation(sqz, ps[:, 2 + 2 * par_, :].rearrange("p (h c) -> p h c", c=HD), ACT.Square)\
                        .then_inc(sqz_done, 1)
                    if h == 0 and last(t, T):
                        in_high(l, 2)
                    a_.wait_ge(var_ready, upto(l, 2 * T, n + 1))
                    sc.activation(st[:, 32:40], st[:, 16:24], ACT.Sqrt).then_inc(sdz, 1)
                    if not first(t):
                        if h == 0:
                            a_.wait_ge(x_ready, upto(l, T, T))
                        evac_turned(h, t - 1, h)
                        if h:
                            evac_turned(h, t - 1, 2)
                    if h and last(t, T):
                        a_.wait_ge(xt_done, upto(l, 2 * T, 2 * T))
                        q_top(0, 0)
                        a_.wait_ge(qk_ready, upto(l, 2 * T, 2 * T))
                        a_.wait_ge(t_evac, upto(l, 3 * T, 3 * T - 2))
                        k_top(0, 0, slice(0, SEQ - P))
                        k_top_again(0, 0, slice(0, SEQ - P))
                    a_.wait_ge(z_done, upto(l, 4 * T, 2 * n + 2))
                    src = ps[:, 3 + 2 * par_, :]
                    if h == 0:
                        sc.activation(v[:, t, :], src, ACT.Copy).then_inc(v_copied, 1)
                    else:
                        sc.activation(u_nat, src.rearrange("p (g c) -> p g c", g=NG), ACT.Copy).then_inc(u_copied, 1)
                    if h == 0 and last(t, T):
                        in_high(l, 3)

                for h in range(2):
                    steps(a_, T, lambda t, par_, m: in_act(t, par_, h), ch)
                    if h == 0:
                        evac_turned(0, T - 1, 0)

                evac_turned(1, T - 1, 1)
                a_.wait_ge(t_evac, upto(l, 3 * T, 3 * T - 1))
                k_top(0, 0, slice(SEQ - P, SEQ))
                k_top_again(0, 0, slice(SEQ - P, SEQ))
                evac_turned(1, T - 1, 2)

                with a_.Fori(0, PAIRS) as p:
                    def exp(n):
                        i, b = n % T, n % 2
                        nk = (i + 1) * P
                        a_.wait_ge(sm_ready, upto(l, 16 * PAIRS, p * 16 + n + 1))
                        sc.activation(pr[b][:, 0:nk], pr[b][:, 0:nk], ACT.Exp, scale=-1.0,
                                          bias=st[:, 64 + n:65 + n], accum_out=st[:, 80 + n:81 + n]).then_inc(p_ready, 1)

                    exp(0)
                    for n in range(16):
                        i, b = n % T, n % 2
                        if n + 1 < 16:
                            exp(n + 1)
                        nb = min(i + 1, 4)
                        a_.wait_ge(pt0_done, upto(l, 16 * PAIRS, p * 16 + n + 1))
                        if n >= 2:
                            a_.wait_ge(pv_done, upto(l, 16 * PAIRS, p * 16 + n - 1))
                        sc.activation(prT[b][:, 0:nb, :], ps[:, 4, 0:nb * P]
                                          .rearrange("p (a c) -> p a c", c=P), ACT.Copy).then_inc(pt0_ev, 1)
                        if n == 0:
                            a_.wait_ge(s_done, upto(l, 16 * PAIRS, p * 16))
                            q_top(p, 1)
                        if n == 8:
                            a_.wait_ge(s_done, upto(l, 16 * PAIRS, p * 16 + 8))
                            q_top((p + 1) % PAIRS, 0)
                        if n == 1:
                            k_top(p, 1)
                        if n == 9:
                            k_top((p + 1) % PAIRS, 0)
                        if n == 2:
                            k_top_again(p, 1)
                        if n == 10:
                            k_top_again((p + 1) % PAIRS, 0)
                    for h in range(2):
                        a_.wait_ge(at_done, upto(l, 2 * PAIRS, p * 2 + h + 1))
                        sc.activation(attT[:, p, h * 512:(h + 1) * 512], ps[:, 4 + h, :], ACT.Copy).then_inc(at_ev, 1)

                ch.restart()

                def store_tokens(t, par_):
                    a_.wait_ge(xs2_ready, upto(l, T, t + 1))
                    a_.dma_start(token_rows[ds(t * P, P), :], xs2[par_]).then_inc(s_tok[par_], 16)

                def cat_high(t, par_):
                    if not first(t):
                        a_.wait_ge(op_done, upto(l, T, t - 1))
                    sc.activation(cat_hi[par_][:, 0:4, :], attT[:, :, ds(t * P, P)], ACT.Copy)
                    sc.activation(cat_hi[par_][:, 4:8, :], poolT[:, :, ds(t * P, P)], ACT.Copy).then_inc(cat_top, 1)

                a_.wait_ge(at_ev, upto(l, 2 * PAIRS, 2 * PAIRS))
                a_.wait_ge(pv_done, upto(l, 16 * PAIRS, 16 * PAIRS))
                a_.wait_ge(poolT_ready, upto(l, 2 * NG, 2 * NG))
                cat_high(0, 0)

                def out_act(t, par_, m):
                    if not last(t, T):
                        cat_high(t + 1, 1 - par_)
                    a_.wait_ge(x_upd, upto(l, T, t + 1))
                    if not first(t):
                        store_tokens(t - 1, 1 - par_)
                    ch.link(sc.activation(junk2, xr[:, t, :], ACT.Square, accum_out=st[:, par_:par_ + 1]))
                    sc.activation(st[:, 2 + par_:3 + par_], st[:, par_:par_ + 1], ACT.Sqrt,
                                      bias=eps, scale=1.0 / D).then_inc(sd2, 1)

                steps(a_, T, out_act, ch)
                store_tokens(T - 1, (T - 1) % 2)

                a_.wait_ge(ge_ready, upto(l, 1, 1))
                sc.activation(R("ee"), R("ge"), ACT.Exp).then_inc(ge_exp, 1)
                a_.wait_ge(dm_ready, upto(l, 1, 1))
                sc.activation(R("e2"), R("dm"), ACT.Exp).then_inc(dm_exp, 1)
                in_high(l + 1, 0)

                def moe_down(t, slot, m):
                    a_.wait_ge(dn_done, upto(l, BLOCKS, t + 1))
                    a_.wait_ge(s_y[slot], l * (16 * USES[slot]) + 16 * m + 1)
                    sc.activation(y[slot][:, 512:1024], ps[:, 5, :], ACT.Copy).then_inc(y1_ready, 1)
                    a_.wait_ge(y0_ready, upto(l, BLOCKS, t + 1))
                    a_.wait_ge(y1_ready, upto(l, BLOCKS, t + 1))
                    a_.dma_start(y_table[ds(t * P, P), :], y[slot]).then_inc(s_y[slot], 16)

                def moe_act(t, slot, m):
                    a_.wait_ge(gu_done, upto(l, BLOCKS, t + 1))
                    sc.activation(sg, ps[:, 2, 0:FE], ACT.Silu).then_inc(silu_done, 1)
                    if not first(t):
                        moe_down(t - 1, *before(slot, m))
                    a_.wait_ge(a_t_done, upto(l, BLOCKS, t + 1))
                    sc.activation(aT, ps[:, 3, 0:FE].rearrange("p (k c) -> p k c", c=P), ACT.Copy).then_inc(aT_ready, 1)

                def maybe_down(t, slot, m):
                    with a_.If(used > t):
                        a_.wait_ge(silu_done, upto(l, BLOCKS, t + 1))
                        a_.wait_ge(aT_ready, upto(l, BLOCKS, t + 1))
                        moe_down(t, slot, m)
                    with a_.Else():
                        a_.sem_inc(y1_ready, 1)
                        a_.sem_inc(s_y[slot], 16)

                def maybe_act(t, slot, m):
                    with a_.If(used > t):
                        moe_act(t, slot, m)
                    with a_.Else():
                        maybe_down(t - 1, *before(slot, m))
                        a_.sem_inc(silu_done, 1)
                        a_.sem_inc(aT_ready, 1)

                a_.wait_ge(routed, upto(l, 1, 1))
                a_.sem_inc(s_passed, 1)
                used = a_.value_load(start_i[0:1, NE:NE + 1], min_val=2 * SEQ // P, max_val=BLOCKS)
                steps(a_, BLOCKS, moe_act, ring=RING, sure=SURE, maybe=maybe_act)
                maybe_down(BLOCKS - 1, (BLOCKS - 1) % RING, (BLOCKS - 1) // RING)

                with a_.If(l < DEPTH - 1):
                    ch.restart()
                    sc.activation(st[:, 158:159], eps, ACT.Sqrt)
                    square_x(l + 1, 0, 0)
                    first_gain(l + 1)
                    in_high(l + 1, 1)

        @block.vector
        def _(dve):
            ve = nc.vector
            ch = Chain(dve, s_dve)
            for s in (staged, win_split, xs_ready, hT_ready, var_ready, zqk_free, qk_ready, sm_ready, pt1_ev, o_ev,
                      poolT_ready, cat_ready, x_upd, xs2_ready, h2T_ready, logits, ge_ready, dm_ready, onehots, located, rows_known, routed,
                      xgT_ready, a_ready, y0_ready):
                dve.sem_inc(s, BIAS)
            ch.link(ve.memset(wr_all[:, DEPTH * K * NR:], 0.0))
            dve.wait_ge(s_cst, 16)

            def rsqrt(ss, sd, r, tmp, scale):
                ch.link(ve.tensor_scalar(tmp, ss, scale, EPS, ALU.mult, ALU.add))
                ch.link(ve.reciprocal(r, sd))
                ch.link(ve.tensor_tensor(out=tmp, in0=tmp, in1=r, op=ALU.mult))
                ch.link(ve.tensor_tensor(out=tmp, in0=tmp, in1=r, op=ALU.mult))
                ch.link(ve.tensor_scalar(tmp, tmp, -0.5, 1.5, ALU.mult, ALU.add))
                ch.link(ve.tensor_tensor(out=r, in0=tmp, in1=r, op=ALU.mult))

            def times_gain(dst, gain, banks, waited):
                for h in range(2):
                    ins = ve.tensor_tensor(out=dst[:, 4 * h:4 * h + 4, :],
                                           in0=ps[:, banks + h, :].rearrange("p (a c) -> p a c", c=P),
                                           in1=spread(gain[:, 4 * h:4 * h + 4], P), op=ALU.mult)
                ins.then_inc(waited, 1)

            def norm_x(l, t, par_):
                dve.wait_ge(sd1, upto(l, T, t + 1))
                r = st[:, 4 + par_:5 + par_]
                rsqrt(st[:, par_:par_ + 1], st[:, 2 + par_:3 + par_], r, st[:, 6:7], 1.0 / D)
                ve.tensor_copy(st[:, ds(128 + t, 1)], r)
                ve.tensor_scalar(xs, xr[:, t, :], r, None, ALU.mult).then_inc(xs_ready, 1)

            def norm_x_again(l, t):
                dve.wait_ge(xt_done, upto(l, 2 * T, T + t))
                dve.sem_inc(s_passed, 1)
                ch.link(ve.tensor_copy(st[:, 7:8], st[:, ds(128 + t, 1)]))
                ve.tensor_scalar(xs, xr[:, t, :], st[:, 7:8], None, ALU.mult).then_inc(xs_ready, 1)

            def gain1(l, n, par_):
                dve.wait_ge(xt_done, upto(l, 2 * T, n + 1))
                hi, lo = hT_hi[par_], hT_lo[par_]
                for h in range(2):
                    ins = ve.tensor_tensor(out=hi[:, 4 * h:4 * h + 4, :],
                                           in0=ps[:, h, :].rearrange("p (a c) -> p a c", c=P),
                                           in1=spread(par[:, G1 + 4 * h:G1 + 4 * h + 4], P), op=ALU.mult)
                ch.link(ins)
                for k in range(K):
                    ins = ve.scalar_tensor_tensor(out=lo[:, k, :], in0=ps[:, k // 4, (k % 4) * P:(k % 4 + 1) * P],
                                                  scalar=par[:, G1 + k:G1 + k + 1], in1=hi[:, k, :].bitcast(f32),
                                                  op0=ALU.mult, op1=ALU.subtract)
                ins.then_inc(hT_ready, 1)

            def in_low(l, i):
                raw = raw_in[i].rearrange("p k n -> p (k n)")
                for g in range(2):
                    c = slice(g * HALF_IN, (g + 1) * HALF_IN)
                    dve.wait_ge(win_top, upto(l, 8, 2 * i + g + 1))
                    ve.tensor_tensor(out=w_in_lo[i % 2][:, c], in0=raw[:, c],
                                     in1=w_in_hi[i % 2][:, c].bitcast(f32), op=ALU.subtract).then_inc(win_split, 1)

            def in_dve(l, t, par_, h):
                n = h * T + t
                if h == 0:
                    if not last(t, T):
                        norm_x(l, t + 1, 1 - par_)
                    else:
                        norm_x_again(l, 0)
                elif not (first(t) or last(t, T)):
                    norm_x_again(l, t + 1)
                if h == 0 or not last(t, T):
                    gain1(l, n + 1, 1 - par_)
                if h == 0 and last(t, T):
                    in_low(l, 2)
                norm_qk(l, t, par_, h)
                if h == 0 and last(t, T):
                    norm_x_again(l, 1)
                    in_low(l, 3)

            def norm_qk(l, t, par_, h):
                n = h * T + t
                dve.wait_ge(sqz_done, upto(l, 2 * T, n + 1))
                ch.link(ve.tensor_reduce(st[:, 16:24], sqz, AX.X, ALU.add))
                ch.link(ve.tensor_scalar(st[:, 16:24], st[:, 16:24], 1.0 / HD, EPS, ALU.mult, ALU.add))
                dve.sem_inc(var_ready, 1)
                dve.wait_ge(sdz, upto(l, 2 * T, n + 1))
                r, tmp, var = st[:, 48:56], st[:, 96:104], st[:, 16:24]
                scale = HD ** -0.5 if h == 0 else 1.0
                ch.link(ve.reciprocal(r, st[:, 32:40]))
                ch.link(ve.tensor_tensor(out=tmp, in0=var, in1=r, op=ALU.mult))
                ch.link(ve.tensor_tensor(out=tmp, in0=tmp, in1=r, op=ALU.mult))
                ch.link(ve.tensor_scalar(tmp, tmp, -0.5 * scale, 1.5 * scale, ALU.mult, ALU.add))
                ch.link(ve.tensor_tensor(out=r, in0=tmp, in1=r, op=ALU.mult))
                z = zn[par_]
                if not first(t):
                    dve.wait_ge(tqk_done, upto(l, 3 * T, t - 1 if h == 0 else T + 2 * t - 3))
                elif h == 1:
                    dve.wait_ge(tqk_done, upto(l, 3 * T, T - 1))
                ve.tensor_tensor(out=z, in0=ps[:, 2 + 2 * par_, :].rearrange("p (h c) -> p h c", c=HD),
                                 in1=spread(r, HD), op=ALU.mult).then_inc(zqk_free, 1)
                dve.wait_ge(zqk_free, upto(l, 2 * T, n + 1))
                g = par[:, GQK + HD * h:GQK + HD * (h + 1)].unsqueeze(1).to_broadcast([P, HEADS, HD])
                ch.link(ve.tensor_tensor(out=z, in0=z, in1=g, op=ALU.mult))
                half = ROT // 2

                def table(at, lo, n):
                    return cst[:, ds(at + lo + t * ROT, n)].unsqueeze(1).to_broadcast([P, HEADS, n])

                ve.tensor_tensor(out=rope[:, 0, :, :], in0=z[:, :, 0:ROT], in1=table(C_COS, 0, ROT), op=ALU.mult)
                ve.tensor_tensor(out=rope[:, 1, :, 0:half], in0=z[:, :, half:ROT], in1=table(C_SIN, 0, half), op=ALU.mult)
                ch.link(ve.tensor_tensor(out=rope[:, 1, :, half:ROT], in0=z[:, :, 0:half],
                                         in1=table(C_SIN, half, half), op=ALU.mult))
                ve.tensor_tensor(out=z[:, :, 0:ROT], in0=rope[:, 0, :, :], in1=rope[:, 1, :, :], op=ALU.add).then_inc(qk_ready, 1)

            norm_x(0, 0, 0)
            dve.wait_ge(gain_in, upto(0, 1, 1))
            gain1(0, 0, 0)
            in_low(0, 0)
            in_low(0, 1)
            norm_x(0, 1, 1)
            gain1(0, 1, 1)
            dve.wait_ge(params, upto(0, 1, 1))
            norm_qk(0, 0, 0, 0)

            with dve.Fori(0, DEPTH) as l:
                ch.restart()
                steps(dve, T, lambda t, par_, m: in_dve(l, t, par_, 0), ch, begun=True)
                steps(dve, T, lambda t, par_, m: in_dve(l, t, par_, 1), ch)

                def q_and_k_low(p, a, n):
                    own, other = slice(HD * a, HD * (a + 1)), slice(HD * (1 - a), HD * (2 - a))
                    dve.wait_ge(q_high_in, upto(l, 2 * PAIRS + 1, n + 1))
                    ve.tensor_tensor(out=q_parts[a][other, :], in0=qT[own, p, :],
                                     in1=q_parts[a][own, :].bitcast(f32), op=ALU.subtract)
                    dve.wait_ge(k_high_in, upto(l, 2 * PAIRS + 2, n + 2))
                    ve.tensor_tensor(out=k_low[own, :], in0=kT[own, p, :],
                                     in1=k_high[a][own, :].bitcast(f32), op=ALU.subtract).then_inc(staged, 1)

                dve.wait_ge(tqk_done, upto(l, 3 * T, 3 * T))
                q_and_k_low(0, 0, 0)

                dve.wait_ge(s_mask, 16)
                with dve.Fori(0, PAIRS) as p:
                    ch.restart()

                    def mask(n):
                        i, b = n % T, n % 2
                        nk = (i + 1) * P
                        if n >= 2:
                            j = n - 2
                            if j % T >= 4:
                                dve.wait_ge(pt1_done, upto(l, 8 * PAIRS, p * 8 + 4 * (j // T) + j % T - 3))
                            else:
                                dve.wait_ge(pt0_done, upto(l, 16 * PAIRS, p * 16 + j + 1))
                        dve.wait_ge(s_done, upto(l, 16 * PAIRS, p * 16 + n + 1))
                        dve.sem_inc(s_passed, 1)
                        ve.tensor_tensor_reduce(
                            out=pr[b][:, 0:nk], in0=ps[:, 2 * b:2 * b + 2, :].rearrange("p a c -> p (a c)")[:, 0:nk],
                            in1=cst[:, C_MASK + SEQ - nk:C_MASK + SEQ], scale=-1.0, scalar=3.0e38, op0=ALU.add,
                            op1=ALU.min, accum_out=st[:, 64 + n:65 + n]).then_inc(sm_ready, 1)

                    def half_evac(n):
                        a, i, b = n // T, n % T, n % 2
                        dve.wait_ge(pt1_done, upto(l, 8 * PAIRS, p * 8 + 4 * a + i - 3))
                        if n >= 2:
                            dve.wait_ge(pv_done, upto(l, 16 * PAIRS, p * 16 + n - 1))
                        ve.tensor_copy(prT[b][:, 4:i + 1, :], ps[:, 5, 0:(i - 3) * P]
                                       .rearrange("p (a c) -> p a c", c=P)).then_inc(pt1_ev, 1)

                    def over_sum(n):
                        a, i, b = n // T, n % T, n % 2
                        dve.wait_ge(p_ready, upto(l, 16 * PAIRS, p * 16 + n + 1))
                        ch.link(ve.reciprocal(st[:, 112 + n:113 + n], st[:, 80 + n:81 + n]))
                        dve.wait_ge(pv_done, upto(l, 16 * PAIRS, p * 16 + n + 1))
                        dve.wait_ge(at_done, upto(l, 2 * PAIRS, p * 2))
                        ve.tensor_scalar(att[:, i, HD * a:HD * (a + 1)], ps[:, 6 + b, HD * a:HD * (a + 1)],
                                         st[:, 112 + n:113 + n], None, ALU.mult).then_inc(o_ev, 1)

                    mask(0)
                    mask(1)
                    for n in range(16):
                        if n % T >= 4:
                            half_evac(n)
                        if n + 2 < 16:
                            mask(n + 2)
                        if n >= 1:
                            over_sum(n - 1)
                        if n == 3:
                            q_and_k_low(p, 1, 2 * p + 1)
                        if n == 11:
                            q_and_k_low((p + 1) % PAIRS, 0, 2 * p + 2)
                    over_sum(15)

                for n in range(2 * NG):
                    g, h = n // 2, n % 2
                    dve.wait_ge(pm_done, upto(l, 2 * NG, n + 1))
                    ve.tensor_scalar(poolT[:, g, 512 * h:512 * h + 512], ps[:, n % 4, :],
                                         par[:, PSC + g:PSC + g + 1], None, ALU.mult).then_inc(poolT_ready, 1)

                ch.restart()

                def add_bias(t, par_):
                    dve.wait_ge(rt_done, upto(l, T, t + 1))
                    ve.tensor_tensor(out=R("lg", NR)[:, ds(t, 1), :],
                                         in0=ps[:, 6 + par_, 0:NR].unsqueeze(1),
                                         in1=par[:, BIAS_R:BIAS_R + NR].unsqueeze(1), op=ALU.add).then_inc(logits, 1)

                def gain2(t, par_):
                    dve.wait_ge(xt2_done, upto(l, T, t + 1))
                    times_gain(h2T[par_], par[:, G2:G2 + K], 4, h2T_ready)

                def cat_low(t, par_):
                    dve.wait_ge(cat_top, upto(l, T, t + 1))
                    for c, src in ((0, attT), (4, poolT)):
                        ins = ve.tensor_tensor(out=cat_lo[par_][:, c:c + 4, :], in0=src[:, :, ds(t * P, P)],
                                               in1=cat_hi[par_][:, c:c + 4, :].bitcast(f32), op=ALU.subtract)
                    ins.then_inc(cat_ready, 1)

                dve.wait_ge(s_fill, 16 * (BLOCKS - 2 * SEQ // P))
                cat_low(0, 0)

                def out_dve(t, par_, m):
                    if not last(t, T):
                        cat_low(t + 1, 1 - par_)
                    if not first(t):
                        gain2(t - 1, 1 - par_)
                    dve.wait_ge(op_done, upto(l, T, t + 1))
                    ve.tensor_tensor(out=xr[:, t, :], in0=ps[:, 2 * par_:2 * par_ + 2, :].rearrange("p a c -> p (a c)"),
                                         in1=xr[:, t, :], op=ALU.add).then_inc(x_upd, 1)
                    dve.wait_ge(sd2, upto(l, T, t + 1))
                    r = st[:, 8 + par_:9 + par_]
                    rsqrt(st[:, par_:par_ + 1], st[:, 2 + par_:3 + par_], r, st[:, 6:7], 1.0 / D)
                    dve.wait_ge(s_tok[par_], l * (16 * (T // 2)) + 16 * m + 1)
                    ve.tensor_scalar(xs2[par_], xr[:, t, :], r, None, ALU.mult).then_inc(xs2_ready, 1)
                    if not first(t):
                        add_bias(t - 1, 1 - par_)

                steps(dve, T, out_dve, ch)
                gain2(T - 1, (T - 1) % 2)
                add_bias(T - 1, (T - 1) % 2)
                dve.wait_ge(logits, upto(l, T, T))

                lg = R("lg", NR)
                gl, el = lg[:, :, 0:EG], lg[:, :, EG:NR]
                dsc = desc.unsqueeze(1).to_broadcast([P, T, 4])

                def tt(out_, a, b, op):
                    ch.link(ve.tensor_tensor(out=out_, in0=a, in1=b, op=op))

                def first_of_max(vals, m, onehot):
                    tt(R("is1", 4), vals, spread(m, 4), ALU.is_equal)
                    tt(R("is1", 4), R("is1", 4), dsc, ALU.mult)
                    ch.link(ve.tensor_reduce(R("sm"), R("is1", 4), AX.X, ALU.max))
                    tt(onehot, dsc, spread(R("sm"), 4), ALU.is_equal)

                ch.link(ve.tensor_reduce(R("gm"), gl, AX.X, ALU.max))
                ch.link(ve.tensor_tensor(out=R("ge", EG), in0=gl, in1=spread(R("gm"), EG), op=ALU.subtract))
                dve.sem_inc(ge_ready, 1)
                first_of_max(gl, R("gm"), R("goh", EG))
                tmp4 = R("tmp")[:, 0:T * 16].rearrange("p (t e g) -> p t e g", e=EPG, g=EG)
                tt(tmp4, el.rearrange("p t (g e) -> p t e g", g=EG),
                   R("goh", EG).unsqueeze(2).to_broadcast([P, T, EPG, EG]), ALU.mult)
                ch.link(ve.tensor_reduce(R("es", EPG), tmp4, AX.X, ALU.add))
                ch.link(ve.tensor_reduce(R("m1"), R("es", EPG), AX.X, ALU.max))
                first_of_max(R("es", EPG), R("m1"), R("oh1", 4))
                ch.link(ve.scalar_tensor_tensor(out=R("es2"), in0=R("oh1"), scalar=NEG, in1=R("es"),
                                                op0=ALU.mult, op1=ALU.add))
                ch.link(ve.tensor_reduce(R("m2"), R("es2", EPG), AX.X, ALU.max))
                tt(R("dm"), R("m2"), R("m1"), ALU.subtract)
                dve.sem_inc(dm_ready, 1)
                first_of_max(R("es2", EPG), R("m2"), R("oh2", 4))
                for OH, oh in (("OH1", "oh1"), ("OH2", "oh2")):
                    tt(R(OH).rearrange("p (t g e) -> p t g e", g=EG, e=EPG),
                       R("goh", EG).unsqueeze(3).to_broadcast([P, T, EG, EPG]),
                       R(oh, 4).unsqueeze(2).to_broadcast([P, T, EG, EPG]), ALU.mult)
                ve.tensor_tensor(out=R("M"), in0=R("OH1"), in1=R("OH2"), op=ALU.add).then_inc(onehots, 1)
                dve.wait_ge(ge_exp, upto(l, 1, 1))
                ch.link(ve.tensor_reduce(R("gs"), R("ee", EG), AX.X, ALU.add))
                ch.link(ve.reciprocal(R("pt"), R("gs")))
                dve.wait_ge(dm_exp, upto(l, 1, 1))
                ch.link(ve.tensor_scalar(R("rd"), R("e2"), 1.0, None, ALU.add))
                ch.link(ve.reciprocal(R("rd"), R("rd")))
                tt(gate_w[:, 0, :], R("rd"), R("pt"), ALU.mult)
                tt(gate_w[:, 1, :], gate_w[:, 0, :], R("e2"), ALU.mult)
                dve.wait_ge(ranks, upto(l, 1, 1))
                ch.link(ve.tensor_copy(R("tot"), ps[:, 1, 0:T * NE]))
                tot, off = R("tot", NE), R("off", NE)
                ch.link(ve.memset(off[:, 0, :], 0.0))
                for t in range(1, T):
                    tt(off[:, t, :], off[:, t - 1, :], tot[:, t - 1, :], ALU.add)
                tt(R("cnt"), off[:, T - 1, :], tot[:, T - 1, :], ALU.add)
                big = R("tmp")[:, 0:NE * T].rearrange("p (e t) -> p e t", t=T)
                tt(big, spread(R("cnt"), T), cst[:, C_THR:C_THR + T].unsqueeze(1).to_broadcast([P, NE, T]), ALU.is_gt)
                ch.link(ve.tensor_reduce(R("te"), big, AX.X, ALU.add))
                big = R("tmp")[:, 0:NE * NE].rearrange("p (e f) -> p e f", f=NE)
                tt(big, R("te").unsqueeze(1).to_broadcast([P, NE, NE]),
                   cst[:, C_LT:C_LT + NE * NE].rearrange("p (e f) -> p e f", f=NE), ALU.mult)
                ch.link(ve.tensor_reduce(R("start"), big, AX.X, ALU.add))
                base = R("base", NE)
                ch.link(ve.scalar_tensor_tensor(out=base, in0=R("start").unsqueeze(1).to_broadcast([P, T, NE]),
                                                scalar=float(P), in1=off, op0=ALU.mult, op1=ALU.add))
                ch.link(ve.tensor_tensor(out=R("base"), in0=ps[:, 0, 0:T * NE], in1=R("base"), op=ALU.add))
                for k, OH in enumerate(("OH1", "OH2")):
                    tt(R("tmp")[:, 0:T * NE], R(OH), R("base"), ALU.mult)
                    ch.link(ve.tensor_reduce(R("posf")[:, k * T:(k + 1) * T],
                                             R("tmp")[:, 0:T * NE].rearrange("p (t e) -> p t e", e=NE), AX.X, ALU.add))
                ch.link(ve.tensor_copy(pos_i[:, :, :].rearrange("p k t -> p (k t)"), R("posf")))
                count = cst[:, C_JJ:C_JJ + 32].unsqueeze(1).to_broadcast([P, 2 * T, 32])
                ch.link(ve.tensor_scalar(R("blk"), R("posf"), 1.0 / P, None, ALU.mult))
                tt(R("tmp", 32), spread(R("blk"), 32), count, ALU.is_ge)
                ch.link(ve.tensor_reduce(R("blk"), R("tmp", 32), AX.X, ALU.add))
                ch.link(ve.tensor_scalar(R("blk"), R("blk"), -1.0, None, ALU.add))
                tt(R("tmp2", 32), spread(R("blk"), 32), count, ALU.is_equal)
                tt(in_block, R("tmp2", 32), spread(cst[:, C_TOK:C_TOK + 2 * T], 32), ALU.mult)
                ch.link(ve.scalar_tensor_tensor(out=R("posf"), in0=R("blk"), scalar=-float(P), in1=R("posf"),
                                                op0=ALU.mult, op1=ALU.add))
                for k in range(2):
                    ve.tensor_tensor(out=in_row[:, k * T:(k + 1) * T, :], in0=spread(R("posf")[:, k * T:(k + 1) * T], P),
                                     in1=cst[:, C_JJ:C_JJ + P].unsqueeze(1).to_broadcast([P, T, P]),
                                     op=ALU.is_equal).then_inc(located, 1)
                dve.wait_ge(listed, upto(l, 1, 1))
                ve.tensor_copy(row_tok[:, :], ps[:, 2, 0:32]).then_inc(rows_known, 1)
                ch.link(ve.tensor_copy(start_i[:, 0:NE], R("start")))
                ch.link(ve.tensor_tensor(out=start_i[:, NE:NE + 1], in0=R("start")[:, NE - 1:NE],
                                         in1=R("te")[:, NE - 1:NE], op=ALU.add))
                big = R("tmp3").rearrange("p (j e) -> p j e", e=NE)
                tt(big, cst[:, C_JJ:C_JJ + 32].unsqueeze(2).to_broadcast([P, 32, NE]),
                   R("start").unsqueeze(1).to_broadcast([P, 32, NE]), ALU.is_ge)
                ch.link(ve.tensor_reduce(R("bef"), big, AX.X, ALU.add))
                ve.tensor_scalar(block_e[:, :], R("bef"), -1.0, None, ALU.add).then_inc(routed, 1)
                dve.wait_ge(routed, upto(l, 1, 1))
                dve.sem_inc(s_passed, 1)
                used = dve.value_load(start_i[0:1, NE:NE + 1], min_val=2 * SEQ // P, max_val=BLOCKS)

                def rows_evac(t):
                    dve.wait_ge(xtm_done, upto(l, BLOCKS, t + 1))
                    times_gain(xgT, par[:, G2:G2 + K], 0, xgT_ready)

                def y_evac(t, slot, m):
                    dve.wait_ge(dn_done, upto(l, BLOCKS, t + 1))
                    dve.wait_ge(s_y[slot], l * (16 * USES[slot]) + 16 * m + 1)
                    ve.tensor_copy(y[slot][:, 0:512], ps[:, 4, :]).then_inc(y0_ready, 1)

                in_low(l + 1, 0)
                rows_evac(0)

                def moe_dve(t, slot, m):
                    if not last(t, BLOCKS):
                        rows_evac(t + 1)
                    dve.wait_ge(silu_done, upto(l, BLOCKS, t + 1))
                    ve.tensor_tensor(out=act, in0=ps[:, 2, FE:2 * FE], in1=sg, op=ALU.mult).then_inc(a_ready, 1)
                    if not first(t):
                        y_evac(t - 1, *before(slot, m))

                def maybe_evac(t, slot, m):
                    with dve.If(used > t):
                        y_evac(t, slot, m)
                        dve.wait_ge(a_ready, upto(l, BLOCKS, t + 1))
                        if not last(t, BLOCKS):
                            dve.wait_ge(xgT_ready, upto(l, BLOCKS, t + 2))
                        dve.wait_ge(y0_ready, upto(l, BLOCKS, t + 1))
                        dve.sem_inc(s_passed, 1)
                    with dve.Else():
                        dve.sem_inc(y0_ready, 1)

                def maybe_dve(t, slot, m):
                    with dve.If(used > t):
                        moe_dve(t, slot, m)
                    with dve.Else():
                        maybe_evac(t - 1, *before(slot, m))
                        if not last(t, BLOCKS):
                            dve.sem_inc(xgT_ready, 1)
                        dve.sem_inc(a_ready, 1)

                steps(dve, BLOCKS, moe_dve, ring=RING, sure=SURE, maybe=maybe_dve)
                maybe_evac(BLOCKS - 1, (BLOCKS - 1) % RING, (BLOCKS - 1) // RING)

                ch.restart()
                for t in range(T):
                    b = t % GATHS
                    dve.wait_ge(s_gath[b], l * (16 * 2 * (T // GATHS)) + 32 * (t // GATHS + 1))
                    ch.link(ve.scalar_tensor_tensor(out=xr[:, t, :], in0=gath[b][:, 0, :], scalar=gate_w[:, 0, t:t + 1],
                                                    in1=xr[:, t, :], op0=ALU.mult, op1=ALU.add))
                    ve.scalar_tensor_tensor(out=xr[:, t, :], in0=gath[b][:, 1, :], scalar=gate_w[:, 1, t:t + 1],
                                                in1=xr[:, t, :], op0=ALU.mult, op1=ALU.add).then_inc(x_ready, 1)
                    if t in (0, 1, 3, 5):
                        with dve.If(l < DEPTH - 1):
                            if t == 0:
                                norm_x(l + 1, 0, 0)
                                dve.wait_ge(gain_in, upto(l + 1, 1, 1))
                                gain1(l + 1, 0, 0)
                                in_low(l + 1, 1)
                            if t == 1:
                                norm_x(l + 1, 1, 1)
                            if t == 3:
                                gain1(l + 1, 1, 1)
                            if t == 5:
                                dve.wait_ge(params, upto(l + 1, 1, 1))
                                norm_qk(l + 1, 0, 0, 0)
                        ch.restart()

        @block.tensor
        def _(pe):
            te = nc.tensor
            for s in (xt_done, z_done, tqk_done, s_done, pt0_done, pt1_done, pv_done, at_done, pm_done,
                      op_done, xt2_done, rt_done, ranks, listed, xtm_done, gu_done, a_t_done, dn_done):
                pe.sem_inc(s, BIAS)
            pe.wait_ge(s_cst, 16)
            pe.wait_ge(s_rows, 3 * 16)
            te.transpose(ps[:, 7, 0:DEPTH * GQK], par_rows, ident[0:DEPTH * GQK, 0:DEPTH * GQK]).then_inc(rows_t, 1)

            def transposes(bank, srcs):
                for i, src in enumerate(srcs):
                    ins = te.transpose(ps[:, bank + i // 4, (i % 4) * P:(i % 4 + 1) * P], src, ident)
                return ins

            def cols(ap, n):
                return [ap[:, i * P:(i + 1) * P] for i in range(n)]

            with pe.Fori(0, DEPTH) as l:
                def xt(n):
                    pe.wait_ge(xs_ready, upto(l, 2 * T, n + 1))
                    transposes(0, cols(xs, K)).then_inc(xt_done, 1)

                def z(par_, i, split):
                    hi = w_in_hi[i].rearrange("p (k n) -> p k n", k=K)
                    lo = w_in_lo[i].rearrange("p (k n) -> p k n", k=K)
                    for k in range(K):
                        if split is not None and k % (K // 2) == 0:
                            pe.wait_ge(win_split, upto(l, 8, 2 * split + k // (K // 2) + 1))
                        for n, (a, b) in enumerate(((hT_hi, hi), (hT_hi, lo), (hT_lo, hi))):
                            ins = te.matmul(ps[:, 2 + 2 * par_ + i, :], a[par_][:, k, :], b[:, k, :],
                                            start=k == 0 and n == 0, stop=k == K - 1 and n == 2)
                    ins.then_inc(z_done, 1)

                def turn(h, t, par_):
                    zr = zn[par_].rearrange("p h c -> p (h c)")
                    pe.wait_ge(qk_ready, upto(l, 2 * T, h * T + t + 1))
                    pe.wait_ge(t_evac, upto(l, 3 * T, t if h == 0 else T + 2 * t))
                    transposes(6, cols(zr, 4)).then_inc(tqk_done, 1)

                def turn_u(t):
                    pe.wait_ge(u_copied, upto(l, T, t + 1))
                    transposes(7, [u_nat[:, g, :] for g in range(NG)]).then_inc(tqk_done, 1)

                xt(0)

                def in_pe(t, par_, h):
                    n = h * T + t
                    pe.wait_ge(hT_ready, upto(l, 2 * T, n + 1))
                    if not (h == 0 and first(t)):
                        pe.wait_ge(zqk_free, upto(l, 2 * T, n - 1))
                    z(par_, 0, 2 * h if first(t) else None)
                    if not first(t):
                        turn(h, t - 1, 1 - par_)
                        if h:
                            turn_u(t - 1)
                    elif h:
                        turn(0, T - 1, 1 - par_)
                    if h == 0 or not last(t, T):
                        xt(n + 1)
                    if h == 0 and not first(t):
                        pe.wait_ge(v_copied, upto(l, T, t - 1))
                    elif h:
                        pe.wait_ge(v_copied, upto(l, T, T))
                        if not first(t):
                            pe.wait_ge(u_copied, upto(l, T, t - 1))
                    z(par_, 1, 2 * h + 1 if first(t) else None)

                for h in range(2):
                    steps(pe, T, lambda t, par_, m: in_pe(t, par_, h))
                turn(1, T - 1, (T - 1) % 2)
                turn_u(T - 1)

                pe.wait_ge(t_evac, upto(l, 3 * T, 3 * T))
                pe.wait_ge(v_copied, upto(l, T, T))
                pe.wait_ge(zqk_free, upto(l, 2 * T, 2 * T))
                pe.sem_inc(s_passed, 1)
                def scores(p, n):
                    a, i, b = n // T, n % T, n % 2
                    r = slice(HD * a, HD * (a + 1))
                    if i == 0:
                        pe.wait_ge(staged, upto(l, 2 * PAIRS + 1, p * 2 + a + 1))
                    if n >= 2:
                        pe.wait_ge(sm_ready, upto(l, 16 * PAIRS, p * 16 + n - 1))
                    nk = (i + 1) * P
                    for c in range(0, nk, 512):
                        w = min(512, -(-(nk - c) // 256) * 256)
                        te.matmul(ps[:, 2 * b + c // 512, 0:w], q_parts[a][:, i * P:(i + 1) * P],
                                  k_high[a][:, c:c + w], start=True, stop=False)
                        ins = te.matmul(ps[:, 2 * b + c // 512, 0:w], q_parts[a][r, i * P:(i + 1) * P],
                                        k_low[r, c:c + w], start=False, stop=True)
                    ins.then_inc(s_done, 1)

                pe.wait_ge(sm_ready, upto(l, 16 * PAIRS, 0))
                scores(0, 0)
                scores(0, 1)
                with pe.Fori(0, PAIRS) as p:
                    pe.wait_ge(at_ev, upto(l, 2 * PAIRS, p * 2))
                    pe.wait_ge(o_ev, upto(l, 16 * PAIRS, p * 16))

                    def probs_t(n):
                        a, i, b = n // T, n % T, n % 2
                        pe.wait_ge(p_ready, upto(l, 16 * PAIRS, p * 16 + n + 1))
                        pe.wait_ge(pt0_ev, upto(l, 16 * PAIRS, p * 16 + n))
                        blocks = cols(pr[b], i + 1)
                        transposes(4, blocks[0:4]).then_inc(pt0_done, 1)
                        if i >= 4:
                            pe.wait_ge(pt1_ev, upto(l, 8 * PAIRS, p * 8 + 4 * a + i - 4))
                            transposes(5, blocks[4:]).then_inc(pt1_done, 1)

                    def probs_v(n):
                        a, i, b = n // T, n % T, n % 2
                        pe.wait_ge(pt0_ev, upto(l, 16 * PAIRS, p * 16 + n + 1))
                        if i >= 4:
                            pe.wait_ge(pt1_ev, upto(l, 8 * PAIRS, p * 8 + 4 * a + i - 3))
                        if n >= 2:
                            pe.wait_ge(o_ev, upto(l, 16 * PAIRS, p * 16 + n - 1))
                        for j in range(i + 1):
                            ins = te.matmul(ps[:, 6 + b, 0:P], prT[b][:, j, :], v[:, j, ds(p * P, P)],
                                            start=j == 0, stop=j == i)
                        ins.then_inc(pv_done, 1)

                    for n in range(16):
                        probs_t(n)
                        if n + 2 < 16:
                            scores(p, n + 2)
                        if n >= 1:
                            probs_v(n - 1)
                    probs_v(15)
                    with pe.If(p < PAIRS - 1):
                        pe.wait_ge(sm_ready, upto(l, 16 * PAIRS, p * 16 + 16))
                        scores(p + 1, 0)
                        scores(p + 1, 1)
                    pe.wait_ge(o_ev, upto(l, 16 * PAIRS, p * 16 + 16))
                    for h in range(2):
                        transposes(4 + h, [att[:, 4 * h + i, :] for i in range(4)]).then_inc(at_done, 1)

                pe.wait_ge(s_wpool, (l + 1) * 16)
                pe.wait_ge(pooled, upto(l, NG, NG))
                for n in range(2 * NG):
                    g, h = n // 2, n % 2
                    if n >= 4:
                        pe.wait_ge(poolT_ready, upto(l, 2 * NG, n - 3))
                    te.matmul(ps[:, n % 4, :], wpool[:, g, :], uT[:, g, PAD + 512 * h:PAD + 512 * h + 512],
                                  start=True, stop=True).then_inc(pm_done, 1)

                pe.wait_ge(poolT_ready, upto(l, 2 * NG, 2 * NG))
                pe.wait_ge(at_ev, upto(l, 2 * PAIRS, 2 * PAIRS))

                def project(par_, h):
                    hi = w_o_hi[h].rearrange("p (k n) -> p k n", k=K)
                    lo = w_o_lo[h].rearrange("p (k n) -> p k n", k=K)
                    for k in range(K):
                        for n, (a, b) in enumerate(((cat_hi, hi), (cat_hi, lo), (cat_lo, hi))):
                            ins = te.matmul(ps[:, 2 * par_ + h, :], a[par_][:, k, :], b[:, k, :],
                                            start=k == 0 and n == 0, stop=k == K - 1 and n == 2)
                    return ins

                def xt2(t, par_):
                    pe.wait_ge(xs2_ready, upto(l, T, t + 1))
                    if not first(t):
                        pe.wait_ge(h2T_ready, upto(l, T, t))
                    transposes(4, cols(xs2[par_], K)).then_inc(xt2_done, 1)

                def router(t, par_):
                    pe.wait_ge(h2T_ready, upto(l, T, t + 1))
                    for k in range(K):
                        ins = te.matmul(ps[:, 6 + par_, 0:P], h2T[par_][:, k, :],
                                        wr_all[:, ds(l * (K * NR) + k * NR, P)],
                                        start=k == 0, stop=k == K - 1)
                    ins.then_inc(rt_done, 1)

                def out_pe(t, par_, m):
                    if first(t):
                        pe.wait_ge(s_wr, DEPTH * 2 * 16)
                    else:
                        pe.wait_ge(x_upd, upto(l, T, t - 1))
                    pe.wait_ge(cat_ready, upto(l, T, t + 1))
                    if first(t):
                        pe.wait_ge(wo_split, upto(l, 2, 1))
                    project(par_, 0)
                    if first(t):
                        pe.wait_ge(wo_split, upto(l, 2, 2))
                    if not first(t):
                        xt2(t - 1, 1 - par_)
                    project(par_, 1).then_inc(op_done, 1)
                    if not first(t):
                        pe.wait_ge(logits, upto(l, T, t - 1))
                        router(t - 1, 1 - par_)

                steps(pe, T, out_pe)
                xt2(T - 1, (T - 1) % 2)
                router(T - 1, (T - 1) % 2)

                pe.wait_ge(onehots, upto(l, 1, 1))
                te.matmul(ps[:, 0, 0:T * NE], low, R("M"), start=True, stop=True)
                te.matmul(ps[:, 1, 0:T * NE], ones, R("M"), start=True, stop=True).then_inc(ranks, 1)

                for k in range(2):
                    pe.wait_ge(located, upto(l, 2, k + 1))
                    for c in range(k * T, (k + 1) * T):
                        ins = te.matmul(ps[:, 2, 0:32], in_row[:, c, :], in_block[:, c, :],
                                        start=c == 0, stop=c == 2 * T - 1)
                ins.then_inc(listed, 1)

                def xtm(t, slot, m):
                    pe.wait_ge(s_xg[slot], l * (16 * USES[slot]) + 16 * (m + 1))
                    if first(t):
                        pe.wait_ge(routed, upto(l, 1, 1))
                    else:
                        pe.wait_ge(xgT_ready, upto(l, BLOCKS, t))
                    transposes(0, cols(xg[slot], K)).then_inc(xtm_done, 1)

                def weights(t):
                    e = pe.value_load(block_e[0:1, ds(t, 1)], min_val=0, max_val=NE - 1)
                    pe.wait_ge(w_loaded, upto(l, NE, e + 1))
                    return ((e + 2) % SLOTS) * E_ALL + AT_E

                def gate_up(t):
                    at = weights(t)
                    for k in range(K):
                        ins = te.matmul(ps[:, 2, :], xgT[:, k, :], big[:, ds(at + k * 2 * FE, 2 * FE)],
                                        start=k == 0, stop=k == K - 1)
                    ins.then_inc(gu_done, 1)

                def down(t):
                    pe.wait_ge(aT_ready, upto(l, BLOCKS, t + 1))
                    if not first(t):
                        pe.wait_ge(y0_ready, upto(l, BLOCKS, t))
                        pe.wait_ge(y1_ready, upto(l, BLOCKS, t))
                    pe.sem_inc(s_passed, 1)
                    at = weights(t)
                    for h in range(2):
                        for k in range(2):
                            ins = te.matmul(ps[:, 4 + h, :], aT[:, k, :], big[:, ds(at + (E_GU + k * D + 512 * h), 512)],
                                            start=k == 0, stop=k == 1)
                    ins.then_inc(dn_done, 1)

                xtm(0, 0, 0)
                used = pe.value_load(start_i[0:1, NE:NE + 1], min_val=2 * SEQ // P, max_val=BLOCKS)

                def moe_pe(t, slot, m):
                    pe.wait_ge(xgT_ready, upto(l, BLOCKS, t + 1))
                    if not first(t):
                        pe.wait_ge(a_ready, upto(l, BLOCKS, t))
                    pe.sem_inc(s_passed, 1)
                    gate_up(t)
                    if not last(t, BLOCKS):
                        xtm(t + 1, *after(slot, m))
                    if not first(t):
                        down(t - 1)
                    pe.wait_ge(a_ready, upto(l, BLOCKS, t + 1))
                    transposes(3, cols(act, 2)).then_inc(a_t_done, 1)

                def maybe_down(t):
                    with pe.If(used > t):
                        down(t)
                        if not last(t, BLOCKS):
                            pe.wait_ge(xtm_done, upto(l, BLOCKS, t + 2))
                        pe.wait_ge(dn_done, upto(l, BLOCKS, t + 1))
                        pe.sem_inc(s_passed, 1)
                    with pe.Else():
                        pe.sem_inc(dn_done, 1)

                def maybe_pe(t, slot, m):
                    with pe.If(used > t):
                        moe_pe(t, slot, m)
                    with pe.Else():
                        maybe_down(t - 1)
                        pe.sem_inc(gu_done, 1)
                        if not last(t, BLOCKS):
                            pe.sem_inc(xtm_done, 1)
                        pe.sem_inc(a_t_done, 1)

                steps(pe, BLOCKS, moe_pe, ring=RING, sure=SURE, maybe=maybe_pe)
                maybe_down(BLOCKS - 1)


_INS = ["x", "norm1_gain", "w_in", "q_norm_gain", "k_norm_gain", "w_pool", "pool_scale", "w_out", "norm2_gain",
        "w_group", "b_group", "w_router", "b_router", "w_gate", "w_up", "w_down"]


def kernel(**inputs):
    import concourse.bacc as bacc
    from concourse.bass_utils import run_bass_kernel_spmd

    nc = bacc.Bacc("TRN2", target_bir_lowering=False, num_devices=1)
    arrays = {n: np.ascontiguousarray(inputs[n]) for n in _INS}
    arrays["consts"] = shape_constants()
    args = [nc.dram_tensor(f"in_{n}", a.shape, mybir.dt.from_np(a.dtype), kind="ExternalInput").ap()
            for n, a in arrays.items()]
    args.append(nc.dram_tensor("out_x", (1, SEQ, D), mybir.dt.float32, kind="ExternalOutput").ap())
    trunk(nc, *args)
    r = run_bass_kernel_spmd(nc, [{f"in_{n}": a for n, a in arrays.items()}], core_ids=[0])
    return r.results[0]["out_x"]
```
